# Optimizing a Trainium2 kernel written in Bass

```python
import math
import jax, jax.numpy as jnp
from jax import lax
import numpy as np

D_MODEL = 1024
BATCH = 1
SEQ = 256
DEPTH = 2

EPS = 1e-6
BLOCK_Q = 128
D_FF = 2816
GLA_HEADS = 4
GLA_DK = 64
GLA_DV = 128
GLA_GATE_RANK = 16
GLA_GATE_NORMALIZER = 16.0
GLA_CHUNK = 64
FOX_HEADS = 8
FOX_DH = 64
DSA_HEADS = 16
DSA_DH = 64
DSA_LATENT = 256
IDX_HEADS = 8
IDX_DIM = 64
TOPK_MAX = 256
T5_BUCKETS = 32
T5_MAX_DIST = 128

N_EVEN = (DEPTH + 1) // 2
N_ODD = DEPTH // 2

EVEN_SIZES = (GLA_HEADS * GLA_DK, GLA_HEADS * GLA_DK, GLA_HEADS * GLA_DV, GLA_HEADS * GLA_DV, GLA_GATE_RANK,
              FOX_HEADS * FOX_DH, FOX_HEADS * FOX_DH, FOX_HEADS * FOX_DH, FOX_HEADS)
ODD_SIZES = (DSA_HEADS * DSA_DH, DSA_LATENT, IDX_HEADS * IDX_DIM, IDX_DIM, IDX_HEADS)
D_IN_EVEN = sum(EVEN_SIZES)
D_IN_ODD = sum(ODD_SIZES)
EVEN_SPLITS = tuple(int(v) for v in np.cumsum(EVEN_SIZES)[:-1])
ODD_SPLITS = tuple(int(v) for v in np.cumsum(ODD_SIZES)[:-1])
D_MIX_EVEN = GLA_HEADS * GLA_DV + FOX_HEADS * FOX_DH
D_MIX_ODD = DSA_HEADS * DSA_DH


def rmsnorm(x, g):
    xf = x.astype(jnp.float32)
    y = xf * lax.rsqrt(jnp.mean(xf * xf, axis=-1, keepdims=True) + EPS)
    return (y * g.astype(jnp.float32)).astype(x.dtype)

def swiglu(h, w_in, w_out):
    a, b = jnp.split(h @ w_in, 2, axis=-1)
    return (jax.nn.silu(a) * b) @ w_out

def to_blocks(t, nb):
    return t.reshape((t.shape[0], nb, BLOCK_Q) + t.shape[2:]).swapaxes(0, 1)

def gla_chunked(q, k, v, gk):
    B, S, H, dk = q.shape
    dv = v.shape[-1]
    C = GLA_CHUNK
    N = S // C

    def chunks(t):
        return t.astype(jnp.float32).reshape(B, N, C, H, t.shape[-1]).transpose(1, 0, 3, 2, 4)

    qc = chunks(q) * (dk ** -0.5)
    kc, vc, gc = chunks(k), chunks(v), chunks(gk)
    G = jnp.cumsum(gc, axis=-2)
    G_last = G[..., -1, :]
    q_dec = qc * jnp.exp(G)
    k_dec = kc * jnp.exp(-G)
    k_to_end = kc * jnp.exp(G_last[..., None, :] - G)
    causal = jnp.tril(jnp.ones((C, C), dtype=bool))
    A = jnp.where(causal, jnp.einsum('nbhid,nbhjd->nbhij', q_dec, k_dec), 0.0)
    o_intra = jnp.einsum('nbhij,nbhjv->nbhiv', A, vc)

    def step(state, inp):
        qd, ke, vv, gl = inp
        o = jnp.einsum('bhid,bhdv->bhiv', qd, state)
        state = jnp.exp(gl)[..., None] * state + jnp.einsum('bhjd,bhjv->bhdv', ke, vv)
        return state, o

    state0 = jnp.zeros((B, H, dk, dv), jnp.float32)
    _, o_inter = lax.scan(step, state0, (q_dec, k_to_end, vc, G_last))
    o = o_intra + o_inter
    return o.transpose(1, 0, 3, 2, 4).reshape(B, S, H, dv)

def fox_attention(q, k, v, log_f):
    B, S, H, dh = q.shape
    nb = S // BLOCK_Q
    F = jnp.cumsum(log_f, axis=1)
    F_keys = F.transpose(0, 2, 1)
    key_pos = jnp.arange(S)

    def one_block(args):
        i, qb, Fb = args
        q_pos = i * BLOCK_Q + jnp.arange(BLOCK_Q)
        s = jnp.einsum('bqhd,bkhd->bhqk', qb, k).astype(jnp.float32) * (dh ** -0.5)
        s = s + (Fb.transpose(0, 2, 1)[..., :, None] - F_keys[..., None, :])
        s = jnp.where(key_pos[None, :] <= q_pos[:, None], s, -jnp.inf)
        p = jax.nn.softmax(s, axis=-1)
        return jnp.einsum('bhqk,bkhd->bqhd', p.astype(v.dtype), v)

    o = lax.map(one_block, (jnp.arange(nb), to_blocks(q, nb), to_blocks(F, nb)))
    return o.swapaxes(0, 1).reshape(B, S, H, dh)

def t5_bucket(dist):
    max_exact = T5_BUCKETS // 2
    d = jnp.maximum(dist, 1).astype(jnp.float32)
    large = max_exact + (jnp.log(d / max_exact) / math.log(T5_MAX_DIST / max_exact)
                         * (T5_BUCKETS - max_exact)).astype(jnp.int32)
    large = jnp.minimum(large, T5_BUCKETS - 1)
    return jnp.where(dist < max_exact, dist, large)

def dsa_attention(q_lat, c, q_idx, k_idx, w_idx, t5_table):
    B, S, H, DL = q_lat.shape
    k_top = min(TOPK_MAX, S // 4)
    nb = S // BLOCK_Q
    key_pos = jnp.arange(S)
    w_scaled = w_idx.astype(jnp.float32) * (IDX_HEADS ** -0.5)
    gather = jax.vmap(lambda cb, ib: cb[ib])

    def one_block(args):
        i, qb, qib, wb = args
        q_pos = i * BLOCK_Q + jnp.arange(BLOCK_Q)
        logit_idx = jnp.einsum('bqhd,bkd->bqhk', qib, k_idx).astype(jnp.float32) * (IDX_DIM ** -0.5)
        score = jnp.einsum('bqh,bqhk->bqk', wb, jax.nn.relu(logit_idx))
        score = jnp.where((key_pos[None, :] <= q_pos[:, None])[None], score, -jnp.inf)
        _, idx = lax.top_k(score, k_top)
        c_sel = gather(c, idx)
        dist = q_pos[None, :, None] - idx
        bias = t5_table[t5_bucket(jnp.maximum(dist, 0))]
        s = jnp.einsum('bqhl,bqkl->bqhk', qb, c_sel).astype(jnp.float32) * (DSA_DH ** -0.5)
        s = s + bias.transpose(0, 1, 3, 2).astype(jnp.float32)
        s = jnp.where((dist >= 0)[:, :, None, :], s, -jnp.inf)
        p = jax.nn.softmax(s, axis=-1)
        return jnp.einsum('bqhk,bqkl->bqhl', p.astype(c.dtype), c_sel)

    o = lax.map(one_block, (jnp.arange(nb), to_blocks(q_lat, nb), to_blocks(q_idx, nb), to_blocks(w_scaled, nb)))
    return o.swapaxes(0, 1).reshape(B, S, H, DL)

def even_mixer(h, w_in, gla_w_gate, gla_b_gate, gla_norm_g, fox_b_f, w_out):
    B, S, _ = h.shape
    q_g, k_g, v_g, g_out, gk_low, q_f, k_f, v_f, f_logit = jnp.split(h @ w_in, EVEN_SPLITS, axis=-1)
    gk = jax.nn.log_sigmoid((gk_low @ gla_w_gate + gla_b_gate).astype(jnp.float32)) / GLA_GATE_NORMALIZER
    o_gla = gla_chunked(q_g.reshape(B, S, GLA_HEADS, GLA_DK), k_g.reshape(B, S, GLA_HEADS, GLA_DK),
                        v_g.reshape(B, S, GLA_HEADS, GLA_DV), gk.reshape(B, S, GLA_HEADS, GLA_DK)).astype(h.dtype)
    o_gla = rmsnorm(o_gla, gla_norm_g) * jax.nn.silu(g_out.reshape(B, S, GLA_HEADS, GLA_DV))
    log_f = jax.nn.log_sigmoid((f_logit + fox_b_f).astype(jnp.float32))
    o_fox = fox_attention(q_f.reshape(B, S, FOX_HEADS, FOX_DH), k_f.reshape(B, S, FOX_HEADS, FOX_DH),
                          v_f.reshape(B, S, FOX_HEADS, FOX_DH), log_f)
    o = jnp.concatenate([o_gla.reshape(B, S, -1), o_fox.reshape(B, S, -1)], axis=-1)
    return o @ w_out

def odd_mixer(h, w_in, kv_norm_g, w_uk, w_uv, w_out, t5_table):
    B, S, _ = h.shape
    q, ckv, q_idx, k_idx, w_idx = jnp.split(h @ w_in, ODD_SPLITS, axis=-1)
    c = rmsnorm(ckv, kv_norm_g)
    q_lat = jnp.einsum('bshd,hdl->bshl', q.reshape(B, S, DSA_HEADS, DSA_DH), w_uk)
    o_lat = dsa_attention(q_lat, c, q_idx.reshape(B, S, IDX_HEADS, IDX_DIM), k_idx, w_idx, t5_table)
    o = jnp.einsum('bshl,hld->bshd', o_lat, w_uv).reshape(B, S, D_MIX_ODD)
    return o @ w_out

def first_inputs(seed: int = 0) -> dict:
    key = jax.random.key(seed)
    ks = jax.random.split(key, 17)
    f32 = jnp.float32

    def nrm(k, shape, fan_in):
        return jax.random.normal(k, shape, f32) * (fan_in ** -0.5)

    def gain(k, shape):
        return 1.0 + 0.02 * jax.random.normal(k, shape, f32)

    return {
        "x": jax.random.normal(ks[0], (BATCH, SEQ, D_MODEL), f32),
        "norm_g": gain(ks[1], (DEPTH, 3, D_MODEL)),
        "ffn_w_in": nrm(ks[2], (DEPTH, 2, D_MODEL, 2 * D_FF), D_MODEL),
        "ffn_w_out": nrm(ks[3], (DEPTH, 2, D_FF, D_MODEL), D_FF),
        "even_w_in": nrm(ks[4], (N_EVEN, D_MODEL, D_IN_EVEN), D_MODEL),
        "gla_w_gate": nrm(ks[5], (N_EVEN, GLA_GATE_RANK, GLA_HEADS * GLA_DK), GLA_GATE_RANK),
        "gla_b_gate": 0.02 * jax.random.normal(ks[6], (N_EVEN, GLA_HEADS * GLA_DK), f32),
        "gla_norm_g": gain(ks[7], (N_EVEN, GLA_DV)),
        "fox_b_f": 2.0 + 0.5 * jax.random.normal(ks[8], (N_EVEN, FOX_HEADS), f32),
        "even_w_out": nrm(ks[9], (N_EVEN, D_MIX_EVEN, D_MODEL), D_MIX_EVEN),
        "odd_w_in": nrm(ks[10], (N_ODD, D_MODEL, D_IN_ODD), D_MODEL),
        "mla_kv_norm_g": gain(ks[11], (N_ODD, DSA_LATENT)),
        "mla_w_uk": nrm(ks[12], (N_ODD, DSA_HEADS, DSA_DH, DSA_LATENT), DSA_LATENT),
        "mla_w_uv": nrm(ks[13], (N_ODD, DSA_HEADS, DSA_LATENT, DSA_DH), DSA_LATENT),
        "odd_w_out": nrm(ks[14], (N_ODD, D_MIX_ODD, D_MODEL), D_MIX_ODD),
        "t5_table": 0.5 * jax.random.normal(ks[15], (T5_BUCKETS, DSA_HEADS), f32),
        "final_norm_g": gain(ks[16], (D_MODEL,)),
    }

def first_block(x, norm_g, ffn_w_in, ffn_w_out, even_w_in, gla_w_gate, gla_b_gate, gla_norm_g, fox_b_f,
              even_w_out, odd_w_in, mla_kv_norm_g, mla_w_uk, mla_w_uv, odd_w_out, t5_table, final_norm_g):
    for layer in range(DEPTH):
        g = norm_g[layer]
        x = x + 0.5 * swiglu(rmsnorm(x, g[0]), ffn_w_in[layer, 0], ffn_w_out[layer, 0])
        h = rmsnorm(x, g[1])
        j = layer // 2
        if layer % 2 == 0:
            x = x + even_mixer(h, even_w_in[j], gla_w_gate[j], gla_b_gate[j], gla_norm_g[j], fox_b_f[j], even_w_out[j])
        else:
            x = x + odd_mixer(h, odd_w_in[j], mla_kv_norm_g[j], mla_w_uk[j], mla_w_uv[j], odd_w_out[j], t5_table)
        x = x + 0.5 * swiglu(rmsnorm(x, g[2]), ffn_w_in[layer, 1], ffn_w_out[layer, 1])
    return rmsnorm(x, final_norm_g)


N_HEADS = 8
HEAD_DIM = 64
ATTN_WIDTH = N_HEADS * HEAD_DIM
ROT_DIM = HEAD_DIM // 4
ROPE_THETA = 500000.0
MOBA_BLOCK = 256
MOBA_TOPK = 3
Q_CHUNK = 32
CONV_WIDTH = D_MODEL // 2
CONV_KERNEL = 31
D_FF_2 = 4 * D_MODEL
IN_COLS = 3 * ATTN_WIDTH + 2 * CONV_WIDTH + 2 * D_MODEL
DN_ALPHA = (2 * DEPTH) ** 0.25
DN_BETA = (8 * DEPTH) ** -0.25
ADA_SCALE = 0.1
LN_EPS = 1e-5
NEG_INF = -1e30


def layer_norm(x, g, b):
    xf = x.astype(jnp.float32)
    mu = jnp.mean(xf, -1, keepdims=True)
    var = jnp.mean(jnp.square(xf - mu), -1, keepdims=True)
    return ((xf - mu) * lax.rsqrt(var + LN_EPS)).astype(x.dtype) * g + b

def partial_rope(x, cos, sin):
    half = ROT_DIM // 2
    x1, x2, rest = x[..., :half], x[..., half:ROT_DIM], x[..., ROT_DIM:]
    return jnp.concatenate([x1 * cos - x2 * sin, x2 * cos + x1 * sin, rest], -1)

def moba_attention(q, k, v):
    B, H, S, hd = q.shape
    n_blk = -(-S // MOBA_BLOCK)
    pad = n_blk * MOBA_BLOCK - S
    kp = jnp.pad(k, ((0, 0), (0, 0), (0, pad), (0, 0)))
    vp = jnp.pad(v, ((0, 0), (0, 0), (0, pad), (0, 0)))
    kb = kp.reshape(B, H, n_blk, MOBA_BLOCK, hd)
    vb = vp.reshape(B, H, n_blk, MOBA_BLOCK, hd)
    k_mean = jnp.mean(kb.astype(jnp.float32), axis=3).astype(q.dtype)
    topk = min(MOBA_TOPK, n_blk)
    scale = hd ** -0.5
    n_chunks = S // Q_CHUNK
    q_chunks = jnp.moveaxis(q.reshape(B, H, n_chunks, Q_CHUNK, hd), 2, 0)
    b_idx = jnp.arange(B)[:, None, None, None]
    h_idx = jnp.arange(H)[None, :, None, None]
    blk_ids = jnp.arange(n_blk)

    def attend_chunk(args):
        ci, qc = args
        q_pos = ci * Q_CHUNK + jnp.arange(Q_CHUNK)
        own = (ci * Q_CHUNK) // MOBA_BLOCK
        gate = jnp.einsum('bhqd,bhnd->bhqn', qc, k_mean, preferred_element_type=jnp.float32)
        gate = jnp.where(blk_ids < own, gate, NEG_INF)
        _, sel = lax.top_k(gate, topk)
        sel_ok = jnp.arange(topk) < own
        k_sel = kb[b_idx, h_idx, sel]
        v_sel = vb[b_idx, h_idx, sel]
        s_sel = jnp.einsum('bhqd,bhqjtd->bhqjt', qc, k_sel, preferred_element_type=jnp.float32) * scale
        s_sel = jnp.where(sel_ok[:, None], s_sel, NEG_INF)
        k_own = lax.dynamic_slice_in_dim(kp, own * MOBA_BLOCK, MOBA_BLOCK, axis=2)
        v_own = lax.dynamic_slice_in_dim(vp, own * MOBA_BLOCK, MOBA_BLOCK, axis=2)
        s_own = jnp.einsum('bhqd,bhtd->bhqt', qc, k_own, preferred_element_type=jnp.float32) * scale
        k_pos = own * MOBA_BLOCK + jnp.arange(MOBA_BLOCK)
        s_own = jnp.where(k_pos[None, :] <= q_pos[:, None], s_own, NEG_INF)
        logits = jnp.concatenate([s_sel.reshape(B, H, Q_CHUNK, topk * MOBA_BLOCK), s_own], -1)
        p = jax.nn.softmax(logits, axis=-1).astype(v.dtype)
        p_sel = p[..., :topk * MOBA_BLOCK].reshape(B, H, Q_CHUNK, topk, MOBA_BLOCK)
        p_own = p[..., topk * MOBA_BLOCK:]
        return (jnp.einsum('bhqjt,bhqjtd->bhqd', p_sel, v_sel)
                + jnp.einsum('bhqt,bhtd->bhqd', p_own, v_own))

    out = lax.map(attend_chunk, (jnp.arange(n_chunks), q_chunks))
    return jnp.moveaxis(out, 0, 2).reshape(B, H, S, hd)

def conformer_conv(glu_in, dw_w, dw_b, ln_g, ln_b, w_pw):
    a, g = jnp.split(glu_in, 2, axis=-1)
    h = a * jax.nn.sigmoid(g)
    h = lax.conv_general_dilated(h, dw_w[:, None, :], window_strides=(1,),
                                 padding=[(CONV_KERNEL - 1, 0)],
                                 dimension_numbers=('NWC', 'WIO', 'NWC'),
                                 feature_group_count=CONV_WIDTH) + dw_b
    h = jax.nn.silu(layer_norm(h, ln_g, ln_b))
    return h @ w_pw

def mixer(u, cos, sin, w_in, w_attn_br, dw_w, dw_b, cln_g, cln_b, w_conv_pw, w_out):
    B, S, _ = u.shape
    proj = u @ w_in
    splits = [ATTN_WIDTH, 2 * ATTN_WIDTH, 3 * ATTN_WIDTH,
              3 * ATTN_WIDTH + 2 * CONV_WIDTH, 3 * ATTN_WIDTH + 2 * CONV_WIDTH + D_MODEL]
    q, k, v, glu_in, g_attn, g_conv = jnp.split(proj, splits, axis=-1)
    q = partial_rope(q.reshape(B, S, N_HEADS, HEAD_DIM), cos, sin).transpose(0, 2, 1, 3)
    k = partial_rope(k.reshape(B, S, N_HEADS, HEAD_DIM), cos, sin).transpose(0, 2, 1, 3)
    v = v.reshape(B, S, N_HEADS, HEAD_DIM).transpose(0, 2, 1, 3)
    attn = moba_attention(q, k, v).transpose(0, 2, 1, 3).reshape(B, S, ATTN_WIDTH)
    y_attn = attn @ w_attn_br
    y_conv = conformer_conv(glu_in, dw_w, dw_b, cln_g, cln_b, w_conv_pw)
    merged = jax.nn.sigmoid(g_attn) * y_attn + jax.nn.sigmoid(g_conv) * y_conv
    return merged @ w_out

def second_inputs(seed: int = 0) -> dict:
    key = jax.random.key(seed)
    ks = jax.random.split(key, 20)
    f32 = jnp.float32
    L, D, A, C = DEPTH, D_MODEL, ATTN_WIDTH, CONV_WIDTH
    nrm = lambda k, shape, s: jax.random.normal(k, shape, f32) * s
    return {
        "x": jax.random.normal(ks[0], (BATCH, SEQ, D), f32),
        "c": jax.random.normal(ks[1], (BATCH, D), f32),
        "positions": jnp.broadcast_to(jnp.arange(SEQ, dtype=jnp.int32), (BATCH, SEQ)),
        "w_in": nrm(ks[2], (L, D, IN_COLS), D ** -0.5),
        "w_attn_br": nrm(ks[3], (L, A, D), A ** -0.5),
        "conv_dw_w": nrm(ks[4], (L, CONV_KERNEL, C), CONV_KERNEL ** -0.5),
        "conv_dw_b": nrm(ks[5], (L, C), 0.02),
        "conv_ln_g": 1.0 + nrm(ks[6], (L, C), 0.02),
        "conv_ln_b": nrm(ks[7], (L, C), 0.02),
        "w_conv_pw": nrm(ks[8], (L, C, D), C ** -0.5),
        "w_out": nrm(ks[9], (L, D, D), DN_BETA * D ** -0.5),
        "w_ada": nrm(ks[10], (L, D, 6 * D), ADA_SCALE * D ** -0.5),
        "b_ada": nrm(ks[11], (L, 6 * D), 0.02),
        "ln_mix_g": 1.0 + nrm(ks[12], (L, D), 0.02),
        "ln_mix_b": nrm(ks[13], (L, D), 0.02),
        "w_up": nrm(ks[14], (L, D, D_FF_2), D ** -0.5),
        "w_down": nrm(ks[15], (L, D_FF_2, D), DN_BETA * D_FF_2 ** -0.5),
        "ln_ffn_g": 1.0 + nrm(ks[16], (L, D), 0.02),
        "ln_ffn_b": nrm(ks[17], (L, D), 0.02),
    }

def second_block(x, c, positions, w_in, w_attn_br, conv_dw_w, conv_dw_b, conv_ln_g, conv_ln_b,
              w_conv_pw, w_out, w_ada, b_ada, ln_mix_g, ln_mix_b, w_up, w_down,
              ln_ffn_g, ln_ffn_b):
    inv_freq = ROPE_THETA ** (-jnp.arange(0, ROT_DIM, 2, dtype=jnp.float32) / ROT_DIM)
    ang = positions.astype(jnp.float32)[..., None] * inv_freq
    cos = jnp.cos(ang)[:, :, None, :].astype(x.dtype)
    sin = jnp.sin(ang)[:, :, None, :].astype(x.dtype)
    c_act = jax.nn.silu(c)
    for l in range(DEPTH):
        ada = c_act @ w_ada[l] + b_ada[l]
        sh1, sc1, gt1, sh2, sc2, gt2 = [t[:, None, :] for t in jnp.split(ada, 6, axis=-1)]
        u = x * (1.0 + sc1) + sh1
        y = mixer(u, cos, sin, w_in[l], w_attn_br[l], conv_dw_w[l], conv_dw_b[l],
                  conv_ln_g[l], conv_ln_b[l], w_conv_pw[l], w_out[l])
        x = layer_norm(DN_ALPHA * x + (1.0 + gt1) * y, ln_mix_g[l], ln_mix_b[l])
        u = x * (1.0 + sc2) + sh2
        h = jnp.square(jax.nn.relu(u @ w_up[l])) @ w_down[l]
        x = layer_norm(DN_ALPHA * x + (1.0 + gt2) * h, ln_ffn_g[l], ln_ffn_b[l])
    return x


def setup_inputs(seed=0):
    out = dict(first_inputs(seed))
    for name, value in second_inputs(seed + 1).items():
        if name != "x":
            out[name + "_2"] = value
    return out


def reference(
    x, norm_g, ffn_w_in, ffn_w_out, even_w_in, gla_w_gate, gla_b_gate, gla_norm_g, fox_b_f,
    even_w_out, odd_w_in, mla_kv_norm_g, mla_w_uk, mla_w_uv, odd_w_out, t5_table, final_norm_g,
    c_2, positions_2, w_in_2, w_attn_br_2, conv_dw_w_2, conv_dw_b_2, conv_ln_g_2, conv_ln_b_2,
    w_conv_pw_2, w_out_2, w_ada_2, b_ada_2, ln_mix_g_2, ln_mix_b_2, w_up_2, w_down_2,
    ln_ffn_g_2, ln_ffn_b_2,
):
    x = first_block(
        x, norm_g, ffn_w_in, ffn_w_out, even_w_in, gla_w_gate, gla_b_gate, gla_norm_g, fox_b_f,
        even_w_out, odd_w_in, mla_kv_norm_g, mla_w_uk, mla_w_uv, odd_w_out, t5_table,
        final_norm_g,
    )
    return second_block(
        x, c_2, positions_2, w_in_2, w_attn_br_2, conv_dw_w_2, conv_dw_b_2, conv_ln_g_2,
        conv_ln_b_2, w_conv_pw_2, w_out_2, w_ada_2, b_ada_2, ln_mix_g_2, ln_mix_b_2, w_up_2,
        w_down_2, ln_ffn_g_2, ln_ffn_b_2,
    )


_drawn_inputs = setup_inputs


def setup_inputs(seed=0):
    import zlib

    import numpy as np

    out = dict(_drawn_inputs(seed))
    spreads = {}
    factors = {'gla_b_gate': 5.069,
     'gla_norm_g': 3.243,
     'mla_kv_norm_g': 8.0,
     'final_norm_g': 2.691,
     'conv_dw_b_2': 7.91,
     'conv_ln_g_2': 26.032,
     'conv_ln_b_2': 24.769}
    for name, (base, spread) in spreads.items():
        noise = np.random.default_rng([zlib.crc32(name.encode()), seed]).standard_normal(out[name].shape)
        drawn = base * np.exp(spread * noise) if base else spread * noise
        out[name] = __import__('jax').numpy.asarray(drawn.astype(out[name].dtype))
    for name, factor in factors.items():
        out[name] = (out[name] * factor).astype(out[name].dtype)
    return out
```

```python
import math
from contextlib import ExitStack

import numpy as np

import concourse.bass as bass
from concourse import mybir

ALU = mybir.AluOpType
ACT = mybir.ActivationFunctionType
AX = mybir.AxisListType
F32 = mybir.dt.float32
F32R = mybir.dt.float32r
I32 = mybir.dt.int32
U32 = mybir.dt.uint32

P = 128
T = 256
TB = T // P
D = 1024
KT = D // P
FF = 2816
FF_STEPS = FF // 256
FF2 = 4096
FF2_STEPS = FF2 // 256
EPS = 1e-6
LN_EPS = 1e-5
NEG = -1e30
PICKED = -3e30
TOPK = 64
HD = 64
SCALE = HD ** -0.5
DV = 128
CH = 64
LAT = 256
CONV_K = 31
CW = 512
CT = CW // P
ROT = HD // 4
ALPHA = 4 ** 0.25
RING = 3
CHUNK = 2048
BIAS_COLS = 384
ARENA = 18944
ADA_PER_FFN = 12

V_NORM, V_FINAL, V_GLA, V_MLA, V_MIXG, V_MIXB, V_FFNG, V_FFNB = 0, 48, 56, 57, 59, 75, 91, 107
V_DWB, V_CLNG, V_CLNB, V_C, V_ADA = 0, 8, 16, 24, 32
V_ROWS = (123, 128, 4 * CONV_K, 4 * CONV_K)

ROUND = 1.5 * 2 ** 23
TWO_PI = [6.28125, float(np.float32(np.floor((2 * math.pi - 6.28125) * 2 ** 20) / 2 ** 20))]
TWO_PI.append(float(np.float32(2 * math.pi - sum(TWO_PI))))
PI_BELOW = 3.1415925


def constants():
    exact = 16
    back = np.maximum(np.arange(BIAS_COLS) - (P - 1), 0)
    large = exact + (np.log(np.maximum(back, 1).astype(np.float32) / exact) / math.log(128 / exact) * (32 - exact)).astype(np.int32)
    bucket = np.where(back < exact, back, np.minimum(large, 31))
    buckets = (np.arange(32)[:, None] == bucket[None, :]).astype(np.float32)
    half = ROT // 2
    freq = np.zeros((P, 1), np.float32)
    turn = np.zeros((P, P), np.float32)
    for first in range(0, P, HD):
        for i in range(half):
            freq[first + i] = freq[first + half + i] = np.float32(500000.0 ** (-2 * i / ROT))
            turn[first + half + i, first + i] = -1.0
            turn[first + i, first + half + i] = 1.0
    return {"buckets": buckets, "rope_freq": freq, "rope_turn": turn}


class Signal:

    def __init__(self, sem):
        self.sem, self.first, self.times, self.total = sem, {}, {}, 0

    def plan(self, stage, times):
        self.first[stage], self.times[stage] = self.total, times
        self.total += times

    def at(self, stage, n=None):
        return self.first[stage] + (self.times[stage] if n is None else n)


def shifted(value, turn, per_turn):
    return value if turn is None else turn * per_turn + value


def build(nc, A, out, upto=None):
    ctx = ExitStack()

    def sb(name, shape, dt=F32):
        return ctx.enter_context(nc.sbuf_tensor(name, shape, dt))

    def signal(name):
        return Signal(ctx.enter_context(nc.semaphore(name)))

    STAGES = [("rms", "rms0"), ("ffn", "ffn0"), ("rms", "rms1"), ("even", "even"), ("rms", "rms2"), ("ffn", "ffn1"),
              ("rms", "rms3"), ("ffn", "ffn2"), ("rms", "rms4"), ("odd", "odd"), ("rms", "rms5"), ("ffn", "ffn3"),
              ("rms", "final"), ("ada", "ada")]
    for l in range(2):
        STAGES += [("mod", f"mod{l}a"), ("mix", f"mix{l}"), ("ln", f"ln{l}a"),
                   ("mod", f"mod{l}b"), ("sq", f"sq{l}"), ("ln", f"ln{l}b")]
    if upto is not None:
        STAGES = STAGES[:[s for _, s in STAGES].index(upto) + 1]
    KIND = {s: k for k, s in STAGES}
    CHUNKS_OF = {"ffn": 3 * FF_STEPS, "sq": 2 * FF2_STEPS, "even": 16, "odd": 11, "mix": 26}
    base, n_chunks = {}, 0
    for kind, s in STAGES:
        base[s] = n_chunks
        n_chunks += CHUNKS_OF.get(kind, 0)

    raw = sb("raw", [P, RING, CHUNK])
    wh = sb("wh", [P, RING, CHUNK], F32R)
    wl = sb("wl", [P, RING, CHUNK], F32R)
    x = sb("x", [P, KT, T])
    xn = sb("xn", [P, KT, T])
    xh = sb("xh", [P, KT, T], F32R)
    xl = sb("xl", [P, KT, T], F32R)
    hh = sb("hh", [P, 3, 512], F32R)
    hl = sb("hl", [P, 3, 512], F32R)
    root = sb("root", [P, T])
    rstd = sb("rstd", [P, T])
    ident = sb("ident", [P, P])
    ones = sb("ones", [P, P])
    vecT = sb("vecT", [P, 4, P])
    adaT = sb("adaT", [P, 2, 2, 48])
    epsc = sb("epsc", [P, 2])
    bias_rows = nc.dram_tensor("bias_rows", (16, BIAS_COLS), F32)
    nm = sb("nm", [P, 2, 2])
    rs = sb("rs", [P, 2, 2])
    ri = sb("ri", [P, 2, 2])
    cmask = sb("cmask", [P, 384])
    tri = sb("tri", [P, P])
    trib = sb("trib", [P, P], I32)
    wsm = sb("wsm", [P, KT, 136])
    bfox = sb("bfox", [P, 1])
    csil = sb("csil", [P, KT])
    arena = sb("arena", [P, ARENA])

    class Carver:

        def __init__(self, at=0):
            self.at = at

        def take(self, size, pattern=None, **sizes):
            v = arena[:, self.at:self.at + size]
            self.at += size
            assert self.at <= ARENA, self.at
            return v.rearrange(pattern, **sizes) if pattern else v

    c = Carver()
    fs = c.take(512, "p (f t) -> p f t", f=2)
    fh = c.take(3 * 512, "p (b f t) -> p b f t", b=3, f=2)
    ada_raw = c.take(2 * CHUNK, "p (b n) -> p b n", b=2)
    at_sum = c.at
    ada_sum = c.take(ADA_PER_FFN * T, "p (n t) -> p n t", n=ADA_PER_FFN)
    c = Carver()
    pj = c.take(12 * 512, "p (n t) -> p n t", n=12)
    glow = c.take(T)
    at_z = c.at
    zs, za, gk = c.take(2 * T), c.take(2 * T), c.take(2 * T)
    fz, fa, fsum = c.take(T), c.take(T), c.take(T)
    gs = c.take(2 * T, "p (m t) -> p m t", m=2)
    at_e = c.at
    eg, eng = c.take(2 * T), c.take(2 * T)
    eke = c.take(2 * T, "p (m t) -> p m t", m=2)
    qd = c.take(2 * T, "p (m t) -> p m t", m=2)
    at_k = c.at
    kd, ke = (c.take(2 * T, "p (m t) -> p m t", m=2) for _ in range(2))
    keT = c.take(2 * T, "p (b m d) -> p b m d", b=2, m=2)
    state = c.take(3 * 2 * DV, "p (c m v) -> p c m v", c=3, m=2)
    egl = c.take(8, "p (m c) -> p m c", m=2)
    sel = c.take(8 * P, "p (h q) -> p h q", h=8)
    wgate, bgate, onesT = c.take(T), c.take(T), c.take(T)
    assert c.at <= ARENA - 2304
    AT = pj[:, 0:2, :]
    osq, oroot, orstd = Carver(at_z).take(4 * T), Carver(at_e).take(4 * T), Carver(at_k).take(4 * T)
    c = Carver(ARENA - 2304)
    ns = c.take(2 * 384, "p (b k) -> p b k", b=2)
    pr = c.take(2 * 384, "p (b k) -> p b k", b=2)
    pt = c.take(2 * 384, "p (b k) -> p b k", b=2)
    c = Carver(7 * 512)
    kix, wix = c.take(T), c.take(T)
    wixT = c.take(TB * 8, "p (b h) -> p b h", b=TB)
    cT = c.take(2 * T, "p (l t) -> p l t", l=2)
    KTm = c.take(8 * T, "p (m t) -> p m t", m=8)
    wukT = c.take(2 * D, "p (l n) -> p l n", l=2)
    wuv = c.take(2 * D, "p (l n) -> p l n", l=2)
    at_b = c.at
    bias8 = c.take(16 * T, "p (h k) -> p h k", h=16)
    wuk = Carver(at_b).take(8 * T, "p (m l) -> p m l", m=8)
    at_m = c.at
    bm = c.take(3 * 384, "p (b k) -> p b k", b=3)
    csq = Carver(at_m).take(2 * T)
    dm = c.take(384)
    assert c.at <= ARENA - 2304
    Vm = xn[:, :, :].rearrange("p (b a) t -> p b (a t)", b=TB)
    c = Carver(ARENA - 2304)
    rl = c.take(2 * 384, "p (b k) -> p b k", b=2)
    sc = c.take(384)
    m8 = c.take(TB * 8, "p (b n) -> p b n", b=TB)
    c = Carver()
    pm = c.take(18 * 512, "p (n t) -> p n t", n=18)
    hpad = c.take(CT * (T + CONV_K - 1), "p (c t) -> p c t", c=CT)
    cacc = c.take(CT * T, "p (c t) -> p c t", c=CT)
    ctmp = c.take(CT * T, "p (c t) -> p c t", c=CT)
    ao = c.take(4 * T, "p (k t) -> p k t", k=4)
    yt = c.take(2 * 512, "p (b t) -> p b t", b=2)
    cmu = c.take(T)
    cosT, sinT, turn = c.take(T), c.take(T), c.take(P)
    freq = c.take(1)
    assert c.at <= ARENA - 2304
    c = Carver(9 * 1024)
    ang, turns, red = c.take(T), c.take(T), c.take(T)
    posi = c.take(T).bitcast(I32)
    part_turns = c.take(T)
    c = Carver(9 * 1024)
    bt = c.take(16 + 2 * BIAS_COLS)
    xin = c.take(TB * D, "p (b d) -> p b d", b=TB)
    rows = c.take(4 * P, "p (a d) -> p a d", a=4)

    bank = [ctx.enter_context(nc.psum_tensor(f"bank{i}", [P, 512], F32)) for i in range(8)]
    STAT = 6
    QUAD = (0, 1, 4, 5)

    loaded = [signal(f"loaded{i}") for i in range(RING)]
    hi_made = signal("hi_made")
    lo_made = signal("lo_made")
    chunk_used = signal("chunk_used")
    in_loaded = signal("in_loaded")
    const_made = signal("const_made")
    setup_pe = signal("setup_pe")
    vec_made = signal("vec_made")
    x_ready = signal("x_ready")
    sq_made = signal("sq_made")
    stat_made = signal("stat_made")
    root_made = signal("root_made")
    rstd_made = signal("rstd_made")
    xn_made = signal("xn_made")
    xh_made = signal("xh_made")
    xl_made = signal("xl_made")
    a_made = signal("a_made")
    act_made = signal("act_made")
    h_made = signal("h_made")
    hh_made = signal("hh_made")
    hl_made = signal("hl_made")
    proj_out = signal("proj_out")
    wsm_loaded = signal("wsm_loaded")
    small_made = signal("small_made")
    gla_pe = signal("gla_pe")
    gla_act = signal("gla_act")
    gla_dve = signal("gla_dve")
    bias_stored = signal("bias_stored")
    mla_loaded = signal("mla_loaded")
    bias_loaded = signal("bias_loaded")
    mla_pe = signal("mla_pe")
    mla_act = signal("mla_act")
    mla_dve = signal("mla_dve")
    bm_made = signal("bm_made")
    dve_step = signal("dve_step")
    act_step = signal("act_step")
    score_made = signal("score_made")
    ns_made = signal("ns_made")
    p_made = signal("p_made")
    pn_made = signal("pn_made")
    pt_made = signal("pt_made")
    pt_out = signal("pt_out")
    pv_made = signal("pv_made")
    rope_loaded = signal("rope_loaded")
    rope_made = signal("rope_made")
    csil_made = signal("csil_made")
    ada_loaded = [signal(f"ada_loaded{i}") for i in range(2)]
    pool_step = signal("pool_step")
    ada_summed = signal("ada_summed")
    ada_turned = signal("ada_turned")
    ada_made = signal("ada_made")
    wuv_loaded = signal("wuv_loaded")
    glu_made = signal("glu_made")
    conv_made = signal("conv_made")
    rope_pe = signal("rope_pe")
    rope_dve = signal("rope_dve")
    ao_made = signal("ao_made")
    cln_pe = signal("cln_pe")
    cln_act = signal("cln_act")
    cln_dve = signal("cln_dve")
    merged = signal("merged")
    y_out = signal("y_out")
    cen_made = signal("cen_made")
    ln_made = signal("ln_made")
    out_made = signal("out_made")
    out_copied = signal("out_copied")
    stored = signal("stored")

    x_ready.plan("in", 4)
    x_of, xstage, heads_of = {}, "in", {}
    for kind, s in STAGES:
        x_of[s] = xstage
        if kind == "rms":
            for g, n in ((sq_made, KT), (stat_made, 1), (root_made, 1), (rstd_made, 1)):
                g.plan(s, n)
            if s != "final":
                xn_made.plan(s, KT)
                xh_made.plan(s, KT)
                xl_made.plan(s, KT)
            else:
                x_ready.plan(s, KT)
                xstage = s
        if kind == "even":
            proj_out.plan(s, 12)
            xh_made.plan(s, 1 + 4)
            xl_made.plan(s, 1 + 4)
            x_ready.plan(s, 4)
            xstage = s
            heads_of[s] = 8
        if kind == "odd":
            proj_out.plan(s, 7)
            xh_made.plan(s, 8)
            xl_made.plan(s, 8)
            x_ready.plan(s, 4)
            xstage = s
            heads_of[s] = 16
        if kind == "mod":
            for g in (xn_made, xh_made, xl_made):
                g.plan(s, KT)
        if kind == "mix":
            heads_of[s] = 8
            proj_out.plan(s, 18)
            glu_made.plan(s, 1)
            conv_made.plan(s, CONV_K * CT)
            for g, n in ((rope_pe, 4), (rope_dve, 4), (ao_made, 4), (cln_pe, 2), (cln_act, 3 + CT), (cln_dve, 1 + CT),
                         (xh_made, 1 + CT + 4), (xl_made, 1 + CT + 4), (merged, 4), (y_out, 4), (x_ready, 4)):
                g.plan(s, n)
            xstage = s
        if kind == "ln":
            for g, n in ((stat_made, 2), (root_made, 2), (cen_made, 4), (sq_made, 4), (rstd_made, 1), (ln_made, KT), (x_ready, KT)):
                g.plan(s, n)
            xstage = s
        if kind == "sq":
            y_out.plan(s, 4)
        if s in heads_of:
            for g in (score_made, ns_made, p_made, pn_made, pt_made, pt_out, pv_made):
                g.plan(s, heads_of[s])
        if kind in ("ffn", "sq"):
            steps = FF_STEPS if kind == "ffn" else FF2_STEPS
            a_made.plan(s, steps)
            for g in (act_made, h_made, hh_made, hl_made):
                g.plan(s, 2 * steps)
            x_ready.plan(s, 4)
            xstage = s

    def xr(stage, k):
        src = x_of[stage]
        return x_ready.at(src, k + 1 if x_ready.times[src] == KT else k // 2 + 1)

    XL_FIRST = {"even": 1, "odd": 0}
    X_TILE = {"even": 4, "odd": 0, "mix0": 0, "mix1": 0}

    def vec(tile, row):
        return vecT[:, tile, row:row + 1]

    G_PE = {n: i + 1 for i, n in enumerate(["z", "G", "kt", "A", "kv", "o", "ostat"])}
    G_ACT = {n: i + 1 for i, n in enumerate(["glow", "z", "lnz", "lnf", "gs", "decays", "keT", "osq", "oroot"])}
    G_DVE = {n: i + 1 for i, n in enumerate(["fz", "zabs", "fabs", "gk", "fsum", "decayed", "A", "state", "o"])}
    EVEN = ["small", 0, "z", 1, "gk", 2, "G", 3, "decay", 4, 5, "kt", 6, "A", 7, "kv", 8, 9, 10, 11, "o", "norm"]
    EVEN_COLS = [256, 0, 512, 768, 1024, 1280, 1552, 1808, 2064, 2320, 2576, 2832]
    E_K, E_Q, E_V, E_G, F_Q, F_K, F_V = 0, 1, 2, 4, 6, 8, 10

    four, eight = range(4), range(8)
    M_PE = {n: i + 1 for i, n in enumerate([*(f"wuk{i}" for i in four), "small", "cstat", "widx", *(f"index{i}" for i in eight),
                                            *(f"K{i}" for i in four), *(f"V{i}" for i in four)])}
    M_ACT = {n: i + 1 for i, n in enumerate([*(f"wuk{i}" for i in four), "small", "csq", "croot", "widx",
                                             *(f"relu{i}" for i in eight), *(f"K{i}" for i in four), *(f"V{i}" for i in four)])}
    M_DVE = {n: i + 1 for i, n in enumerate(["c", *(f"scored{i}" for i in eight), "mask"])}
    ODD = ["wuk", 0, "small", 1, "cnorm", 2, "index", 3, "top", 4, "top", "K", 5, "top", "V", 6, "top", "mask"]
    ODD_COLS = [1024, 1280, 1536, 0, 256, 512, 768]
    O_C, O_QI, O_Q = 0, 1, 3
    SEARCH_ROUNDS = TOPK // 8 // ODD.count("top")

    MIX = [0, 1, 2, 3, "glu", 4, 5, "ropeq", 6, 7, "ropek", 8, 9]
    MIX_COLS = [1536 + 256 * i for i in range(4)] + [256 * i for i in range(6)] + [2560 + 256 * i for i in range(8)]
    X_Q, X_K, X_V, X_GA, X_GC = 4, 6, 8, 10, 14
    CONV_PER_STEP = 10

    def ada(l, part, k, plus_one=0):
        return adaT[:, l, plus_one, part * KT + k:part * KT + k + 1]

    def half(h):
        return slice(HD * (h % 2), HD * (h % 2) + HD)

    def in_slots(first, h, pj=pj):
        t = h // 2
        return pj[half(h), first + t // 2, (t % 2) * T:(t % 2 + 1) * T]

    def att_of(s):
        if s == "even":
            return (lambda h: in_slots(F_Q, h), lambda h: in_slots(F_K, h),
                    lambda h, b: pj[:, F_V + h // 4, b * T + (h % 4) * HD:b * T + (h % 4 + 1) * HD],
                    lambda h: cmask[:, :])

        if KIND[s] == "mix":
            return (lambda h: in_slots(X_Q, h, pm), lambda h: in_slots(X_K, h, pm),
                    lambda h, b: pm[:, X_V + h // 4, b * T + (h % 4) * HD:b * T + (h % 4 + 1) * HD],
                    lambda h: cmask[:, :])
        if s == "odd":
            return (lambda h: in_slots(O_Q, h), lambda h: KTm[half(h), h // 2, :],
                    lambda h, b: Vm[:, b, h * HD:(h + 1) * HD], lambda h: bm[:, h % 3, :])

    def steps_of(eng, n, head, body, step):
        turns = (n - head) // body
        for i in range(head):
            step(i, i, None)
        with eng.Fori(0, turns) as g:
            for j in range(body):
                step(g * body + (head + j), head + j, g)
        for i in range(head + turns * body, n):
            step(i, i, None)

    def ffn_shape(s):
        return (2, FF_STEPS, 2, 2) if KIND[s] == "ffn" else (1, FF2_STEPS, 3, 3)

    ADA_OF = {f"ffn{i}": divmod(i * ADA_PER_FFN, 24) for i in range(4)}
    for s in ADA_OF:
        ada_summed.plan(s, ADA_PER_FFN)
        ada_made.plan(s, 1)

    block = ctx.enter_context(nc.Block())

    N_CONST = 18

    @block.sync
    def _(sp):
        sp.dma_start(xin, A["x"][0].rearrange("(b p) d -> p b d", p=P)).then_inc(in_loaded.sem, 16)
        t0 = [("norm_g", "l i (k d) -> (l i k) d", V_NORM, 0), ("final_norm_g", "(k d) -> k d", V_FINAL, 0),
              ("gla_norm_g", "l (k d) -> (l k) d", V_GLA, 0), ("mla_kv_norm_g", "l (k d) -> (l k) d", V_MLA, 0),
              ("ln_mix_g_2", "l (k d) -> (l k) d", V_MIXG, 0), ("ln_mix_b_2", "l (k d) -> (l k) d", V_MIXB, 0),
              ("ln_ffn_g_2", "l (k d) -> (l k) d", V_FFNG, 0), ("ln_ffn_b_2", "l (k d) -> (l k) d", V_FFNB, 0),
              ("conv_dw_b_2", "l (k d) -> (l k) d", V_DWB, 1), ("conv_ln_g_2", "l (k d) -> (l k) d", V_CLNG, 1),
              ("conv_ln_b_2", "l (k d) -> (l k) d", V_CLNB, 1), ("c_2", "l (k d) -> (l k) d", V_C, 1),
              ("b_ada_2", "l (k d) -> (l k) d", V_ADA, 1)]
        for name, pattern, row, tile in t0:
            src = A[name].rearrange(pattern, d=P)
            sp.dma_start(rows[row:row + src.shape[0], tile, :], src).then_inc(in_loaded.sem, 16)
        for l in range(2):
            src = A["conv_dw_w_2"][l].rearrange("j (k d) -> (j k) d", d=P)
            sp.dma_start(rows[0:src.shape[0], 2 + l, :], src).then_inc(in_loaded.sem, 16)
        sp.dma_start(bt[0:32, 0:16], A["t5_table"]).then_inc(in_loaded.sem, 16)
        sp.dma_start(bt[0:32, 16:16 + BIAS_COLS], A["buckets"]).then_inc(in_loaded.sem, 16)
        w = A["even_w_in"][0].rearrange("(k p) n -> p k n", p=P)
        sp.wait_ge(const_made.sem, N_CONST)
        sp.dma_start(wsm[:, :, 0:16], w[:, :, 1536:1552]).then_inc(wsm_loaded.sem, 16)
        sp.dma_start(wsm[:, :, 32:40], w[:, :, 3088:3096]).then_inc(wsm_loaded.sem, 16)
        sp.dma_start(wgate[0:16, :], A["gla_w_gate"][0]).then_inc(wsm_loaded.sem, 16)
        sp.dma_start(bgate[0:1, :], A["gla_b_gate"]).then_inc(wsm_loaded.sem, 16)
        sp.dma_start(bfox[32:40, :], A["fox_b_f"].rearrange("a h -> h a")).then_inc(wsm_loaded.sem, 16)

        def load(c, src, view, turn=None, per_turn=0):
            if c >= RING:
                sp.wait_ge(lo_made.sem, shifted(c - RING + 1, turn, per_turn))
            sp.dma_start(raw[:, c % RING, :].rearrange(*view[0:1], **view[1]), src).then_inc(loaded[c % RING].sem, 16)

        A_VIEW = ("p (k n) -> p k n", {"k": KT})
        B_VIEW = ("p (k n) -> p k n", {"k": 2})

        def columns(w, col):
            return w.rearrange("(k p) n -> p k n", p=P)[:, :, bass.ds(col, 256)]

        def sp_ffn(s):
            n_in, steps, body, _ = ffn_shape(s)
            c0 = base[s]
            if KIND[s] == "ffn":
                l, i = divmod(int(s[3:]), 2)
                w_in, w_out = A["ffn_w_in"][l, i], A["ffn_w_out"][l, i]
            else:
                w_in, w_out = A["w_up_2"][int(s[2:])], A["w_down_2"][int(s[2:])]
            w_out = w_out.rearrange("(k p) n -> p k n", p=P)

            def step(i, st, turn):
                c = c0 + (0 if st == 0 else n_in + (n_in + 1) * (st - 1))
                per = (n_in + 1) * body
                for half in range(n_in):
                    load(c + half, columns(w_in, i * 256 + half * FF), A_VIEW, turn, per)
                if st > 0:
                    load(c + n_in, w_out[:, bass.ds(i * 2 - 2, 2), :], B_VIEW, turn, per)

            def load_ada(n, slot, times):
                l, first = ADA_OF[s]
                if times is not None:
                    sp.wait_ge(ada_summed.sem, times)
                sp.dma_start(ada_raw[:, slot, :].rearrange("p (k n) -> p k n", k=KT),
                             columns(A["w_ada_2"][l], (first + n) * T)).then_inc(ada_loaded[slot].sem, 16)

            def with_ada(i, st, turn):
                step(i, st, turn)
                if s in ADA_OF and st >= 2:
                    load_ada(i, st % 2, shifted(ada_summed.at(s, st - 1), turn, body))
                if s in ADA_OF and st == 1:
                    if s != "ffn0":
                        sp.wait_ge(x_ready.sem, x_ready.at(x_of[s]))
                    for n in range(2):
                        load_ada(n, n, ada_summed.at(s, 0) if s != "ffn0" else None)

            steps_of(sp, steps, 2, body, with_ada)
            if s in ADA_OF:
                load_ada(ADA_PER_FFN - 1, (ADA_PER_FFN - 1) % 2, ada_summed.at(s, ADA_PER_FFN - 2))
            if s == "ffn3":
                for dst, src in ((posi, A["positions_2"].broadcast_to((P, T))),
                                 (freq, A["rope_freq"]), (turn, A["rope_turn"])):
                    sp.dma_start(dst, src).then_inc(rope_loaded.sem, 16)
            load(c0 + (n_in + 1) * steps - 1, w_out[:, 2 * steps - 2:2 * steps, :], B_VIEW)

        def sp_even(s):
            w = A["even_w_in"][0]
            for n, col in enumerate(EVEN_COLS):
                load(base[s] + n, columns(w, col), A_VIEW)
            for j in range(4):
                load(base[s] + 12 + j, columns(A["even_w_out"][0], j * 256), A_VIEW)

        def sp_odd_small():
            sp.wait_ge(x_ready.sem, x_ready.at("even"))
            w = A["odd_w_in"][0].rearrange("(k p) n -> p k n", p=P)
            for at in (0, 64):
                sp.dma_start(wsm[:, :, at:at + 64], w[:, :, 1792:1856]).then_inc(wsm_loaded.sem, 16)
            sp.dma_start(wsm[:, :, 128:136], w[:, :, 1856:1864]).then_inc(wsm_loaded.sem, 16)
            sp.dma_start(wuk, A["mla_w_uk"][0].rearrange("(m a) d l -> (a d) m l", a=2)).then_inc(mla_loaded.sem, 16)

        def sp_odd(s):
            for n, col in enumerate(ODD_COLS):
                load(base[s] + n, columns(A["odd_w_in"][0], col), A_VIEW)
                if n == 3:
                    sp.wait_ge(mla_act.sem, M_ACT["wuk3"])
                    sp.wait_ge(mla_pe.sem, M_PE["wuk3"])
                    sp.wait_ge(bias_stored.sem, 16)
                    src = bass.AP(bias_rows, 0, [[1, P], [BIAS_COLS, 16], [1, T]])
                    sp.dma_start(bias8, src).then_inc(bias_loaded.sem, 16)
                if n == 2:
                    sp.wait_ge(ada_made.sem, ada_made.at("ffn2"))
                    for l in range(2):
                        sp.dma_start(wuv[:, l, :].rearrange("p (h d) -> p h d", d=HD),
                                     A["mla_w_uv"][0, :, l * P:(l + 1) * P, :].rearrange("h p d -> p h d")).then_inc(wuv_loaded.sem, 16)
            for j in range(4):
                load(base[s] + 7 + j, columns(A["odd_w_out"][0], j * 256), A_VIEW)

        def sp_mix(s):
            l, c0 = int(s[3:]), base[s]
            for n, col in enumerate(MIX_COLS):
                load(c0 + n, columns(A["w_in_2"][l], col), A_VIEW)
            for n in range(4):
                w = (A["w_attn_br_2"], A["w_conv_pw_2"])[n % 2][l].rearrange("(k p) n -> p k n", p=P)
                load(c0 + 18 + n, w[:, :, (n // 2) * 512:(n // 2 + 1) * 512], ("p (k n) -> p k n", {"k": 4}))
            for j in range(4):
                load(c0 + 22 + j, columns(A["w_out_2"][l], j * 256), A_VIEW)

        for kind, s in STAGES:
            if kind == "mix":
                sp_mix(s)
            if kind in ("ffn", "sq"):
                sp_ffn(s)
                if s == "ffn1":
                    sp_odd_small()
            if kind == "odd":
                sp_odd(s)
            if kind == "even":
                sp_even(s)
        for b in range(TB):
            sp.wait_ge(out_copied.sem, 2 * b + 2)
            sp.dma_start(out[0, b * P:(b + 1) * P, :], xin[:, b, :]).then_inc(stored.sem, 16)
        sp.wait_ge(stored.sem, 16 * TB)

    N_IN = 16 * 18

    @block.gpsimd
    def _(pool):
        made = [0]

        def const(ins):
            made[0] += 1
            ins.then_inc(const_made.sem, 1)
            pool.wait_ge(const_made.sem, made[0])

        def keep(m, compare, fill, base, pattern, per_partition):
            const(pool.affine_select(out=m, in_=m, compare_op=compare, fill=fill, base=base, pattern=pattern,
                                     channel_multiplier=per_partition))

        const(pool.memset(ident[:, :], 0.0))
        keep(ident[:, :], ALU.not_equal, 1.0, 0, [[-1, P]], 1)
        const(pool.memset(ones[:, :], 1.0))
        const(pool.memset(epsc[:, 0:1], EPS))
        const(pool.memset(epsc[:, 1:2], LN_EPS))
        const(pool.memset(wsm[:, :, 0:40], 0.0))
        const(pool.memset(onesT, 1.0))
        const(pool.memset(sel[32:40, :, :], 0.0))
        keep(sel[32:40, :, :], ALU.not_equal, -8.0, 0, [[-1, 8], [0, P]], 1)
        const(pool.memset(cmask[:, :], 0.0))
        for at in (0, 256):
            keep(cmask[:, at:at + P], ALU.is_ge, NEG, 0, [[-1, P]], 1)
        for m, value in ((tri, 1.0 / 16), (trib, 1)):
            const(pool.memset(m[:, :], value))
            keep(m[:, :], ALU.is_ge, 0.0, 0, [[1, P]], -1)
            const(pool.memset(m[0:CH, CH:P], 0))
        assert made[0] == N_CONST

        def pool_odd(s):
            pool.wait_ge(bias_loaded.sem, 16)
            pool.wait_ge(mla_dve.sem, M_DVE["mask"])
            for h in range(heads_of[s]):
                if h >= 3:
                    pool.wait_ge(ns_made.sem, ns_made.at(s, h - 2))
                pool.tensor_tensor(bm[:, h % 3, 0:P], bias8[:, h, P - 1::-1], dm[:, 0:P], ALU.add)
                pool.tensor_tensor(bm[:, h % 3, P:384], bias8[:, h, ::-1], dm[:, P:384], ALU.add).then_inc(bm_made.sem, 1)

        def link(ins):
            n_step[0] += 1
            ins.then_inc(pool_step.sem, 1)
            pool.wait_ge(pool_step.sem, n_step[0])

        n_step = [0]

        def pool_ada(s):
            first, c0 = n_step[0], ada_summed.at(s, 0)
            per_chunk = 3
            pool.wait_ge(csil_made.sem, 1)
            if s != "ffn0":
                pool.wait_ge(ada_turned.sem, int(s[3:]))
            with pool.Fori(0, ADA_PER_FFN // 2) as g:
                for slot in range(2):
                    def done(n):
                        return g * (2 * per_chunk) + (first + slot * per_chunk + n)
                    w = ada_raw[:, slot, :]
                    tiles = w.rearrange("p (k n) -> p k n", k=KT)
                    pool.wait_ge(ada_loaded[slot].sem, g * 16 + 16 * (c0 // 2 + 1))
                    pool.tensor_tensor(tiles, tiles, csil[:, :].unsqueeze(2).broadcast_to((P, KT, T)), ALU.mult).then_inc(pool_step.sem, 1)
                    for n, size in ((1, 1024), (2, 512)):
                        pool.wait_ge(pool_step.sem, done(n))
                        pool.tensor_tensor(w[:, 0:size], w[:, 0:size], w[:, size:2 * size], ALU.add).then_inc(pool_step.sem, 1)
                    pool.wait_ge(pool_step.sem, done(3))
                    pool.tensor_tensor(arena[:, bass.ds(g * (2 * T) + (at_sum + slot * T), T)], w[:, 0:T], w[:, T:2 * T],
                                       ALU.add).then_inc(ada_summed.sem, 1)
            n_step[0] += per_chunk * ADA_PER_FFN

        def pool_rope():
            pool.wait_ge(rope_loaded.sem, 16 * 3)
            link(pool.tensor_copy(turns, posi))
            link(pool.tensor_scalar(ang, turns, freq, None, ALU.mult))
            for i in range(2):
                link(pool.tensor_scalar(turns, ang, 1 / (2 * math.pi), 0.25 * i, ALU.mult, ALU.add))
                link(pool.tensor_scalar(turns, turns, ROUND, ROUND, ALU.add, ALU.subtract))
                if i == 1:
                    pool.wait_ge(rope_made.sem, 2)
                src = ang
                for part in TWO_PI:
                    link(pool.tensor_scalar(part_turns, turns, part, None, ALU.mult))
                    link(pool.tensor_tensor(red, src, part_turns, ALU.subtract))
                    src = red
                link(pool.tensor_scalar(red, red, 0.5 * math.pi * i, PI_BELOW, ALU.add, ALU.min))
                pool.tensor_scalar(red, red, -PI_BELOW, None, ALU.max).then_inc(rope_made.sem, 1)

        for kind, s in STAGES:
            if kind == "odd":
                pool_odd(s)
            if s in ADA_OF:
                pool_ada(s)
            if kind == "ada":
                pool_rope()

    @block.tensor
    def _(pe):
        def three(o, wa, wb, ma, mb, start, stop, **kw):
            pe.matmul(o, wa, ma, start=start, stop=False, **kw)
            pe.matmul(o, wa, mb, start=False, stop=False, **kw)
            return pe.matmul(o, wb, ma, start=False, stop=stop, **kw)

        def tile_of(c, k, m, n):
            at = slice(k * n + m * P, k * n + (m + 1) * P)
            return wh[:, c % RING, at], wl[:, c % RING, at]

        def pe_setup():
            pe.wait_ge(const_made.sem, N_CONST)
            pe.wait_ge(in_loaded.sem, N_IN)
            for v in range(4):
                last = pe.transpose(bank[7][:, v * P:v * P + V_ROWS[v]], rows[0:V_ROWS[v], v, :],
                                    ident[0:V_ROWS[v], 0:V_ROWS[v]])
            last.then_inc(setup_pe.sem, 1)
            pe.matmul(bank[STAT][0:16, 0:BIAS_COLS], bt[0:32, 0:16], bt[0:32, 16:16 + BIAS_COLS], start=True,
                      stop=True).then_inc(setup_pe.sem, 1)
            for q in range(4):
                for j in range(2):
                    for b in range(TB):
                        k = 2 * q + j
                        last = pe.transpose(bank[q][:, j * T + b * P:j * T + (b + 1) * P],
                                            xin[:, b, k * P:(k + 1) * P], ident[:, :])
                last.then_inc(setup_pe.sem, 1)

        def pe_rms(s):
            for k in range(KT):
                pe.wait_ge(sq_made.sem, sq_made.at(s, k + 1))
                last = pe.matmul(bank[STAT][:, 0:T], ones[:, :], xn[:, k, :], start=(k == 0), stop=(k == KT - 1))
            last.then_inc(stat_made.sem, 1)

        def pe_ffn(s, moving):
            n_in, steps, body, bufs = ffn_shape(s)
            c0 = base[s]

            def down(c, i, st, turn):
                pe.wait_ge(lo_made.sem, shifted(c + 1, turn, (n_in + 1) * body))
                pe.wait_ge(hl_made.sem, shifted(hl_made.at(s, 2 * st + 2), turn, 2 * body))
                for k in range(2):
                    for m in range(KT):
                        o = bank[m // 2][:, (m % 2) * T:(m % 2 + 1) * T]
                        a, b = tile_of(c, k, m, D)
                        mv = slice(k * T, (k + 1) * T)
                        last = three(o, a, b, hh[:, st % bufs, mv], hl[:, st % bufs, mv],
                                     start=(st == 0 and k == 0 and m % 2 == 0),
                                     stop=(st == steps - 1 and k == 1), skip_group_check=True)
                last.then_inc(chunk_used.sem, 1)

            def step(i, st, turn):
                c = c0 + (0 if st == 0 else n_in + (n_in + 1) * (st - 1))
                per = (n_in + 1) * body
                if st > 0:
                    pe.wait_ge(h_made.sem, shifted(h_made.at(s, 2 * st), turn, 2 * body))
                for half in range(n_in):
                    pe.wait_ge(lo_made.sem, shifted(c + half + 1, turn, per))
                    for f in range(2):
                        for k in range(KT):
                            if st == 0 and half == 0 and f == 0:
                                pe.wait_ge(xl_made.sem, xl_made.at(moving, k + 1))
                            last = three(bank[4 + f][:, half * T:(half + 1) * T], *tile_of(c + half, k, f, T),
                                         xh[:, k, :], xl[:, k, :], start=(k == 0), stop=(k == KT - 1))
                        if f == 0 and half == n_in - 1:
                            last.then_inc(a_made.sem, 1)
                    last.then_inc(chunk_used.sem, 1)
                if st > 0:
                    down(c + n_in, i, st - 1, turn)

            steps_of(pe, steps, 2, body, step)
            down(c0 + (n_in + 1) * steps - 1, None, steps - 1, None)

        def pe_chunk(s, n, c, tokens_out, moving, first):
            if n >= 2:
                pe.wait_ge(proj_out.sem, proj_out.at(s, n - 1))
            pe.wait_ge(lo_made.sem, c + 1)
            for m in range(2):
                for k in range(KT):
                    if first and m == 0:
                        pe.wait_ge(xl_made.sem, xl_made.at(moving, k + 1))
                    o = bank[2 + n % 2][:, m * T:(m + 1) * T]
                    if tokens_out:
                        tok = slice(m * P, (m + 1) * P)
                        col = slice(k * T, (k + 1) * T)
                        last = three(o, xh[:, k, tok], xl[:, k, tok], wh[:, c % RING, col], wl[:, c % RING, col],
                                     start=(k == 0), stop=(k == KT - 1))
                    else:
                        last = three(o, *tile_of(c, k, m, T), xh[:, k, :], xl[:, k, :], start=(k == 0), stop=(k == KT - 1))
            last.then_inc(chunk_used.sem, 1)

        def pe_out(s, c0):
            pe.wait_ge(xl_made.sem, xl_made.at(s))
            for j in range(4):
                c = c0 + j
                pe.wait_ge(lo_made.sem, c + 1)
                if j >= 2:
                    if KIND[s] == "mix":
                        pe.wait_ge(y_out.sem, y_out.at(s, j - 1))
                    else:
                        pe.wait_ge(x_ready.sem, x_ready.at(s, j - 1))
                for m in range(2):
                    for k in range(KT):
                        last = three(bank[2 + j % 2][:, m * T:(m + 1) * T], *tile_of(c, k, m, T), xh[:, k, :], xl[:, k, :],
                                     start=(k == 0), stop=(k == KT - 1))
                last.then_inc(chunk_used.sem, 1)

        def pe_attention(s, meanwhile=None):
            H = heads_of[s]
            q, k, v, _ = att_of(s)

            def scores(h):
                if h >= 2:
                    pe.wait_ge(ns_made.sem, ns_made.at(s, h - 1))
                b = bank[4 + h % 2]
                fox = s == "even"
                for o, qt, kt in ((b[:, 0:P], slice(0, P), slice(0, P)), (b[:, P:384], slice(P, T), slice(0, T))):
                    last = pe.matmul(o, q(h)[:, qt], k(h)[:, kt], start=True, stop=not fox)
                    if fox:
                        last = pe.matmul(o, sel[32:40, h, :], fsum[32:40, kt], start=False, stop=True)
                last.then_inc(score_made.sem, 1)

            def transposes(h):
                pe.wait_ge(pn_made.sem, pn_made.at(s, h + 1))
                if h >= 2:
                    pe.wait_ge(pt_out.sem, pt_out.at(s, h - 1))
                for j in range(3):
                    at = slice(j * P, (j + 1) * P)
                    last = pe.transpose(bank[6 + h % 2][:, at], pr[:, h % 2, at], ident[:, :])
                last.then_inc(pt_made.sem, 1)

            def output(h):
                pe.wait_ge(pt_out.sem, pt_out.at(s, h + 1))
                pair = h // 2
                if pair >= 2 and h % 2 == 0:
                    if KIND[s] == "mix":
                        pe.wait_ge(ao_made.sem, ao_made.at(s, pair - 1))
                    else:
                        pe.wait_ge(xl_made.sem, xl_made.at(s, XL_FIRST[s] + pair - 1))
                b = bank[pair % 2]
                pe.matmul(b[half(h), 0:T], v(h, 0), pt[:, h % 2, 0:T], start=True, stop=False)
                pe.matmul(b[half(h), P:T], v(h, 1), pt[:, h % 2, T:384], start=False, stop=True).then_inc(pv_made.sem, 1)

            for i in range(H + 2):
                if i < H:
                    scores(i)
                if meanwhile:
                    meanwhile(i)
                if 1 <= i <= H:
                    transposes(i - 1)
                if i >= 2:
                    output(i - 2)

        def pe_even(s, moving):
            c0 = base[s]

            def small():
                pe.wait_ge(wsm_loaded.sem, 16 * 5)
                for k in range(KT):
                    pe.wait_ge(xn_made.sem, xn_made.at(moving, k + 1))
                    last = pe.matmul(bank[STAT][0:40, 0:T], wsm[:, k, 0:40], xn[:, k, :], start=(k == 0), stop=(k == KT - 1))
                last.then_inc(small_made.sem, 1)

            def z():
                pe.wait_ge(gla_act.sem, G_ACT["glow"])
                for b in range(TB):
                    o = bank[7][:, b * T:(b + 1) * T]
                    pe.matmul(o, glow[0:16, b * P:(b + 1) * P], wgate[0:16, :], start=True, stop=False)
                    last = pe.matmul(o, ones[0:1, :], bgate[0:1, :], start=False, stop=True)
                last.then_inc(gla_pe.sem, 1)

            def cumulate():
                pe.wait_ge(gla_dve.sem, G_DVE["gk"])
                for m in range(2):
                    for b in range(TB):
                        last = pe.matmul(bank[7][:, m * T + b * P:m * T + (b + 1) * P],
                                         gk[:, b * T + m * P:b * T + (m + 1) * P], tri[:, :], start=True, stop=True)
                last.then_inc(gla_pe.sem, 1)

            def turn_keys():
                pe.wait_ge(gla_dve.sem, G_DVE["decayed"])
                for b in range(TB):
                    for m in range(2):
                        last = pe.transpose(bank[7][:, (b * 2 + m) * P:(b * 2 + m + 1) * P], ke[:, m, b * P:(b + 1) * P], ident[:, :])
                last.then_inc(gla_pe.sem, 1)

            def scores():
                pe.wait_ge(gla_act.sem, G_ACT["keT"])
                for h in range(4):
                    for b in range(TB):
                        tok = slice(b * P, (b + 1) * P)
                        last = pe.matmul(bank[6 + h % 2][:, (h // 2) * T + b * P:(h // 2) * T + (b + 1) * P],
                                         kd[half(h), h // 2, tok], qd[half(h), h // 2, tok], start=True, stop=True)
                last.then_inc(gla_pe.sem, 1)

            def chunk_states():
                pe.wait_ge(gla_dve.sem, G_DVE["A"])
                for ch in range(3):
                    rows_ = slice((ch % 2) * CH, (ch % 2 + 1) * CH)
                    for h in range(4):
                        o = bank[6 + ch % 2][half(h), (ch // 2) * T + (h // 2) * P:(ch // 2) * T + (h // 2 + 1) * P]
                        last = pe.matmul(o, keT[rows_, ch // 2, h // 2, half(h)],
                                         pj[rows_, E_V + h // 2, (ch // 2) * T + (h % 2) * P:(ch // 2) * T + (h % 2 + 1) * P],
                                         start=True, stop=True)
                last.then_inc(gla_pe.sem, 1)

            def outputs():
                pe.wait_ge(gla_dve.sem, G_DVE["state"])
                for h in range(4):
                    o, at = bank[6 + h % 2], (h // 2) * T
                    for b in range(TB):
                        pe.matmul(o[:, at + b * P:at + (b + 1) * P],
                                  pj[:, E_V + h // 2, b * T + (h % 2) * P:b * T + (h % 2 + 1) * P],
                                  AT[:, h % 2, at + b * P:at + (b + 1) * P],
                                  start=(h // 2 == 0 and b == 0), stop=False, skip_group_check=True)
                    for ch in range(1, 4):
                        last = pe.matmul(o[:, at + ch * CH:at + (ch + 1) * CH], state[half(h), ch - 1, h // 2, :],
                                         qd[half(h), h // 2, ch * CH:(ch + 1) * CH], start=False, stop=True, skip_group_check=True)
                last.then_inc(gla_pe.sem, 1)

            def norm():
                pe.wait_ge(gla_act.sem, G_ACT["osq"])
                for q in range(2):
                    last = pe.matmul(bank[4 + q][:, :], ones[:, :], osq[:, q * 512:(q + 1) * 512], start=True, stop=True)
                last.then_inc(gla_pe.sem, 1)

            todo = {"small": small, "z": z, "G": cumulate, "kt": turn_keys, "A": scores, "kv": chunk_states,
                    "o": outputs, "norm": norm}
            for step in EVEN:
                if isinstance(step, int):
                    pe_chunk(s, step, c0 + step, step in (2, 3, 10, 11), moving, step == 0)
                elif step in todo:
                    todo[step]()
            pe.wait_ge(xl_made.sem, xl_made.at(s, 1))
            pe.wait_ge(gla_dve.sem, G_DVE["fsum"])
            pe_attention(s)
            pe_out(s, c0 + 12)

        def pe_odd(s, moving):
            c0 = base[s]

            def turn_wuk():
                pe.wait_ge(mla_loaded.sem, 16)
                for g in range(4):
                    for j in range(4):
                        m = 4 * (g % 2) + j
                        last = pe.transpose(bank[QUAD[g]][:, j * P:(j + 1) * P], wuk[:, m, (g // 2) * P:(g // 2 + 1) * P], ident[:, :])
                    last.then_inc(mla_pe.sem, 1)

            def small():
                pe.wait_ge(wsm_loaded.sem, 16 * 8)
                for o, cols in ((bank[6][:, 0:T], slice(0, P)), (bank[6][0:8, T:2 * T], slice(P, P + 8))):
                    for k in range(KT):
                        pe.wait_ge(xn_made.sem, xn_made.at(moving, k + 1))
                        last = pe.matmul(o, wsm[:, k, cols], xn[:, k, :], start=(k == 0), stop=(k == KT - 1))
                last.then_inc(mla_pe.sem, 1)

            def cnorm():
                pe.wait_ge(mla_act.sem, M_ACT["csq"])
                for l in range(2):
                    last = pe.matmul(bank[7][:, 0:T], ones[:, :], csq[:, l * T:(l + 1) * T], start=(l == 0), stop=(l == 1))
                last.then_inc(mla_pe.sem, 1)
                for b in range(TB):
                    last = pe.transpose(bank[6][:, b * 8:(b + 1) * 8], wix[0:8, b * P:(b + 1) * P], ident[0:8, 0:8])
                last.then_inc(mla_pe.sem, 1)

            def index():
                for h in range(8):
                    pe.wait_ge(proj_out.sem, proj_out.at(s, 3))
                    pe.wait_ge(mla_act.sem, M_ACT[f"relu{h - 4}"] if h >= 4 else M_ACT["widx"])
                    b = bank[QUAD[h % 4]]
                    for o, qt, kt in ((b[:, 0:P], slice(0, P), slice(0, P)), (b[:, P:384], slice(P, T), slice(0, T))):
                        last = pe.matmul(o, in_slots(O_QI, h)[:, qt], kix[half(h), kt], start=True, stop=True)
                    last.then_inc(mla_pe.sem, 1)

            def keys():
                pe.wait_ge(mla_act.sem, M_ACT["relu7"])
                pe.wait_ge(mla_dve.sem, M_DVE["c"])
                for g in range(4):
                    for j in range(2):
                        for l in range(2):
                            m = 2 * g + j
                            last = pe.matmul(bank[QUAD[g]][:, j * T:(j + 1) * T], wukT[:, l, m * P:(m + 1) * P], cT[:, l, :],
                                             start=(l == 0), stop=(l == 1))
                    last.then_inc(mla_pe.sem, 1)

            def values():
                pe.wait_ge(wuv_loaded.sem, 16 * 2)
                for g in range(4):
                    pe.wait_ge(mla_act.sem, M_ACT[f"K{g}"])
                    for l in range(2):
                        last = pe.matmul(bank[QUAD[g]][:, :], cT[:, l, (g // 2) * P:(g // 2 + 1) * P],
                                         wuv[:, l, (g % 2) * 512:(g % 2 + 1) * 512], start=(l == 0), stop=(l == 1))
                    last.then_inc(mla_pe.sem, 1)

            todo = {"wuk": turn_wuk, "small": small, "cnorm": cnorm, "index": index, "K": keys, "V": values}
            for step in ODD:
                if isinstance(step, int):
                    pe_chunk(s, step, c0 + step, False, moving, step == 0)
                elif step in todo:
                    todo[step]()
            pe.wait_ge(mla_act.sem, M_ACT["V3"])
            pe.wait_ge(proj_out.sem, proj_out.at(s))
            pe_attention(s)
            pe_out(s, c0 + 7)

        def pe_ada(s):
            pe.wait_ge(ada_summed.sem, ada_summed.at(s))
            for n in range(2 * ADA_PER_FFN):
                last = pe.matmul(bank[7][:, n:n + 1], ada_sum[:, n // 2, (n % 2) * P:(n % 2 + 1) * P], ones[:, 0:1], start=True, stop=True)
            last.then_inc(ada_turned.sem, 1)

        def pe_mix(s, moving):
            c0 = base[s]

            def turned(first):
                for i in range(2):
                    n = first + i
                    pe.wait_ge(proj_out.sem, proj_out.at(s, n + 1))
                    if first == X_K:
                        pe.wait_ge(rope_dve.sem, rope_dve.at(s, i + 1))
                    for m in range(2):
                        last = pe.matmul(bank[6 + i][:, m * T:(m + 1) * T], turn, pm[:, n, m * T:(m + 1) * T], start=True, stop=True)
                    last.then_inc(rope_pe.sem, 1)

            todo = {"ropeq": lambda: turned(X_Q), "ropek": lambda: turned(X_K)}
            for step in MIX:
                if isinstance(step, int):
                    pe_chunk(s, step, c0 + step, step in (8, 9), moving, step == 0)
                elif step in todo:
                    todo[step]()
            pe.wait_ge(proj_out.sem, proj_out.at(s, 10))
            pe.wait_ge(rope_dve.sem, rope_dve.at(s))
            pe_attention(s, lambda i: pe_chunk(s, 10 + i, c0 + 10 + i, False, moving, False) if i < 8 else None)
            pe.wait_ge(conv_made.sem, conv_made.at(s))
            for ct in range(CT):
                last = pe.matmul(bank[6][:, 0:T], ones[:, :], cacc[:, ct, :], start=(ct == 0), stop=(ct == CT - 1))
            last.then_inc(cln_pe.sem, 1)
            pe.wait_ge(cln_act.sem, cln_act.at(s, 2))
            for ct in range(CT):
                last = pe.matmul(bank[7][:, 0:T], ones[:, :], ctmp[:, ct, :], start=(ct == 0), stop=(ct == CT - 1))
            last.then_inc(cln_pe.sem, 1)
            pe.wait_ge(proj_out.sem, proj_out.at(s))
            for n in range(4):
                c, first = c0 + 18 + n, (0, 2, 4, 6)[n]
                pe.wait_ge(lo_made.sem, c + 1)
                pe.wait_ge(xl_made.sem, xl_made.at(s, 1 if n % 2 == 0 else 1 + CT))
                for m in range(4):
                    for k in range(4):
                        at = slice(k * 512 + m * P, k * 512 + (m + 1) * P)
                        kk = 4 * (n % 2) + k
                        last = three(bank[first + m // 2][:, (m % 2) * T:(m % 2 + 1) * T], wh[:, c % RING, at], wl[:, c % RING, at],
                                     xh[:, kk, :], xl[:, kk, :], start=(k == 0), stop=(k == 3))
                last.then_inc(chunk_used.sem, 1)
            pe_out(s, c0 + 22)

        def pe_ln(s):
            for k in range(KT):
                pe.wait_ge(x_ready.sem, xr(s, k))
                last = pe.matmul(bank[6][:, 0:T], ones[:, :], x[:, k, :], start=(k == 0), stop=(k == KT - 1))
            last.then_inc(stat_made.sem, 1)
            for k in range(KT):
                pe.wait_ge(sq_made.sem, sq_made.at(s, k // 2 + 1))
                last = pe.matmul(bank[7][:, 0:T], ones[:, :], xn[:, k, :], start=(k == 0), stop=(k == KT - 1))
            last.then_inc(stat_made.sem, 1)

        def pe_store():
            for b in range(TB):
                for q in range(2):
                    n = 2 * b + q
                    for k in range(4 * q, 4 * q + 4):
                        pe.wait_ge(x_ready.sem, x_ready.at(xstage))
                        last = pe.transpose(bank[n][:, (k % 4) * P:(k % 4 + 1) * P], x[:, k, b * P:(b + 1) * P], ident[:, :])
                    last.then_inc(out_made.sem, 1)

        pe_setup()
        moving = None
        for kind, s in STAGES:
            if kind == "rms":
                pe_rms(s)
                moving = s
            if kind in ("ffn", "sq"):
                pe_ffn(s, moving)
            if s in ADA_OF:
                pe_ada(s)
            if kind == "even":
                pe_even(s, moving)
            if kind == "odd":
                pe_odd(s, moving)
            if kind == "mod":
                moving = s
            if kind == "mix":
                pe_mix(s, moving)
            if kind == "ln":
                pe_ln(s)
        pe_store()

    @block.scalar
    def _(act):
        def hi(c, turn=None, per_turn=0):
            if turn is None and c >= n_chunks:
                return
            act.wait_ge(loaded[c % RING].sem, shifted(16 * (c // RING + 1), turn, 16 * per_turn // RING))
            if c >= RING:
                act.wait_ge(chunk_used.sem, shifted(c - RING + 1, turn, per_turn))
            act.activation(wh[:, c % RING, :], raw[:, c % RING, :], ACT.Copy).then_inc(hi_made.sem, 1)

        def act_setup():
            rows8 = bt[0:16, 16 + BIAS_COLS:16 + 2 * BIAS_COLS]
            act.wait_ge(setup_pe.sem, 2)
            act.activation(rows8, bank[STAT][0:16, 0:BIAS_COLS], ACT.Copy, scale=8.0).then_inc(act_step.sem, 1)
            act.wait_ge(act_step.sem, 1)
            act.dma_start(bias_rows.ap(), rows8).then_inc(bias_stored.sem, 16)
            for q in range(4):
                act.wait_ge(setup_pe.sem, q + 3)
                act.activation(x[:, 2 * q:2 * q + 2, :].rearrange("p k t -> p (k t)"), bank[q][:, :], ACT.Copy).then_inc(x_ready.sem, 1)

        def act_rms(s):
            for k in range(KT):
                act.wait_ge(x_ready.sem, xr(s, k))
                act.activation(xn[:, k, :], x[:, k, :], ACT.Square).then_inc(sq_made.sem, 1)
            act.wait_ge(stat_made.sem, stat_made.at(s))
            act.activation(root[:, :], bank[STAT][:, 0:T], ACT.Sqrt, scale=1.0 / D, bias=epsc[:, 0:1]).then_inc(root_made.sem, 1)
            if s == "final":
                return
            for k in range(KT):
                act.wait_ge(xn_made.sem, xn_made.at(s, k + 1))
                act.activation(xh[:, k, :], xn[:, k, :], ACT.Copy).then_inc(xh_made.sem, 1)

        def act_ffn(s):
            n_in, steps, body, bufs = ffn_shape(s)
            func = ACT.Silu if KIND[s] == "ffn" else ACT.Relu
            c0 = base[s]

            def step(i, st, turn):
                c = c0 + (0 if st == 0 else n_in + (n_in + 1) * (st - 1))
                per = (n_in + 1) * body
                if n_in == 2:
                    hi(c + RING, turn, per)
                act.wait_ge(a_made.sem, shifted(a_made.at(s, st + 1), turn, body))
                act.activation(fs[:, 0, :], bank[4][:, 0:T], func).then_inc(act_made.sem, 1)
                act.wait_ge(chunk_used.sem, shifted(c + n_in, turn, per))
                act.activation(fs[:, 1, :], bank[5][:, 0:T], func).then_inc(act_made.sem, 1)
                hi(c + n_in - 1 + RING, turn, per)
                for f in range(2):
                    act.wait_ge(h_made.sem, shifted(h_made.at(s, 2 * st + f + 1), turn, 2 * body))
                    act.activation(hh[:, st % bufs, f * T:(f + 1) * T], fh[:, st % bufs, f, :], ACT.Copy).then_inc(hh_made.sem, 1)
                if st > 0:
                    hi(c + n_in + RING, turn, per)

            steps_of(act, steps, 2, body, step)
            if KIND[s] == "sq":
                act.wait_ge(chunk_used.sem, c0 + (n_in + 1) * steps)
                for q in range(4):
                    if q >= 2:
                        act.wait_ge(x_ready.sem, x_ready.at(s, q - 1))
                    for m in range(2):
                        last = act.activation(yt[:, q % 2, m * T:(m + 1) * T], bank[q][:, m * T:(m + 1) * T], ACT.Identity,
                                              scale=ada(int(s[2:]), 5, 2 * q + m, 1))
                    last.then_inc(y_out.sem, 1)
            hi(c0 + (n_in + 1) * steps - 1 + RING)

        n_step = [1]

        def link(ins):
            n_step[0] += 1
            ins.then_inc(act_step.sem, 1)
            act.wait_ge(act_step.sem, n_step[0])

        def act_chunk(s, n, c, func=ACT.Copy, pj=pj):
            act.wait_ge(chunk_used.sem, c + 1)
            act.activation(pj[:, n, :], bank[2 + n % 2][:, :], func).then_inc(proj_out.sem, 1)
            hi(c + RING)

        def act_attention(s, meanwhile=None):
            H = heads_of[s]

            def exps(h):
                act.wait_ge(ns_made.sem, ns_made.at(s, h + 1))
                if h >= 2:
                    act.wait_ge(pt_made.sem, pt_made.at(s, h - 1))
                act.activation(pr[:, h % 2, 0:P], ns[:, h % 2, 0:P], ACT.Exp, bias=nm[:, h % 2, 0:1], scale=-1.0,
                               accum_out=rs[:, h % 2, 0:1])
                act.activation(pr[:, h % 2, P:384], ns[:, h % 2, P:384], ACT.Exp, bias=nm[:, h % 2, 1:2], scale=-1.0,
                               accum_out=rs[:, h % 2, 1:2]).then_inc(p_made.sem, 1)

            def evacuate(h):
                act.wait_ge(pt_made.sem, pt_made.at(s, h + 1))
                act.activation(pt[:, h % 2, :], bank[6 + h % 2][:, 0:384], ACT.Copy).then_inc(pt_out.sem, 1)

            def upper(pair):
                act.wait_ge(pv_made.sem, pv_made.at(s, 2 * pair + 2))
                if KIND[s] == "mix":
                    act.activation(ao[:, pair, :], bank[pair % 2][:, 0:T], ACT.Copy).then_inc(ao_made.sem, 1)
                    return
                act.activation(xh[:, X_TILE[s] + pair, :], bank[pair % 2][:, 0:T], ACT.Copy).then_inc(xh_made.sem, 1)

            for i in range(H + 3):
                if i < H:
                    exps(i)
                if 1 <= i <= H:
                    evacuate(i - 1)
                if meanwhile:
                    meanwhile(i)
                if i >= 3 and i % 2 == 1:
                    upper((i - 3) // 2)

        def act_even(s):
            c0 = base[s]
            act.wait_ge(bias_stored.sem, 16)

            def small():
                act.wait_ge(small_made.sem, 1)
                act.activation(glow[0:16, :], bank[STAT][0:16, 0:T], ACT.Copy).then_inc(gla_act.sem, 1)

            def z():
                act.wait_ge(gla_pe.sem, G_PE["z"])
                act.activation(zs, bank[7][:, :], ACT.Copy).then_inc(gla_act.sem, 1)

            def log_sigmoid():
                act.wait_ge(gla_dve.sem, G_DVE["fabs"])
                link(act.activation(za, za, ACT.Exp, scale=-1.0))
                link(act.activation(fa[32:40, :], fa[32:40, :], ACT.Exp, scale=-1.0))
                act.activation(za, za, ACT.Ln, bias=1.0).then_inc(gla_act.sem, 1)
                act.activation(fa[32:40, :], fa[32:40, :], ACT.Ln, bias=1.0).then_inc(gla_act.sem, 1)

            def cumulated():
                act.wait_ge(gla_pe.sem, G_PE["G"])
                act.activation(gs.rearrange("p m t -> p (m t)"), bank[7][:, :], ACT.Copy).then_inc(gla_act.sem, 1)

            def decays():
                act.wait_ge(gla_act.sem, G_ACT["gs"])
                g = gs.rearrange("p m t -> p (m t)")
                act.activation(eg, g, ACT.Exp)
                act.activation(eng, g, ACT.Exp, scale=-1.0)
                for m in range(2):
                    for ch in range(4):
                        end = (ch + 1) * CH
                        act.activation(eke[:, m, end - CH:end], gs[:, m, end - CH:end], ACT.Exp, scale=-1.0,
                                       bias=gs[:, m, end - 1:end])
                act.activation(egl, gs[:, :, CH - 1::CH], ACT.Exp).then_inc(gla_act.sem, 1)

            def keys():
                act.wait_ge(gla_pe.sem, G_PE["kt"])
                act.activation(keT.rearrange("p b m d -> p (b m d)"), bank[7][:, :], ACT.Copy).then_inc(gla_act.sem, 1)

            def norm():
                act.wait_ge(gla_pe.sem, G_PE["o"])
                act.activation(osq[:, 0:512], bank[6][:, :], ACT.Square)
                act.activation(osq[:, 512:1024], bank[7][:, :], ACT.Square).then_inc(gla_act.sem, 1)
                act.wait_ge(gla_pe.sem, G_PE["ostat"])
                act.activation(oroot[:, 0:512], bank[4][:, :], ACT.Sqrt, scale=1.0 / DV, bias=epsc[:, 0:1])
                act.activation(oroot[:, 512:1024], bank[5][:, :], ACT.Sqrt, scale=1.0 / DV, bias=epsc[:, 0:1]).then_inc(gla_act.sem, 1)
                act.wait_ge(gla_dve.sem, G_DVE["o"])
                act.activation(xh[:, 0:4, :].rearrange("p (a b) t -> p a b t", b=2), osq.rearrange("p (b a t) -> p a b t", a=2, b=2),
                               ACT.Copy).then_inc(xh_made.sem, 1)

            todo = {"small": small, "z": z, "gk": log_sigmoid, "G": cumulated, "decay": decays, "kt": keys, "norm": norm}
            for step in EVEN:
                if isinstance(step, int):
                    act_chunk(s, step, c0 + step, ACT.Silu if step in (E_G, E_G + 1) else ACT.Copy)
                elif step in todo:
                    todo[step]()
            act_attention(s)
            for j in range(4):
                hi(c0 + 12 + j + RING)

        def act_odd(s):
            c0 = base[s]

            def turn_wuk():
                for g in range(4):
                    act.wait_ge(mla_pe.sem, M_PE[f"wuk{g}"])
                    act.activation(wukT[:, g // 2, (g % 2) * 512:(g % 2 + 1) * 512], bank[QUAD[g]][:, :], ACT.Copy).then_inc(mla_act.sem, 1)

            def small():
                act.wait_ge(mla_pe.sem, M_PE["small"])
                act.activation(kix, bank[6][:, 0:T], ACT.Copy)
                act.activation(wix[0:8, :], bank[6][0:8, T:2 * T], ACT.Copy).then_inc(mla_act.sem, 1)
                act.wait_ge(proj_out.sem, proj_out.at(s, 1))
                act.activation(csq, pj[:, O_C, :], ACT.Square).then_inc(mla_act.sem, 1)

            def cnorm():
                act.wait_ge(mla_pe.sem, M_PE["cstat"])
                act.activation(root[:, :], bank[7][:, 0:T], ACT.Sqrt, scale=1.0 / LAT, bias=epsc[:, 0:1]).then_inc(mla_act.sem, 1)
                act.wait_ge(mla_pe.sem, M_PE["widx"])
                act.activation(wixT.rearrange("p b h -> p (b h)"), bank[6][:, 0:16], ACT.Copy, scale=8 ** -0.5).then_inc(mla_act.sem, 1)

            def index():
                for h in range(8):
                    act.wait_ge(mla_pe.sem, M_PE[f"index{h}"])
                    if h >= 2:
                        act.wait_ge(mla_dve.sem, M_DVE[f"scored{h - 2}"])
                    act.activation(rl[:, h % 2, :], bank[QUAD[h % 4]][:, 0:384], ACT.Relu, scale=SCALE).then_inc(mla_act.sem, 1)

            def keys():
                for g in range(4):
                    act.wait_ge(mla_pe.sem, M_PE[f"K{g}"])
                    act.activation(KTm[:, 2 * g:2 * g + 2, :].rearrange("p m t -> p (m t)"), bank[QUAD[g]][:, :], ACT.Copy).then_inc(mla_act.sem, 1)

            def values():
                for g in range(4):
                    act.wait_ge(mla_pe.sem, M_PE[f"V{g}"])
                    act.activation(Vm[:, g // 2, (g % 2) * 512:(g % 2 + 1) * 512], bank[QUAD[g]][:, :], ACT.Copy).then_inc(mla_act.sem, 1)

            todo = {"wuk": turn_wuk, "small": small, "cnorm": cnorm, "index": index, "K": keys, "V": values}
            for step in ODD:
                if isinstance(step, int):
                    act_chunk(s, step, c0 + step)
                elif step in todo:
                    todo[step]()
            act_attention(s)
            for j in range(4):
                hi(c0 + 7 + j + RING)

        def act_rope():
            for dst, at in ((sinT, 1), (cosT, 3)):
                act.wait_ge(rope_made.sem, at)
                act.activation(dst, red, ACT.Sin).then_inc(rope_made.sem, 1)

        def act_split_tiles(s, tiles, first=0):
            for i, k in enumerate(tiles):
                act.wait_ge(xn_made.sem, xn_made.at(s, first + i + 1))
                act.activation(xh[:, k, :], xn[:, k, :], ACT.Copy).then_inc(xh_made.sem, 1)

        def act_mix(s):
            l, c0 = int(s[3:]), base[s]
            for step in MIX:
                if isinstance(step, int):
                    act_chunk(s, step, c0 + step, ACT.Sigmoid if step in (2, 3) else ACT.Copy, pm)
            act_attention(s, lambda i: act_chunk(s, 10 + i, c0 + 10 + i, ACT.Sigmoid, pm) if i < 8 else None)
            flat = lambda v: v.rearrange("p k t -> p (k t)")
            act.wait_ge(ao_made.sem, ao_made.at(s))
            act.activation(flat(xh[:, 0:4, :]), flat(ao), ACT.Copy).then_inc(xh_made.sem, 1)
            act.wait_ge(cln_pe.sem, cln_pe.at(s, 1))
            act.activation(cmu, bank[6][:, 0:T], ACT.Copy, scale=1.0 / CW).then_inc(cln_act.sem, 1)
            act.wait_ge(cln_dve.sem, cln_dve.at(s, 1))
            act.activation(flat(ctmp), flat(cacc), ACT.Square).then_inc(cln_act.sem, 1)
            act.wait_ge(cln_pe.sem, cln_pe.at(s, 2))
            act.activation(root[:, :], bank[7][:, 0:T], ACT.Sqrt, scale=1.0 / CW, bias=epsc[:, 1:2]).then_inc(cln_act.sem, 1)
            for ct in range(CT):
                act.wait_ge(cln_dve.sem, cln_dve.at(s, 2 + ct))
                act.activation(ctmp[:, ct, :], cacc[:, ct, :], ACT.Silu, bias=vec(1, V_CLNB + 4 * l + ct)).then_inc(cln_act.sem, 1)
                act.wait_ge(cln_act.sem, cln_act.at(s, 4 + ct))
                act.activation(xh[:, 4 + ct, :], ctmp[:, ct, :], ACT.Copy).then_inc(xh_made.sem, 1)
            for n in range(4):
                hi(c0 + 18 + n + RING)
            for i in range(4):
                act.wait_ge(merged.sem, merged.at(s, i + 1))
                act.activation(flat(xh[:, 2 * i:2 * i + 2, :]), flat(xn[:, 2 * i:2 * i + 2, :]), ACT.Copy).then_inc(xh_made.sem, 1)
            act_scaled(s, c0 + 22, l, 2)

        def act_scaled(s, c0, l, part):
            for j in range(4):
                act.wait_ge(chunk_used.sem, c0 + j + 1)
                if j >= 2:
                    act.wait_ge(x_ready.sem, x_ready.at(s, j - 1))
                for m in range(2):
                    last = act.activation(yt[:, j % 2, m * T:(m + 1) * T], bank[2 + j % 2][:, m * T:(m + 1) * T], ACT.Identity,
                                          scale=ada(l, part, 2 * j + m, 1))
                last.then_inc(y_out.sem, 1)
                hi(c0 + j + RING)

        def act_ln(s):
            l, b = int(s[2]), V_MIXB if s[3] == "a" else V_FFNB
            act.wait_ge(stat_made.sem, stat_made.at(s, 1))
            act.activation(rstd[:, :], bank[6][:, 0:T], ACT.Copy, scale=1.0 / D).then_inc(root_made.sem, 1)
            for q in range(4):
                act.wait_ge(cen_made.sem, cen_made.at(s, q + 1))
                act.activation(xn[:, 2 * q:2 * q + 2, :], x[:, 2 * q:2 * q + 2, :], ACT.Square).then_inc(sq_made.sem, 1)
            act.wait_ge(stat_made.sem, stat_made.at(s, 2))
            act.activation(root[:, :], bank[7][:, 0:T], ACT.Sqrt, scale=1.0 / D, bias=epsc[:, 1:2]).then_inc(root_made.sem, 1)
            for k in range(KT):
                act.wait_ge(ln_made.sem, ln_made.at(s, k + 1))
                act.activation(x[:, k, :], x[:, k, :], ACT.Identity, bias=vec(0, b + KT * l + k)).then_inc(x_ready.sem, 1)

        def act_store():
            for n in range(2 * TB):
                act.wait_ge(out_made.sem, n + 1)
                act.activation(xin[:, n // 2, (n % 2) * 512:(n % 2 + 1) * 512], bank[n][:, :], ACT.Copy).then_inc(out_copied.sem, 1)

        act_setup()
        act.wait_ge(vec_made.sem, 1)
        act.activation(csil[:, :], vecT[:, 1, V_C:V_C + KT], ACT.Silu).then_inc(csil_made.sem, 1)
        for c in range(RING):
            hi(c)
        for kind, s in STAGES:
            if kind == "rms":
                act_rms(s)
            if kind in ("ffn", "sq"):
                act_ffn(s)
            if kind == "even":
                act_even(s)
            if kind == "odd":
                act_odd(s)
            if kind == "ada":
                act_rope()
            if kind == "mod":
                act_split_tiles(s, range(KT))
            if kind == "mix":
                act_mix(s)
            if kind == "ln":
                act_ln(s)
        act_store()

    @block.vector
    def _(dve):
        def lo(c, turn=None, per_turn=0):
            if turn is None and c >= n_chunks:
                return
            dve.wait_ge(hi_made.sem, shifted(c + 1, turn, per_turn))
            dve.tensor_tensor(wl[:, c % RING, :], raw[:, c % RING, :], wh[:, c % RING, :].bitcast(F32), ALU.subtract).then_inc(lo_made.sem, 1)

        def dve_setup():
            dve.wait_ge(setup_pe.sem, 1)
            for v in range(4):
                last = dve.tensor_copy(vecT[:, v, 0:V_ROWS[v]], bank[7][:, v * P:v * P + V_ROWS[v]])
            last.then_inc(vec_made.sem, 1)
            dve.wait_ge(vec_made.sem, 1)

        def xrest(s, k):
            dve.wait_ge(xh_made.sem, xh_made.at(s, k + 1))
            dve.tensor_tensor(xl[:, k, :], xn[:, k, :], xh[:, k, :].bitcast(F32), ALU.subtract).then_inc(xl_made.sem, 1)

        def dve_rms(s):
            g = V_FINAL if s == "final" else V_NORM + int(s[3:]) * KT
            dve.wait_ge(root_made.sem, root_made.at(s))
            dve.reciprocal(rstd[:, :], root[:, :]).then_inc(rstd_made.sem, 1)
            dve.wait_ge(rstd_made.sem, rstd_made.at(s))
            for k in range(KT):
                dst = x if s == "final" else xn
                dve.scalar_tensor_tensor(out=dst[:, k, :], in0=x[:, k, :], scalar=vec(0, g + k), in1=rstd[:, :],
                                         op0=ALU.mult, op1=ALU.mult).then_inc((x_ready if s == "final" else xn_made).sem, 1)
                if k >= 1 and s != "final":
                    xrest(s, k - 1)
            if s != "final":
                xrest(s, KT - 1)

        def dve_ffn(s):
            n_in, steps, body, bufs = ffn_shape(s)
            c0 = base[s]

            def step(i, st, turn):
                c = c0 + (0 if st == 0 else n_in + (n_in + 1) * (st - 1))
                per = (n_in + 1) * body
                if n_in == 2:
                    lo(c + RING, turn, per)
                for f in range(2):
                    dve.wait_ge(act_made.sem, shifted(act_made.at(s, 2 * st + f + 1), turn, 2 * body))
                    other = bank[4 + f][:, T:2 * T] if n_in == 2 else fs[:, f, :]
                    dve.tensor_tensor(fh[:, st % bufs, f, :], fs[:, f, :], other, ALU.mult).then_inc(h_made.sem, 1)
                lo(c + n_in - 1 + RING, turn, per)
                for f in range(2):
                    dve.wait_ge(hh_made.sem, shifted(hh_made.at(s, 2 * st + f + 1), turn, 2 * body))
                    mv = slice(f * T, (f + 1) * T)
                    dve.tensor_tensor(hl[:, st % bufs, mv], fh[:, st % bufs, f, :], hh[:, st % bufs, mv].bitcast(F32),
                                      ALU.subtract).then_inc(hl_made.sem, 1)
                if st > 0:
                    lo(c + n_in + RING, turn, per)

            steps_of(dve, steps, 2, body, step)
            dve.wait_ge(chunk_used.sem, c0 + (n_in + 1) * steps)
            for q in range(4):
                xs = x[:, 2 * q:2 * q + 2, :].rearrange("p k t -> p (k t)")
                if KIND[s] == "ffn":
                    dve.scalar_tensor_tensor(out=xs, in0=bank[q][:, :], scalar=0.5, in1=xs, op0=ALU.mult,
                                             op1=ALU.add).then_inc(x_ready.sem, 1)
                else:
                    dve.wait_ge(y_out.sem, y_out.at(s, q + 1))
                    dve.scalar_tensor_tensor(out=xs, in0=xs, scalar=ALPHA, in1=yt[:, q % 2, :], op0=ALU.mult,
                                             op1=ALU.add).then_inc(x_ready.sem, 1)
            lo(c0 + (n_in + 1) * steps - 1 + RING)

        n_step = [0]

        def link(ins):
            n_step[0] += 1
            ins.then_inc(dve_step.sem, 1)
            dve.wait_ge(dve_step.sem, n_step[0])

        def dve_attention(s, meanwhile=None):
            H = heads_of[s]
            mask = att_of(s)[3]

            def masked(h):
                dve.wait_ge(score_made.sem, score_made.at(s, h + 1))
                if s == "odd":
                    dve.wait_ge(bm_made.sem, h + 1)
                for b, at in enumerate((slice(0, P), slice(P, 384))):
                    last = dve.tensor_tensor_reduce(ns[:, h % 2, at], bank[4 + h % 2][:, at], mask(h)[:, at], -SCALE, 3e38,
                                                    ALU.add, ALU.min, nm[:, h % 2, b:b + 1])
                last.then_inc(ns_made.sem, 1)

            def normalise(h):
                dve.wait_ge(p_made.sem, p_made.at(s, h + 1))
                link(dve.reciprocal(ri[:, h % 2, :], rs[:, h % 2, :]))
                for b, at in enumerate((slice(0, P), slice(P, 384))):
                    last = dve.tensor_scalar(pr[:, h % 2, at], pr[:, h % 2, at], ri[:, h % 2, b:b + 1], None, ALU.mult)
                last.then_inc(pn_made.sem, 1)

            def rest(pair):
                if KIND[s] == "mix":
                    return
                i = XL_FIRST[s] + pair
                dve.wait_ge(xh_made.sem, xh_made.at(s, i + 1))
                t = X_TILE[s] + pair
                dve.tensor_tensor(xl[:, t, :], bank[pair % 2][:, 0:T], xh[:, t, :].bitcast(F32), ALU.subtract).then_inc(xl_made.sem, 1)

            for i in range(H + 3):
                if i < H:
                    masked(i)
                if 1 <= i <= H:
                    normalise(i - 1)
                if meanwhile:
                    meanwhile(i)
                if i >= 3 and i % 2 == 1:
                    rest((i - 3) // 2)

        def dve_out(s, c0):
            for j in range(4):
                dve.wait_ge(chunk_used.sem, c0 + j + 1)
                xs = x[:, 2 * j:2 * j + 2, :].rearrange("p k t -> p (k t)")
                dve.tensor_tensor(xs, bank[2 + j % 2][:, :], xs, ALU.add).then_inc(x_ready.sem, 1)
                lo(c0 + j + RING)

        def dve_even(s):
            c0 = base[s]

            def small():
                dve.wait_ge(small_made.sem, 1)
                dve.tensor_scalar(fz[32:40, :], bank[STAT][32:40, 0:T], bfox[32:40, 0:1], None, ALU.add).then_inc(gla_dve.sem, 1)

            def z():
                dve.wait_ge(gla_dve.sem, G_DVE["fz"])
                dve.wait_ge(gla_act.sem, G_ACT["z"])
                dve.scalar_tensor_tensor(out=za, in0=zs, scalar=-1.0, in1=zs, op0=ALU.mult, op1=ALU.max).then_inc(gla_dve.sem, 1)
                dve.scalar_tensor_tensor(out=fa[32:40, :], in0=fz[32:40, :], scalar=-1.0, in1=fz[32:40, :], op0=ALU.mult,
                                         op1=ALU.max).then_inc(gla_dve.sem, 1)

            def log_sigmoid():
                dve.wait_ge(gla_act.sem, G_ACT["lnf"])
                dve.scalar_tensor_tensor(out=gk, in0=zs, scalar=0.0, in1=za, op0=ALU.min, op1=ALU.subtract).then_inc(gla_dve.sem, 1)
                link(dve.scalar_tensor_tensor(out=fz[32:40, :], in0=fz[32:40, :], scalar=0.0, in1=fa[32:40, :], op0=ALU.min,
                                              op1=ALU.subtract))
                dve.tensor_tensor_scan(fsum[32:40, :], onesT[32:40, :], fz[32:40, :], 0.0, ALU.mult, ALU.add).then_inc(gla_dve.sem, 1)

            def decayed():
                dve.wait_ge(gla_act.sem, G_ACT["decays"])
                dve.wait_ge(proj_out.sem, proj_out.at(s, 2))
                flat = lambda v: v.rearrange("p m t -> p (m t)")
                dve.scalar_tensor_tensor(out=flat(qd), in0=pj[:, E_Q, :], scalar=SCALE, in1=eg, op0=ALU.mult, op1=ALU.mult)
                dve.tensor_tensor(flat(kd), pj[:, E_K, :], eng, ALU.mult)
                dve.tensor_tensor(flat(ke), pj[:, E_K, :], flat(eke), ALU.mult).then_inc(gla_dve.sem, 1)
                dve.wait_ge(gla_dve.sem, G_DVE["decayed"])
                link(dve.memset(AT[:, :, :], 0.0))

            def scores():
                dve.wait_ge(gla_pe.sem, G_PE["A"])
                for q in range(2):
                    last = dve.copy_predicated(AT[:, q, :].rearrange("p (b i) -> p b i", b=4),
                                               trib[:, :].unsqueeze(1).broadcast_to((P, 4, P)),
                                               bank[6 + q][:, :].rearrange("p (b i) -> p b i", b=4))
                last.then_inc(gla_dve.sem, 1)

            def states():
                dve.wait_ge(gla_pe.sem, G_PE["kv"])
                kv = lambda ch, m: bank[6 + ch % 2][:, (ch // 2) * T + m * P:(ch // 2) * T + (m + 1) * P]
                for m in range(2):
                    last = dve.tensor_copy(state[:, 0, m, :], kv(0, m))
                for ch in (1, 2):
                    link(last)
                    for m in range(2):
                        last = dve.scalar_tensor_tensor(out=state[:, ch, m, :], in0=state[:, ch - 1, m, :],
                                                        scalar=egl[:, m, ch:ch + 1], in1=kv(ch, m), op0=ALU.mult, op1=ALU.add)
                last.then_inc(gla_dve.sem, 1)

            def norm():
                dve.wait_ge(gla_act.sem, G_ACT["oroot"])
                link(dve.reciprocal(orstd, oroot))
                for q in range(2):
                    at = slice(q * 512, (q + 1) * 512)
                    last = dve.scalar_tensor_tensor(out=osq[:, at], in0=bank[6 + q][:, :], scalar=vec(0, V_GLA),
                                                    in1=orstd[:, at], op0=ALU.mult, op1=ALU.mult)
                link(last)
                o4 = osq.rearrange("p (b a t) -> p a b t", a=2, b=2)
                dve.tensor_tensor(o4, o4, pj[:, E_G:E_G + 2, :].rearrange("p a (b t) -> p a b t", b=2), ALU.mult).then_inc(gla_dve.sem, 1)
                dve.wait_ge(xh_made.sem, xh_made.at(s, 1))
                dve.tensor_tensor(xl[:, 0:4, :].rearrange("p (a b) t -> p a b t", b=2), o4,
                                  xh[:, 0:4, :].rearrange("p (a b) t -> p a b t", b=2).bitcast(F32), ALU.subtract).then_inc(xl_made.sem, 1)

            todo = {"small": small, "z": z, "gk": log_sigmoid, "decay": decayed, "A": scores, "kv": states, "norm": norm}
            for step in EVEN:
                if isinstance(step, int):
                    lo(c0 + step + RING)
                elif step in todo:
                    todo[step]()
            dve_attention(s)
            dve_out(s, c0 + 12)

        def dve_odd(s):
            c0 = base[s]
            blocks = (slice(0, P), slice(P, 384))

            def cnorm():
                dve.wait_ge(mla_act.sem, M_ACT["croot"])
                link(dve.reciprocal(rstd[:, :], root[:, :]))
                for l in range(2):
                    last = dve.scalar_tensor_tensor(out=cT[:, l, :], in0=pj[:, O_C, l * T:(l + 1) * T], scalar=vec(0, V_MLA + l),
                                                    in1=rstd[:, :], op0=ALU.mult, op1=ALU.mult)
                last.then_inc(mla_dve.sem, 1)

            def index():
                for h in range(8):
                    dve.wait_ge(mla_act.sem, M_ACT[f"relu{h}"])
                    if h > 0:
                        dve.wait_ge(mla_dve.sem, M_DVE[f"scored{h - 1}"])
                    for b, at in enumerate(blocks):
                        w = wixT[:, b, h:h + 1]
                        if h == 0:
                            last = dve.tensor_scalar(sc[:, at], rl[:, 0, at], w, None, ALU.mult)
                        else:
                            last = dve.scalar_tensor_tensor(out=sc[:, at], in0=rl[:, h % 2, at], scalar=w, in1=sc[:, at],
                                                            op0=ALU.mult, op1=ALU.add)
                    last.then_inc(mla_dve.sem, 1)
                dve.wait_ge(mla_dve.sem, M_DVE["scored7"])
                link(dve.tensor_tensor(sc, sc, cmask[:, :], ALU.add))

            def search():
                for _ in range(SEARCH_ROUNDS):
                    for b, at in enumerate(blocks):
                        last = dve.max(m8[:, b, :], sc[:, at])
                    link(last)
                    for b, at in enumerate(blocks):
                        last = dve.match_replace(sc[:, at], m8[:, b, :], sc[:, at], PICKED)
                    link(last)

            def mask():
                link(dve.tensor_scalar(dm, sc, 0.5 * (PICKED + NEG), NEG, ALU.is_gt, ALU.mult))
                dve.tensor_tensor(dm, dm, cmask[:, :], ALU.add).then_inc(mla_dve.sem, 1)

            todo = {"cnorm": cnorm, "index": index, "top": search, "mask": mask}
            for step in ODD:
                if isinstance(step, int):
                    lo(c0 + step + RING)
                elif step in todo:
                    todo[step]()
            dve_attention(s)
            dve_out(s, c0 + 7)

        def dve_ada(s):
            (l, first), n = ADA_OF[s], 2 * ADA_PER_FFN
            at = slice(2 * first, 2 * first + n)
            dve.wait_ge(ada_turned.sem, ada_made.at(s))
            link(dve.tensor_tensor(adaT[:, l, 0, at], bank[7][:, 0:n], vecT[:, 1, V_ADA + 48 * l + 2 * first:V_ADA + 48 * l + 2 * first + n], ALU.add))
            dve.tensor_scalar(adaT[:, l, 1, at], adaT[:, l, 0, at], 1.0, None, ALU.add).then_inc(ada_made.sem, 1)

        def dve_mod(s):
            l, part = int(s[3]), 0 if s[4] == "a" else 3
            dve.wait_ge(ada_made.sem, 4)
            for k in range(KT):
                dve.wait_ge(x_ready.sem, xr(s, k))
                dve.tensor_scalar(xn[:, k, :], x[:, k, :], ada(l, part + 1, k, 1), ada(l, part, k), ALU.mult,
                                  ALU.add).then_inc(xn_made.sem, 1)
                if k >= 1:
                    xrest(s, k - 1)
            xrest(s, KT - 1)

        def dve_mix(s):
            l, c0 = int(s[3:]), base[s]
            flat = lambda v: v.rearrange("p k t -> p (k t)")
            taps = [(j, ct) for j in range(CONV_K) for ct in range(CT)]

            def convolve(count):
                for _ in range(min(count, len(taps))):
                    j, ct = taps.pop(0)
                    n = j * CT + ct
                    w = vec(2 + l, j * CT + ct)
                    src = hpad[:, ct, j:j + T]
                    if j == 0:
                        if ct == 0:
                            dve.wait_ge(glu_made.sem, glu_made.at(s))
                        dve.tensor_scalar(cacc[:, ct, :], src, w, vec(1, V_DWB + 4 * l + ct), ALU.mult, ALU.add).then_inc(conv_made.sem, 1)
                    else:
                        dve.wait_ge(conv_made.sem, conv_made.at(s, n - CT + 1))
                        dve.scalar_tensor_tensor(out=cacc[:, ct, :], in0=src, scalar=w, in1=cacc[:, ct, :], op0=ALU.mult,
                                                 op1=ALU.add).then_inc(conv_made.sem, 1)

            def gated():
                dve.wait_ge(proj_out.sem, proj_out.at(s, 4))
                tiles = lambda n: pm[:, n:n + 2, :].rearrange("p n (j t) -> p (n j) t", j=2)
                dve.tensor_tensor(hpad[:, :, CONV_K - 1:], tiles(0), tiles(2), ALU.mult).then_inc(glu_made.sem, 1)

            def rope(first):
                for i in range(2):
                    n = first + i
                    dve.wait_ge(rope_pe.sem, rope_pe.at(s, (first - X_Q) + i + 1))
                    two = lambda v: v.unsqueeze(1).broadcast_to((P, 2, T))
                    split = lambda v: v.rearrange("p (m t) -> p m t", m=2)
                    t = ctmp[:, 2 * i:2 * i + 2, :]
                    dve.tensor_tensor(t, split(bank[6 + i][:, :]), two(sinT), ALU.mult)
                    link(dve.tensor_tensor(split(pm[:, n, :]), split(pm[:, n, :]), two(cosT), ALU.mult))
                    dve.tensor_tensor(split(pm[:, n, :]), split(pm[:, n, :]), t, ALU.add).then_inc(rope_dve.sem, 1)

            todo = {"glu": gated, "ropeq": lambda: rope(X_Q), "ropek": lambda: rope(X_K)}
            for step in MIX:
                if isinstance(step, int):
                    lo(c0 + step + RING)
                    if step >= X_Q:
                        convolve(CONV_PER_STEP)
                elif step in todo:
                    todo[step]()

            def meanwhile(i):
                if i < 8:
                    lo(c0 + 10 + i + RING)
                    convolve(CONV_PER_STEP)

            dve_attention(s, meanwhile)
            convolve(len(taps))
            dve.wait_ge(xh_made.sem, xh_made.at(s, 1))
            dve.tensor_tensor(flat(xl[:, 0:4, :]), flat(ao), flat(xh[:, 0:4, :]).bitcast(F32), ALU.subtract).then_inc(xl_made.sem, 1)
            dve.wait_ge(cln_act.sem, cln_act.at(s, 1))
            dve.tensor_tensor(cacc, cacc, cmu.unsqueeze(1).broadcast_to((P, CT, T)), ALU.subtract).then_inc(cln_dve.sem, 1)
            dve.wait_ge(cln_act.sem, cln_act.at(s, 3))
            link(dve.reciprocal(rstd[:, :], root[:, :]))
            for ct in range(CT):
                dve.scalar_tensor_tensor(out=cacc[:, ct, :], in0=cacc[:, ct, :], scalar=vec(1, V_CLNG + 4 * l + ct), in1=rstd[:, :],
                                         op0=ALU.mult, op1=ALU.mult).then_inc(cln_dve.sem, 1)
            for ct in range(CT):
                dve.wait_ge(xh_made.sem, xh_made.at(s, 2 + ct))
                dve.tensor_tensor(xl[:, 4 + ct, :], ctmp[:, ct, :], xh[:, 4 + ct, :].bitcast(F32), ALU.subtract).then_inc(xl_made.sem, 1)
            for n in range(4):
                lo(c0 + 18 + n + RING)
                if n % 2 == 1:
                    for q in range(2):
                        i = 2 * (n // 2) + q
                        a, b = bank[4 * (n // 2) + q], bank[4 * (n // 2) + 2 + q]
                        m = flat(xn[:, 2 * i:2 * i + 2, :])
                        t = flat(ctmp[:, 2 * q:2 * q + 2, :])
                        dve.wait_ge(chunk_used.sem, c0 + 18 + n + 1)
                        dve.tensor_tensor(t, b[:, :], pm[:, X_GC + i, :], ALU.mult)
                        link(dve.tensor_tensor(m, a[:, :], pm[:, X_GA + i, :], ALU.mult))
                        dve.tensor_tensor(m, m, t, ALU.add).then_inc(merged.sem, 1)
            for i in range(4):
                dve.wait_ge(xh_made.sem, xh_made.at(s, 1 + CT + i + 1))
                at = slice(2 * i, 2 * i + 2)
                dve.tensor_tensor(flat(xl[:, at, :]), flat(xn[:, at, :]), flat(xh[:, at, :]).bitcast(F32), ALU.subtract).then_inc(xl_made.sem, 1)
            for j in range(4):
                dve.wait_ge(y_out.sem, y_out.at(s, j + 1))
                xs = flat(x[:, 2 * j:2 * j + 2, :])
                dve.scalar_tensor_tensor(out=xs, in0=xs, scalar=ALPHA, in1=yt[:, j % 2, :], op0=ALU.mult, op1=ALU.add).then_inc(x_ready.sem, 1)
                lo(c0 + 22 + j + RING)

        def dve_ln(s):
            l, g = int(s[2]), V_MIXG if s[3] == "a" else V_FFNG
            dve.wait_ge(root_made.sem, root_made.at(s, 1))
            for q in range(4):
                xs = x[:, 2 * q:2 * q + 2, :]
                last = dve.tensor_tensor(xs, xs, rstd[:, :].unsqueeze(1).broadcast_to((P, 2, T)), ALU.subtract).then_inc(cen_made.sem, 1)
            dve.wait_ge(root_made.sem, root_made.at(s, 2))
            dve.reciprocal(rstd[:, :], root[:, :]).then_inc(rstd_made.sem, 1)
            dve.wait_ge(rstd_made.sem, rstd_made.at(s))
            for k in range(KT):
                dve.scalar_tensor_tensor(out=x[:, k, :], in0=x[:, k, :], scalar=vec(0, g + KT * l + k), in1=rstd[:, :],
                                         op0=ALU.mult, op1=ALU.mult).then_inc(ln_made.sem, 1)

        dve_setup()
        for c in range(RING):
            lo(c)
        for kind, s in STAGES:
            if kind == "rms":
                dve_rms(s)
            if kind in ("ffn", "sq"):
                dve_ffn(s)
            if kind == "even":
                dve_even(s)
            if kind == "odd":
                dve_odd(s)
            if s in ADA_OF:
                dve_ada(s)
            if kind == "ada":
                dve.wait_ge(rope_made.sem, 4)
                dve.memset(hpad[:, :, 0:CONV_K - 1], 0.0)
            if kind == "mod":
                dve_mod(s)
            if kind == "mix":
                dve_mix(s)
            if kind == "ln":
                dve_ln(s)

    ctx.close()


OUTS = [((1, T, D), "float32")]


def kernel(**inputs):
    import numpy as _np
    import concourse.bacc as _bacc
    from concourse import mybir as _mybir
    from concourse.bass_utils import run_bass_kernel_spmd as _run

    nc = _bacc.Bacc("TRN2", target_bir_lowering=False, num_devices=1)
    arrays, aps = {}, {}
    for name, value in {**inputs, **constants()}.items():
        a = _np.ascontiguousarray(value)
        arrays[f"in_{name}"] = a
        aps[name] = nc.dram_tensor(f"in_{name}", a.shape, _mybir.dt.from_np(a.dtype), kind="ExternalInput").ap()
    out = nc.dram_tensor("out_0", OUTS[0][0], F32, kind="ExternalOutput").ap()
    build(nc, aps, out)
    r = _run(nc, [arrays], core_ids=[0])
    return r.results[0]["out_0"]
```

```python
import math
from contextlib import ExitStack

import numpy as np

import concourse.bass as bass
from concourse import mybir

ALU = mybir.AluOpType
ACT = mybir.ActivationFunctionType
F32 = mybir.dt.float32
F32R = mybir.dt.float32r
I32 = mybir.dt.int32

P = 128
T = 256
TB = T // P
D = 1024
KT = D // P
FF = 2816
FF_STEPS = FF // 256
FF2 = 4096
FF2_STEPS = FF2 // 256
EPS = 1e-6
LN_EPS = 1e-5
NEG = -1e30
PICKED = -3e30
TOPK = 64
HD = 64
SCALE = HD ** -0.5
DV = 128
CH = 64
LAT = 256
CONV_K = 31
CW = 512
CT = CW // P
ROT = HD // 4
ALPHA = 4 ** 0.25
RING = 3
CHUNK = 2048
BIAS_COLS = 384
ARENA = 19088
ATT = 7 * 384
ADA_PER_FFN = 12

V_NORM, V_FINAL, V_GLA, V_MLA, V_MIXG, V_MIXB, V_FFNG, V_FFNB = 0, 48, 56, 57, 59, 75, 91, 107
V_DWB, V_CLNG, V_CLNB, V_C, V_ADA = 0, 8, 16, 24, 32
V_ROWS = (123, 128, 4 * CONV_K, 4 * CONV_K)

ROUND = 1.5 * 2 ** 23
TWO_PI = [6.28125, float(np.float32(np.floor((2 * math.pi - 6.28125) * 2 ** 20) / 2 ** 20))]
TWO_PI.append(float(np.float32(2 * math.pi - sum(TWO_PI))))
PI_BELOW = 3.1415925


def constants():
    exact = 16
    back = np.maximum(np.arange(BIAS_COLS) - (P - 1), 0)
    large = exact + (np.log(np.maximum(back, 1).astype(np.float32) / exact) / math.log(128 / exact) * (32 - exact)).astype(np.int32)
    bucket = np.where(back < exact, back, np.minimum(large, 31))
    buckets = (np.arange(32)[:, None] == bucket[None, :]).astype(np.float32)
    half = ROT // 2
    freq = np.zeros((P, 1), np.float32)
    turn = np.zeros((P, P), np.float32)
    for first in range(0, P, HD):
        for i in range(half):
            freq[first + i] = freq[first + half + i] = np.float32(500000.0 ** (-2 * i / ROT))
            turn[first + half + i, first + i] = -1.0
            turn[first + i, first + half + i] = 1.0
    return {"buckets": buckets, "rope_freq": freq, "rope_turn": turn}


class Signal:

    def __init__(self, sem):
        self.sem, self.first, self.times, self.total = sem, {}, {}, 0

    def plan(self, stage, times):
        self.first[stage], self.times[stage] = self.total, times
        self.total += times

    def at(self, stage, n=None):
        return self.first[stage] + (self.times[stage] if n is None else n)


def shifted(value, turn, per_turn):
    return value if turn is None else turn * per_turn + value


def build(nc, A, out, upto=None):
    ctx = ExitStack()

    def sb(name, shape, dt=F32):
        return ctx.enter_context(nc.sbuf_tensor(name, shape, dt))

    def signal(name):
        return Signal(ctx.enter_context(nc.semaphore(name)))

    STAGES = [("rms", "rms0"), ("ffn", "ffn0"), ("rms", "rms1"), ("even", "even"), ("rms", "rms2"), ("ffn", "ffn1"),
              ("rms", "rms3"), ("ffn", "ffn2"), ("rms", "rms4"), ("odd", "odd"), ("rms", "rms5"), ("ffn", "ffn3"),
              ("rms", "final"), ("rope", "rope")]
    for l in range(2):
        STAGES += [("mod", f"mod{l}a"), ("mix", f"mix{l}"), ("ln", f"ln{l}a"),
                   ("mod", f"mod{l}b"), ("sq", f"sq{l}"), ("ln", f"ln{l}b")]
    if upto is not None:
        STAGES = STAGES[:[s for _, s in STAGES].index(upto) + 1]
    KIND = {s: k for k, s in STAGES}
    CHUNKS_OF = {"ffn": 3 * FF_STEPS, "sq": 2 * FF2_STEPS, "even": 16, "odd": 11, "mix": 26}
    base, n_chunks = {}, 0
    for kind, s in STAGES:
        base[s] = n_chunks
        n_chunks += CHUNKS_OF.get(kind, 0)

    raw = sb("raw", [P, RING, CHUNK])
    wh = sb("wh", [P, RING, CHUNK], F32R)
    wl = sb("wl", [P, RING, CHUNK], F32R)
    x = sb("x", [P, KT, T])
    xn = sb("xn", [P, KT, T])
    xh = sb("xh", [P, KT, T], F32R)
    xl = sb("xl", [P, KT, T], F32R)
    hh = sb("hh", [P, 3, 512], F32R)
    hl = sb("hl", [P, 3, 512], F32R)
    root = sb("root", [P, T])
    rstd = sb("rstd", [P, T])
    ident = sb("ident", [P, P])
    ones = sb("ones", [P, P])
    vecT = sb("vecT", [P, 4, P])
    adaT = sb("adaT", [P, 2, 2, 48])
    fold = sb("fold", [P, 4, 2, KT])
    epsc = sb("epsc", [P, 2])
    bias_rows = nc.dram_tensor("bias_rows", (16, BIAS_COLS), F32)
    nm = sb("nm", [P, 2, 2])
    rs = sb("rs", [P, 2, 2])
    ri = sb("ri", [P, 2, 2])
    cmask = sb("cmask", [P, 384])
    tri = sb("tri", [P, P])
    trib = sb("trib", [P, P], I32)
    wsm = sb("wsm", [P, KT, 136])
    bfox = sb("bfox", [P, 1])
    csil = sb("csil", [P, KT])
    arena = sb("arena", [P, ARENA])

    class Carver:

        def __init__(self, at=0):
            self.at = at

        def take(self, size, pattern=None, **sizes):
            v = arena[:, self.at:self.at + size]
            self.at += size
            assert self.at <= ARENA, self.at
            return v.rearrange(pattern, **sizes) if pattern else v

    c = Carver()
    fs = c.take(512, "p (f t) -> p f t", f=2)
    fh = c.take(3 * 512, "p (b f t) -> p b f t", b=3, f=2)
    ada_raw = c.take(2 * CHUNK, "p (b n) -> p b n", b=2)
    at_sum = c.at
    ada_sum = c.take(ADA_PER_FFN * T, "p (n t) -> p n t", n=ADA_PER_FFN)
    c = Carver()
    pj = c.take(12 * 512, "p (n t) -> p n t", n=12)
    glow = c.take(T)
    at_z = c.at
    zs, za, gk = c.take(2 * T), c.take(2 * T), c.take(2 * T)
    fz, fa, fsum = c.take(T), c.take(T), c.take(T)
    gs = c.take(2 * T, "p (m t) -> p m t", m=2)
    at_e = c.at
    eg, eng = c.take(2 * T), c.take(2 * T)
    eke = c.take(2 * T, "p (m t) -> p m t", m=2)
    qd = c.take(2 * T, "p (m t) -> p m t", m=2)
    at_k = c.at
    kd, ke = (c.take(2 * T, "p (m t) -> p m t", m=2) for _ in range(2))
    keT = c.take(2 * T, "p (b m d) -> p b m d", b=2, m=2)
    state = c.take(3 * 2 * DV, "p (c m v) -> p c m v", c=3, m=2)
    egl = c.take(8, "p (m c) -> p m c", m=2)
    sel = c.take(8 * P, "p (h q) -> p h q", h=8)
    wgate, bgate, onesT = c.take(T), c.take(T), c.take(T)
    assert c.at <= ARENA - ATT
    AT = pj[:, 0:2, :]
    osq, oroot, orstd = Carver(at_z).take(4 * T), Carver(at_e).take(4 * T), Carver(at_k).take(4 * T)
    c = Carver(ARENA - ATT)
    ns = c.take(2 * 384, "p (b k) -> p b k", b=2)
    pr = c.take(3 * 384, "p (b k) -> p b k", b=3)
    pt = c.take(2 * 384, "p (b k) -> p b k", b=2)
    c = Carver(7 * 512)
    kix, wix = c.take(T), c.take(T)
    wixT = c.take(TB * 8, "p (b h) -> p b h", b=TB)
    cT = c.take(2 * T, "p (l t) -> p l t", l=2)
    KTm = c.take(8 * T, "p (m t) -> p m t", m=8)
    wukT = c.take(2 * D, "p (l n) -> p l n", l=2)
    wuv = c.take(2 * D, "p (l n) -> p l n", l=2)
    at_b = c.at
    bias8 = c.take(16 * T, "p (h k) -> p h k", h=16)
    wuk = Carver(at_b).take(8 * T, "p (m l) -> p m l", m=8)
    at_m = c.at
    bm = c.take(3 * 384, "p (b k) -> p b k", b=3)
    csq = Carver(at_m).take(2 * T)
    dm = c.take(384)
    assert c.at <= ARENA - ATT
    Vm = xn[:, :, :].rearrange("p (b a) t -> p b (a t)", b=TB)
    c = Carver(ARENA - ATT)
    rl = c.take(2 * 384, "p (b k) -> p b k", b=2)
    sc = c.take(384)
    m8 = c.take(TB * 8, "p (b n) -> p b n", b=TB)
    c = Carver()
    pm = c.take(18 * 512, "p (n t) -> p n t", n=18)
    hpad = c.take(CT * (T + CONV_K - 1), "p (c t) -> p c t", c=CT)
    cacc = c.take(CT * T, "p (c t) -> p c t", c=CT)
    ctmp = c.take(CT * T, "p (c t) -> p c t", c=CT)
    ao = c.take(4 * T, "p (k t) -> p k t", k=4)
    yt = c.take(2 * 512, "p (b t) -> p b t", b=2)
    cmu = c.take(T)
    cosT, sinT, turn = c.take(T), c.take(T), c.take(P)
    freq = c.take(1)
    ptmp = c.take(2 * 2 * T, "p (b c t) -> p b c t", b=2, c=2)
    assert c.at <= ARENA - ATT
    c = Carver(9 * 1024)
    ang, turns, red = c.take(T), c.take(T), c.take(T)
    posi = c.take(T).bitcast(I32)
    part_turns = c.take(T)
    c = Carver(9 * 1024)
    bt = c.take(16 + 2 * BIAS_COLS)
    xin = c.take(TB * D, "p (b d) -> p b d", b=TB)
    rows = c.take(4 * P, "p (a d) -> p a d", a=4)

    bank = [ctx.enter_context(nc.psum_tensor(f"bank{i}", [P, 512], F32)) for i in range(8)]
    STAT = 6
    QUAD = (0, 1, 4, 5)

    loaded = [signal(f"loaded{i}") for i in range(RING)]
    hi_made = signal("hi_made")
    lo_made = signal("lo_made")
    chunk_used = signal("chunk_used")
    x_loaded = signal("x_loaded")
    in_loaded = signal("in_loaded")
    table_loaded = signal("table_loaded")
    const_made = signal("const_made")
    setup_pe = signal("setup_pe")
    vec_made = signal("vec_made")
    x_ready = signal("x_ready")
    sq_made = signal("sq_made")
    stat_made = signal("stat_made")
    root_made = signal("root_made")
    rstd_made = signal("rstd_made")
    xn_made = signal("xn_made")
    xh_made = signal("xh_made")
    xl_made = signal("xl_made")
    a_made = signal("a_made")
    acc_made = signal("acc_made")
    act_made = signal("act_made")
    h_made = signal("h_made")
    hh_made = signal("hh_made")
    hl_made = signal("hl_made")
    proj_out = signal("proj_out")
    wsm_loaded = signal("wsm_loaded")
    small_made = signal("small_made")
    gla_pe = signal("gla_pe")
    gla_act = signal("gla_act")
    gla_dve = signal("gla_dve")
    bias_stored = signal("bias_stored")
    mla_loaded = signal("mla_loaded")
    bias_loaded = signal("bias_loaded")
    mla_pe = signal("mla_pe")
    mla_act = signal("mla_act")
    mla_dve = signal("mla_dve")
    bm_made = signal("bm_made")
    dve_step = signal("dve_step")
    act_step = signal("act_step")
    score_made = signal("score_made")
    ns_made = signal("ns_made")
    p_made = signal("p_made")
    pn_made = signal("pn_made")
    pt_made = signal("pt_made")
    pt_out = signal("pt_out")
    pv_made = signal("pv_made")
    rope_loaded = signal("rope_loaded")
    rope_made = signal("rope_made")
    csil_made = signal("csil_made")
    ada_loaded = [signal(f"ada_loaded{i}") for i in range(2)]
    pool_step = signal("pool_step")
    ada_summed = signal("ada_summed")
    ada_turned = signal("ada_turned")
    ada_made = signal("ada_made")
    fold_made = signal("fold_made")
    wuv_loaded = signal("wuv_loaded")
    glu_made = signal("glu_made")
    conv_made = signal("conv_made")
    rope_pe = signal("rope_pe")
    rope_dve = signal("rope_dve")
    ao_made = signal("ao_made")
    cln_pe = signal("cln_pe")
    cln_act = signal("cln_act")
    cln_dve = signal("cln_dve")
    merged = signal("merged")
    y_out = signal("y_out")
    cen_made = signal("cen_made")
    ln_made = signal("ln_made")
    out_made = signal("out_made")
    out_copied = signal("out_copied")
    out_copied_dve = signal("out_copied_dve")
    stored = signal("stored")

    x_ready.plan("in", 4)
    x_of, xstage, heads_of = {}, "in", {}
    for kind, s in STAGES:
        x_of[s] = xstage
        if kind == "rms":
            for g, n in ((sq_made, KT), (stat_made, 1), (root_made, 1), (rstd_made, 1)):
                g.plan(s, n)
            if s != "final":
                xn_made.plan(s, KT)
                xh_made.plan(s, KT)
                xl_made.plan(s, KT)
            else:
                x_ready.plan(s, KT)
                xstage = s
        if kind == "even":
            proj_out.plan(s, 12)
            xh_made.plan(s, 1 + 4)
            xl_made.plan(s, 1 + 4)
            x_ready.plan(s, 4)
            xstage = s
            heads_of[s] = 8
        if kind == "odd":
            proj_out.plan(s, 7)
            xh_made.plan(s, 8)
            xl_made.plan(s, 8)
            x_ready.plan(s, 4)
            xstage = s
            heads_of[s] = 16
        if kind == "mod":
            for g in (xn_made, xh_made, xl_made):
                g.plan(s, KT)
        if kind == "mix":
            heads_of[s] = 8
            proj_out.plan(s, 18)
            glu_made.plan(s, 1)
            conv_made.plan(s, CONV_K * 2)
            for g, n in ((rope_pe, 4), (rope_dve, 4), (ao_made, 4), (cln_pe, 2), (cln_act, 3 + CT), (cln_dve, 1 + CT),
                         (xh_made, 1 + 2 + 4), (xl_made, 1 + 2 + 4), (merged, 4), (y_out, 4), (x_ready, 4)):
                g.plan(s, n)
            xstage = s
        if kind == "ln":
            for g, n in ((stat_made, 2), (root_made, 2), (cen_made, 4), (sq_made, 4), (rstd_made, 1), (ln_made, KT), (x_ready, KT)):
                g.plan(s, n)
            xstage = s
        if kind == "sq":
            y_out.plan(s, 4)
        if s in heads_of:
            for g in (score_made, ns_made, p_made, pn_made, pt_made, pt_out, pv_made):
                g.plan(s, heads_of[s])
        if kind in ("ffn", "sq"):
            steps = FF_STEPS if kind == "ffn" else FF2_STEPS
            acc_made.plan(s, 3)
            if kind == "ffn":
                a_made.plan(s, steps)
            for g in (act_made, h_made, hh_made, hl_made):
                g.plan(s, (2 if kind == "ffn" else 1) * steps)
            x_ready.plan(s, 4)
            xstage = s

    def xr(stage, k):
        src = x_of[stage]
        return x_ready.at(src, k + 1 if x_ready.times[src] == KT else k // 2 + 1)

    XL_FIRST = {"even": 1, "odd": 0}
    X_TILE = {"even": 4, "odd": 0, "mix0": 0, "mix1": 0}

    def flat(v):
        return v.rearrange("p k t -> p (k t)")

    def vec(tile, row):
        return vecT[:, tile, row:row + 1]

    G_PE = {n: i + 1 for i, n in enumerate(["z", "G", "kt", "A", "kv", "o", "ostat"])}
    G_ACT = {n: i + 1 for i, n in enumerate(["glow", "z", "lnz", "lnf", "gs", "decays", "keT", "osq", "oroot"])}
    G_DVE = {n: i + 1 for i, n in enumerate(["fz", "zabs", "fabs", "gk", "fsum", "decayed", "A", "state", "o"])}
    EVEN = ["small", 0, "z", 1, "gk", 2, "G", 3, "decay", 4, 5, "kt", 6, "A", 7, "kv", 8, "o", 9, "norm", 10, 11, "halves"]
    EVEN_COLS = [256, 0, 512, 768, 1024, 1280, 1552, 1808, 2064, 2320, 2576, 2832]
    E_K, E_Q, E_V, E_G, F_Q, F_K, F_V = 0, 1, 2, 4, 6, 8, 10

    four, eight = range(4), range(8)
    M_PE = {n: i + 1 for i, n in enumerate([*(f"wuk{i}" for i in four), "small", "widx", *(f"index{i}" for i in eight), "cstat",
                                            *(f"K{i}" for i in four), *(f"V{i}" for i in four)])}
    M_ACT = {n: i + 1 for i, n in enumerate([*(f"wuk{i}" for i in four), "small", "widx",
                                             *(f"relu{i}" for i in eight), "csq", "croot", *(f"K{i}" for i in four), *(f"V{i}" for i in four)])}
    M_DVE = {n: i + 1 for i, n in enumerate([*(f"scored{i}" for i in eight), "c", "mask"])}
    ODD = ["wuk", 0, "small", 1, "index", 2, "csq", "top", 3, "cnorm", "top", 4, "top", "K", 5, "top", "V", "mask", 6]
    ODD_COLS = [1280, 1536, 1024, 0, 256, 512, 768]
    O_C, O_QI, O_Q = 2, 0, 3
    SEARCH_ROUNDS = TOPK // 8 // ODD.count("top")

    MIX = [0, 1, 2, 3, "glu", 4, 5, "ropeq", 6, 7, "ropek", 8, 9]
    MIX_COLS = [1536 + 256 * i for i in range(4)] + [256 * i for i in range(6)] + [2560 + 256 * i for i in range(8)]
    X_Q, X_K, X_V, X_GA, X_GC = 4, 6, 8, 10, 14
    TAPS_PER_STEP = 5
    ROPE_STEPS = 2 + 2 * 9

    def ada(l, part, k, plus_one=0):
        return adaT[:, l, plus_one, part * KT + k:part * KT + k + 1]

    def half(h):
        return slice(HD * (h % 2), HD * (h % 2) + HD)

    def in_slots(first, h, pj=pj):
        t = h // 2
        return pj[half(h), first + t // 2, (t % 2) * T:(t % 2 + 1) * T]

    def att_of(s):
        if s == "even":
            return (lambda h: in_slots(F_Q, h), lambda h: in_slots(F_K, h),
                    lambda h, b: pj[:, F_V + h // 4, b * T + (h % 4) * HD:b * T + (h % 4 + 1) * HD],
                    lambda h: cmask[:, :])

        if KIND[s] == "mix":
            return (lambda h: in_slots(X_Q, h, pm), lambda h: in_slots(X_K, h, pm),
                    lambda h, b: pm[:, X_V + h // 4, b * T + (h % 4) * HD:b * T + (h % 4 + 1) * HD],
                    lambda h: cmask[:, :])
        if s == "odd":
            return (lambda h: in_slots(O_Q, h), lambda h: KTm[half(h), h // 2, :],
                    lambda h, b: Vm[:, b, h * HD:(h + 1) * HD], lambda h: bm[:, h % 3, :])

    def steps_of(eng, n, head, body, step):
        turns = (n - head) // body
        for i in range(head):
            step(i, i, None)
        with eng.Fori(0, turns) as g:
            for j in range(body):
                step(g * body + (head + j), head + j, g)
        for i in range(head + turns * body, n):
            step(i, i, None)

    def ffn_shape(s):
        return (2, FF_STEPS, 2, 2) if KIND[s] == "ffn" else (1, FF2_STEPS, 3, 3)

    def acc_ready(eng, s, q):
        if q < 3:
            eng.wait_ge(acc_made.sem, acc_made.at(s, q + 1))
        else:
            eng.wait_ge(chunk_used.sem, base[s] + CHUNKS_OF[KIND[s]])

    per_conv = 2 + 2 * (CONV_K - 1)
    pool_conv = {f"mix{l}": 4 * 3 * ADA_PER_FFN + ROPE_STEPS + (l + 1) * per_conv for l in range(2)}
    MODS = ["mod0a", "mod0b", "mod1a", "mod1b"]

    ADA_OF = {f"ffn{i}": divmod(i * ADA_PER_FFN, 24) for i in range(4)}
    for s in ADA_OF:
        ada_summed.plan(s, ADA_PER_FFN)
        ada_made.plan(s, 1)

    block = ctx.enter_context(nc.Block())

    N_IDENT, N_ONES, N_CONST = 2, 5, 18

    @block.sync
    def _(sp):
        for b in range(TB):
            sp.dma_start(xin[:, b, :], A["x"][0, b * P:(b + 1) * P, :]).then_inc(x_loaded.sem, 16)
        t0 = [("norm_g", "l i (k d) -> (l i k) d", V_NORM, 0), ("final_norm_g", "(k d) -> k d", V_FINAL, 0),
              ("gla_norm_g", "l (k d) -> (l k) d", V_GLA, 0), ("mla_kv_norm_g", "l (k d) -> (l k) d", V_MLA, 0),
              ("ln_mix_g_2", "l (k d) -> (l k) d", V_MIXG, 0), ("ln_mix_b_2", "l (k d) -> (l k) d", V_MIXB, 0),
              ("ln_ffn_g_2", "l (k d) -> (l k) d", V_FFNG, 0), ("ln_ffn_b_2", "l (k d) -> (l k) d", V_FFNB, 0),
              ("conv_dw_b_2", "l (k d) -> (l k) d", V_DWB, 1), ("conv_ln_g_2", "l (k d) -> (l k) d", V_CLNG, 1),
              ("conv_ln_b_2", "l (k d) -> (l k) d", V_CLNB, 1), ("c_2", "l (k d) -> (l k) d", V_C, 1),
              ("b_ada_2", "l (k d) -> (l k) d", V_ADA, 1)]
        for name, pattern, row, tile in t0:
            src = A[name].rearrange(pattern, d=P)
            sp.dma_start(rows[row:row + src.shape[0], tile, :], src).then_inc(in_loaded.sem, 16)
        for l in range(2):
            src = A["conv_dw_w_2"][l].rearrange("j (k d) -> (j k) d", d=P)
            sp.dma_start(rows[0:src.shape[0], 2 + l, :], src).then_inc(in_loaded.sem, 16)

        def sp_small():
            sp.dma_start(bt[0:32, 0:16], A["t5_table"]).then_inc(table_loaded.sem, 16)
            sp.dma_start(bt[0:32, 16:16 + BIAS_COLS], A["buckets"]).then_inc(table_loaded.sem, 16)
            w = A["even_w_in"][0].rearrange("(k p) n -> p k n", p=P)
            sp.wait_ge(const_made.sem, N_CONST)
            sp.dma_start(wsm[:, :, 0:16], w[:, :, 1536:1552]).then_inc(wsm_loaded.sem, 16)
            sp.dma_start(wsm[:, :, 32:40], w[:, :, 3088:3096]).then_inc(wsm_loaded.sem, 16)
            sp.dma_start(wgate[0:16, :], A["gla_w_gate"][0]).then_inc(wsm_loaded.sem, 16)
            sp.dma_start(bgate[0:1, :], A["gla_b_gate"]).then_inc(wsm_loaded.sem, 16)
            sp.dma_start(bfox[32:40, :], A["fox_b_f"].rearrange("a h -> h a")).then_inc(wsm_loaded.sem, 16)

        def load(c, src, view, turn=None, per_turn=0):
            if c >= RING:
                sp.wait_ge(lo_made.sem, shifted(c - RING + 1, turn, per_turn))
            sp.dma_start(raw[:, c % RING, :].rearrange(*view[0:1], **view[1]), src).then_inc(loaded[c % RING].sem, 16)

        A_VIEW = ("p (k n) -> p k n", {"k": KT})
        B_VIEW = ("p (k n) -> p k n", {"k": 2})

        def columns(w, col):
            return w.rearrange("(k p) n -> p k n", p=P)[:, :, bass.ds(col, 256)]

        def sp_ffn(s):
            n_in, steps, body, _ = ffn_shape(s)
            c0 = base[s]
            if KIND[s] == "ffn":
                l, i = divmod(int(s[3:]), 2)
                w_in, w_out = A["ffn_w_in"][l, i], A["ffn_w_out"][l, i]
            else:
                w_in, w_out = A["w_up_2"][int(s[2:])], A["w_down_2"][int(s[2:])]
            w_out = w_out.rearrange("(k p) n -> p k n", p=P)

            def step(i, st, turn):
                c = c0 + (0 if st == 0 else n_in + (n_in + 1) * (st - 1))
                per = (n_in + 1) * body
                for half in range(n_in):
                    load(c + half, columns(w_in, i * 256 + half * FF), A_VIEW, turn, per)
                if st > 0:
                    load(c + n_in, w_out[:, bass.ds(i * 2 - 2, 2), :], B_VIEW, turn, per)

            def load_ada(n, slot, times):
                l, first = ADA_OF[s]
                if times is not None:
                    sp.wait_ge(ada_summed.sem, times)
                sp.dma_start(ada_raw[:, slot, :].rearrange("p (k n) -> p k n", k=KT),
                             columns(A["w_ada_2"][l], (first + n) * T)).then_inc(ada_loaded[slot].sem, 16)

            def with_ada(i, st, turn):
                step(i, st, turn)
                if s == "ffn0" and st == 0:
                    sp_small()
                if s in ADA_OF and st >= 2:
                    load_ada(i, st % 2, shifted(ada_summed.at(s, st - 1), turn, body))
                if s in ADA_OF and st == 1:
                    if s != "ffn0":
                        sp.wait_ge(x_ready.sem, x_ready.at(x_of[s]))
                    for n in range(2):
                        load_ada(n, n, ada_summed.at(s, 0) if s != "ffn0" else None)

            steps_of(sp, steps, 2, body, with_ada)
            if s in ADA_OF:
                load_ada(ADA_PER_FFN - 1, (ADA_PER_FFN - 1) % 2, ada_summed.at(s, ADA_PER_FFN - 2))
            if s == "ffn3":
                for dst, src in ((posi, A["positions_2"].broadcast_to((P, T))),
                                 (freq, A["rope_freq"]), (turn, A["rope_turn"])):
                    sp.dma_start(dst, src).then_inc(rope_loaded.sem, 16)
            load(c0 + (n_in + 1) * steps - 1, w_out[:, 2 * steps - 2:2 * steps, :], B_VIEW)

        def sp_even(s):
            w = A["even_w_in"][0]
            for n, col in enumerate(EVEN_COLS):
                load(base[s] + n, columns(w, col), A_VIEW)
            for j in range(4):
                load(base[s] + 12 + j, columns(A["even_w_out"][0], j * 256), A_VIEW)

        def sp_odd_small():
            sp.wait_ge(x_ready.sem, x_ready.at("even"))
            w = A["odd_w_in"][0].rearrange("(k p) n -> p k n", p=P)
            for at in (0, 64):
                sp.dma_start(wsm[:, :, at:at + 64], w[:, :, 1792:1856]).then_inc(wsm_loaded.sem, 16)
            sp.dma_start(wsm[:, :, 128:136], w[:, :, 1856:1864]).then_inc(wsm_loaded.sem, 16)
            sp.dma_start(wuk, A["mla_w_uk"][0].rearrange("(m a) d l -> (a d) m l", a=2)).then_inc(mla_loaded.sem, 16)

        def sp_odd(s):
            for n, col in enumerate(ODD_COLS):
                load(base[s] + n, columns(A["odd_w_in"][0], col), A_VIEW)
                if n == 4:
                    sp.wait_ge(mla_act.sem, M_ACT["wuk3"])
                    sp.wait_ge(mla_pe.sem, M_PE["wuk3"])
                    sp.wait_ge(bias_stored.sem, 16)
                    src = bass.AP(bias_rows, 0, [[1, P], [BIAS_COLS, 16], [1, T]])
                    sp.dma_start(bias8, src).then_inc(bias_loaded.sem, 16)
                if n == 5:
                    sp.wait_ge(ada_made.sem, ada_made.at("ffn2"))
                    for l in range(2):
                        sp.dma_start(wuv[:, l, :].rearrange("p (h d) -> p h d", d=HD),
                                     A["mla_w_uv"][0, :, l * P:(l + 1) * P, :].rearrange("h p d -> p h d")).then_inc(wuv_loaded.sem, 16)
            for j in range(4):
                load(base[s] + 7 + j, columns(A["odd_w_out"][0], j * 256), A_VIEW)

        def sp_mix(s):
            l, c0 = int(s[3:]), base[s]
            for n, col in enumerate(MIX_COLS):
                load(c0 + n, columns(A["w_in_2"][l], col), A_VIEW)
            for n in range(4):
                w = (A["w_attn_br_2"], A["w_conv_pw_2"])[n // 2][l].rearrange("(k p) n -> p k n", p=P)
                load(c0 + 18 + n, w[:, :, (n % 2) * 512:(n % 2 + 1) * 512], ("p (k n) -> p k n", {"k": 4}))
            for j in range(4):
                load(c0 + 22 + j, columns(A["w_out_2"][l], j * 256), A_VIEW)

        for kind, s in STAGES:
            if kind == "mix":
                sp_mix(s)
            if kind in ("ffn", "sq"):
                sp_ffn(s)
                if s == "ffn1":
                    sp_odd_small()
            if kind == "odd":
                sp_odd(s)
            if kind == "even":
                sp_even(s)
        for q in range(2):
            for b, copied in enumerate((out_copied, out_copied_dve)):
                sp.wait_ge(copied.sem, q + 1)
                sp.dma_start(out[0, b * P:(b + 1) * P, q * 512:(q + 1) * 512], xin[:, b, q * 512:(q + 1) * 512]).then_inc(stored.sem, 16)
        sp.wait_ge(stored.sem, 16 * 2 * TB)

    N_IN = 16 * 15

    @block.gpsimd
    def _(pool):
        made = [0]

        def const(ins):
            made[0] += 1
            ins.then_inc(const_made.sem, 1)
            pool.wait_ge(const_made.sem, made[0])

        def keep(m, compare, fill, base, pattern, per_partition):
            const(pool.affine_select(out=m, in_=m, compare_op=compare, fill=fill, base=base, pattern=pattern,
                                     channel_multiplier=per_partition))

        const(pool.memset(ident[:, :], 0.0))
        keep(ident[:, :], ALU.not_equal, 1.0, 0, [[-1, P]], 1)
        assert made[0] == N_IDENT
        const(pool.memset(ones[:, :], 1.0))
        const(pool.memset(epsc[:, 0:1], EPS))
        const(pool.memset(epsc[:, 1:2], LN_EPS))
        assert made[0] == N_ONES
        const(pool.memset(wsm[:, :, 0:40], 0.0))
        const(pool.memset(onesT, 1.0))
        const(pool.memset(sel[32:40, :, :], 0.0))
        keep(sel[32:40, :, :], ALU.not_equal, -8.0, 0, [[-1, 8], [0, P]], 1)
        const(pool.memset(cmask[:, :], 0.0))
        for at in (0, 256):
            keep(cmask[:, at:at + P], ALU.is_ge, NEG, 0, [[-1, P]], 1)
        for m, value in ((tri, 1.0 / 16), (trib, 1)):
            const(pool.memset(m[:, :], value))
            keep(m[:, :], ALU.is_ge, 0.0, 0, [[1, P]], -1)
            const(pool.memset(m[0:CH, CH:P], 0))
        assert made[0] == N_CONST

        def pool_odd(s):
            pool.wait_ge(bias_loaded.sem, 16)
            pool.wait_ge(mla_dve.sem, M_DVE["mask"])
            for h in range(heads_of[s]):
                if h >= 3:
                    pool.wait_ge(ns_made.sem, ns_made.at(s, h - 2))
                pool.tensor_tensor(bm[:, h % 3, 0:P], bias8[:, h, P - 1::-1], dm[:, 0:P], ALU.add)
                pool.tensor_tensor(bm[:, h % 3, P:384], bias8[:, h, ::-1], dm[:, P:384], ALU.add).then_inc(bm_made.sem, 1)

        def link(ins):
            n_step[0] += 1
            ins.then_inc(pool_step.sem, 1)
            pool.wait_ge(pool_step.sem, n_step[0])

        n_step = [0]

        def pool_ada(s):
            first, c0 = n_step[0], ada_summed.at(s, 0)
            per_chunk = 3
            pool.wait_ge(csil_made.sem, 1)
            if s != "ffn0":
                pool.wait_ge(ada_turned.sem, int(s[3:]))
            with pool.Fori(0, ADA_PER_FFN // 2) as g:
                for slot in range(2):
                    def done(n):
                        return g * (2 * per_chunk) + (first + slot * per_chunk + n)
                    w = ada_raw[:, slot, :]
                    tiles = w.rearrange("p (k n) -> p k n", k=KT)
                    pool.wait_ge(ada_loaded[slot].sem, g * 16 + 16 * (c0 // 2 + 1))
                    pool.tensor_tensor(tiles, tiles, csil[:, :].unsqueeze(2).broadcast_to((P, KT, T)), ALU.mult).then_inc(pool_step.sem, 1)
                    for n, size in ((1, 1024), (2, 512)):
                        pool.wait_ge(pool_step.sem, done(n))
                        pool.tensor_tensor(w[:, 0:size], w[:, 0:size], w[:, size:2 * size], ALU.add).then_inc(pool_step.sem, 1)
                    pool.wait_ge(pool_step.sem, done(3))
                    pool.tensor_tensor(arena[:, bass.ds(g * (2 * T) + (at_sum + slot * T), T)], w[:, 0:T], w[:, T:2 * T],
                                       ALU.add).then_inc(ada_summed.sem, 1)
            n_step[0] += per_chunk * ADA_PER_FFN

        def pool_rope():
            pool.wait_ge(rope_loaded.sem, 16 * 3)
            link(pool.tensor_copy(turns, posi))
            link(pool.tensor_scalar(ang, turns, freq, None, ALU.mult))
            for i in range(2):
                link(pool.tensor_scalar(turns, ang, 1 / (2 * math.pi), 0.25 * i, ALU.mult, ALU.add))
                link(pool.tensor_scalar(turns, turns, ROUND, ROUND, ALU.add, ALU.subtract))
                if i == 1:
                    pool.wait_ge(rope_made.sem, 2)
                src = ang
                for part in TWO_PI:
                    link(pool.tensor_scalar(part_turns, turns, part, None, ALU.mult))
                    link(pool.tensor_tensor(red, src, part_turns, ALU.subtract))
                    src = red
                link(pool.tensor_scalar(red, red, 0.5 * math.pi * i, PI_BELOW, ALU.add, ALU.min))
                pool.tensor_scalar(red, red, -PI_BELOW, None, ALU.max).then_inc(rope_made.sem, 1)

        def pool_mix(s):
            l, acc, first = int(s[3:]), cacc[:, 2:4, :], n_step[0]
            pool.wait_ge(glu_made.sem, glu_made.at(s))
            for ct in (2, 3):
                pool.tensor_scalar(cacc[:, ct, :], hpad[:, ct, 0:T], vec(2 + l, ct), vec(1, V_DWB + 4 * l + ct), ALU.mult,
                                   ALU.add).then_inc(pool_step.sem, 1)
            with pool.Fori(0, (CONV_K - 1) // 2) as g:
                for b in range(2):
                    w = vecT[:, 2 + l, bass.ds(g * (2 * CT) + ((1 + b) * CT + 2), 2)].unsqueeze(2).broadcast_to((P, 2, T))
                    pool.tensor_tensor(ptmp[:, b, :, :], hpad[:, 2:4, bass.ds(g * 2 + (1 + b), T)], w, ALU.mult).then_inc(pool_step.sem, 1)
                    pool.wait_ge(pool_step.sem, g * 4 + (first + 3 + 2 * b))
                    pool.tensor_tensor(acc, acc, ptmp[:, b, :, :], ALU.add).then_inc(pool_step.sem, 1)
            n_step[0] += per_conv
            assert n_step[0] == pool_conv[s]

        for kind, s in STAGES:
            if kind == "odd":
                pool_odd(s)
            if kind == "mix":
                pool_mix(s)
            if s in ADA_OF:
                pool_ada(s)
            if kind == "rope":
                pool_rope()

    @block.tensor
    def _(pe):
        def three(o, wa, wb, ma, mb, start, stop, **kw):
            pe.matmul(o, wa, ma, start=start, stop=False, **kw)
            pe.matmul(o, wa, mb, start=False, stop=False, **kw)
            return pe.matmul(o, wb, ma, start=False, stop=stop, **kw)

        def tile_of(c, k, m, n):
            at = slice(k * n + m * P, k * n + (m + 1) * P)
            return wh[:, c % RING, at], wl[:, c % RING, at]

        def pe_setup():
            pe.wait_ge(const_made.sem, N_IDENT)
            pe.wait_ge(x_loaded.sem, 16 * TB)
            for q in range(4):
                for j in range(2):
                    for b in range(TB):
                        k = 2 * q + j
                        last = pe.transpose(bank[q][:, j * T + b * P:j * T + (b + 1) * P],
                                            xin[:, b, k * P:(k + 1) * P], ident[:, :])
                last.then_inc(setup_pe.sem, 1)
            pe.wait_ge(in_loaded.sem, N_IN)
            for v in range(4):
                last = pe.transpose(bank[7][:, v * P:v * P + V_ROWS[v]], rows[0:V_ROWS[v], v, :],
                                    ident[0:V_ROWS[v], 0:V_ROWS[v]])
            last.then_inc(setup_pe.sem, 1)
            pe.wait_ge(const_made.sem, N_ONES)

        def pe_table():
            pe.wait_ge(const_made.sem, N_CONST)
            pe.wait_ge(table_loaded.sem, 16 * 2)
            pe.wait_ge(root_made.sem, 1)
            pe.matmul(bank[STAT][0:16, 0:BIAS_COLS], bt[0:32, 0:16], bt[0:32, 16:16 + BIAS_COLS], start=True,
                      stop=True).then_inc(setup_pe.sem, 1)

        def pe_rms(s):
            for k in range(KT):
                pe.wait_ge(sq_made.sem, sq_made.at(s, k + 1))
                last = pe.matmul(bank[STAT][:, 0:T], ones[:, :], xn[:, k, :], start=(k == 0), stop=(k == KT - 1))
            last.then_inc(stat_made.sem, 1)

        def pe_ffn(s, moving):
            n_in, steps, body, bufs = ffn_shape(s)
            c0 = base[s]

            def down(c, i, st, turn):
                pe.wait_ge(lo_made.sem, shifted(c + 1, turn, (n_in + 1) * body))
                pe.wait_ge(hl_made.sem, shifted(hl_made.at(s, n_in * (st + 1)), turn, n_in * body))
                final = st == steps - 1
                for k, m in [(k, m) for m in range(KT) for k in range(2)] if final else [(k, m) for k in range(2) for m in range(KT)]:
                    o = bank[m // 2][:, (m % 2) * T:(m % 2 + 1) * T]
                    a, b = tile_of(c, k, m, D)
                    mv = slice(k * T, (k + 1) * T)
                    last = three(o, a, b, hh[:, st % bufs, mv], hl[:, st % bufs, mv],
                                 start=(st == 0 and k == 0 and m % 2 == 0),
                                 stop=(final and k == 1), skip_group_check=True)
                    if final and k == 1 and m % 2 == 1 and m < KT - 1:
                        last.then_inc(acc_made.sem, 1)
                last.then_inc(chunk_used.sem, 1)

            def up_sq(c, st, turn, per):
                o = bank[4 + st % 3]
                pe.wait_ge(lo_made.sem, shifted(c + 1, turn, per))
                if st >= 2:
                    pe.wait_ge(act_made.sem, shifted(act_made.at(s, st - 2), turn, body))
                for f, k in [(f, k) for f in range(2) for k in range(KT)] if st > 0 else [(f, k) for k in range(KT) for f in range(2)]:
                    if st == 0 and f == 0:
                        pe.wait_ge(xl_made.sem, xl_made.at(moving, k + 1))
                    last = three(o[:, f * T:(f + 1) * T], *tile_of(c, k, f, T), xh[:, k, :], xl[:, k, :],
                                 start=(k == 0 and f == 0) if st == 0 else (k == 0), stop=(k == KT - 1), skip_group_check=True)
                last.then_inc(chunk_used.sem, 1)

            def step(i, st, turn):
                c = c0 + (0 if st == 0 else n_in + (n_in + 1) * (st - 1))
                per = (n_in + 1) * body
                if n_in == 1:
                    up_sq(c, st, turn, per)
                    if st > 0:
                        down(c + n_in, i, st - 1, turn)
                    return
                if s == "ffn0" and st == 1:
                    pe_table()
                if st > 0:
                    pe.wait_ge(h_made.sem, shifted(h_made.at(s, 2 * st), turn, 2 * body))
                for half in range(n_in):
                    pe.wait_ge(lo_made.sem, shifted(c + half + 1, turn, per))
                    tiles = [(f, k) for f in range(2) for k in range(KT)] if st > 0 or half > 0 else [(f, k) for k in range(KT) for f in range(2)]
                    for f, k in tiles:
                        if st == 0 and half == 0 and f == 0:
                            pe.wait_ge(xl_made.sem, xl_made.at(moving, k + 1))
                        last = three(bank[4 + f][:, half * T:(half + 1) * T], *tile_of(c + half, k, f, T),
                                     xh[:, k, :], xl[:, k, :], start=(k == 0), stop=(k == KT - 1))
                        if f == 0 and k == KT - 1 and half == n_in - 1:
                            last.then_inc(a_made.sem, 1)
                    last.then_inc(chunk_used.sem, 1)
                if st == 0:
                    return
                down(c + n_in, i, st - 1, turn)

            steps_of(pe, steps, 2, body, step)
            down(c0 + (n_in + 1) * steps - 1, None, steps - 1, None)

        def pe_first_chunk(s, c, moving):
            pe.wait_ge(lo_made.sem, c + 1)
            for k in range(KT):
                pe.wait_ge(xl_made.sem, xl_made.at(moving, k + 1))
                for m in range(2):
                    last = three(bank[2][:, m * T:(m + 1) * T], *tile_of(c, k, m, T), xh[:, k, :], xl[:, k, :],
                                 start=(k == 0 and m == 0), stop=(k == KT - 1), skip_group_check=True)
            last.then_inc(chunk_used.sem, 1)

        def pe_chunk(s, n, c, tokens_out):
            if n >= 2:
                pe.wait_ge(proj_out.sem, proj_out.at(s, n - 1))
            pe.wait_ge(lo_made.sem, c + 1)
            for m in range(2):
                for k in range(KT):
                    o = bank[2 + n % 2][:, m * T:(m + 1) * T]
                    if tokens_out:
                        tok = slice(m * P, (m + 1) * P)
                        col = slice(k * T, (k + 1) * T)
                        last = three(o, xh[:, k, tok], xl[:, k, tok], wh[:, c % RING, col], wl[:, c % RING, col],
                                     start=(k == 0), stop=(k == KT - 1))
                    else:
                        last = three(o, *tile_of(c, k, m, T), xh[:, k, :], xl[:, k, :], start=(k == 0), stop=(k == KT - 1))
            last.then_inc(chunk_used.sem, 1)

        def ready(s, k):
            return {"mix": 3 + 1 + k // 2, "even": 1 + max(0, k - 3), "odd": k + 1}[KIND[s]]

        def pe_out(s, c0):
            pe.wait_ge(lo_made.sem, c0 + 2)
            if KIND[s] == "mix":
                pe.wait_ge(merged.sem, merged.at(s, 2))
            for ks in (range(0, 4), range(4, KT)):
                for j in range(2):
                    for m in range(2):
                        for k in ks:
                            pe.wait_ge(xl_made.sem, xl_made.at(s, ready(s, k)))
                            last = three(bank[2 + j][:, m * T:(m + 1) * T], *tile_of(c0 + j, k, m, T), xh[:, k, :], xl[:, k, :],
                                         start=(k == 0 and m == 0), stop=(k == KT - 1), skip_group_check=True)
                    if ks[0] > 0:
                        last.then_inc(chunk_used.sem, 1)
            for j in range(2, 4):
                c = c0 + j
                pe.wait_ge(lo_made.sem, c + 1)
                if j >= 2:
                    if KIND[s] == "mix":
                        pe.wait_ge(y_out.sem, y_out.at(s, j - 1))
                    else:
                        pe.wait_ge(x_ready.sem, x_ready.at(s, j - 1))
                for m in range(2):
                    for k in range(KT):
                        last = three(bank[2 + j % 2][:, m * T:(m + 1) * T], *tile_of(c, k, m, T), xh[:, k, :], xl[:, k, :],
                                     start=(k == 0), stop=(k == KT - 1))
                last.then_inc(chunk_used.sem, 1)

        def pe_attention(s, meanwhile=None):
            H = heads_of[s]
            q, k, v, _ = att_of(s)

            def scores(h):
                if h >= 2:
                    pe.wait_ge(ns_made.sem, ns_made.at(s, h - 1))
                b = bank[4 + h % 2]
                fox = s == "even"
                for o, qt, kt in ((b[:, 0:P], slice(0, P), slice(0, P)), (b[:, P:384], slice(P, T), slice(0, T))):
                    last = pe.matmul(o, q(h)[:, qt], k(h)[:, kt], start=True, stop=not fox)
                    if fox:
                        last = pe.matmul(o, sel[32:40, h, :], fsum[32:40, kt], start=False, stop=True)
                last.then_inc(score_made.sem, 1)

            def transposes(h):
                pe.wait_ge(pn_made.sem, pn_made.at(s, h + 1))
                if h >= 2:
                    pe.wait_ge(pt_out.sem, pt_out.at(s, h - 1))
                for j in range(3):
                    at = slice(j * P, (j + 1) * P)
                    last = pe.transpose(bank[6 + h % 2][:, at], pr[:, h % 3, at], ident[:, :])
                last.then_inc(pt_made.sem, 1)

            def output(h):
                pe.wait_ge(pt_out.sem, pt_out.at(s, h + 1))
                pair = h // 2
                if pair >= 2 and h % 2 == 0:
                    if KIND[s] == "mix":
                        pe.wait_ge(ao_made.sem, ao_made.at(s, pair - 1))
                    else:
                        pe.wait_ge(xl_made.sem, xl_made.at(s, XL_FIRST[s] + pair - 1))
                b = bank[pair % 2]
                pe.matmul(b[half(h), 0:T], v(h, 0), pt[:, h % 2, 0:T], start=True, stop=False)
                pe.matmul(b[half(h), P:T], v(h, 1), pt[:, h % 2, T:384], start=False, stop=True).then_inc(pv_made.sem, 1)

            for i in range(H + 3):
                if i < H:
                    scores(i)
                if meanwhile:
                    meanwhile(i)
                if 2 <= i < H + 2:
                    transposes(i - 2)
                if i >= 3:
                    output(i - 3)

        def pe_even(s, moving):
            c0 = base[s]

            def small():
                pe.wait_ge(wsm_loaded.sem, 16 * 5)
                for k in range(KT):
                    pe.wait_ge(xn_made.sem, xn_made.at(moving, k + 1))
                    last = pe.matmul(bank[STAT][0:40, 0:T], wsm[:, k, 0:40], xn[:, k, :], start=(k == 0), stop=(k == KT - 1))
                last.then_inc(small_made.sem, 1)

            def z():
                pe.wait_ge(gla_act.sem, G_ACT["glow"])
                pe.wait_ge(ada_made.sem, ada_made.at("ffn0"))
                for b in range(TB):
                    o = bank[7][:, b * T:(b + 1) * T]
                    pe.matmul(o, glow[0:16, b * P:(b + 1) * P], wgate[0:16, :], start=True, stop=False)
                    last = pe.matmul(o, ones[0:1, :], bgate[0:1, :], start=False, stop=True)
                last.then_inc(gla_pe.sem, 1)

            def cumulate():
                pe.wait_ge(gla_dve.sem, G_DVE["gk"])
                for m in range(2):
                    for b in range(TB):
                        last = pe.matmul(bank[7][:, m * T + b * P:m * T + (b + 1) * P],
                                         gk[:, b * T + m * P:b * T + (m + 1) * P], tri[:, :], start=True, stop=True)
                last.then_inc(gla_pe.sem, 1)

            def turn_keys():
                pe.wait_ge(gla_dve.sem, G_DVE["decayed"])
                for b in range(TB):
                    for m in range(2):
                        last = pe.transpose(bank[7][:, (b * 2 + m) * P:(b * 2 + m + 1) * P], ke[:, m, b * P:(b + 1) * P], ident[:, :])
                last.then_inc(gla_pe.sem, 1)

            def scores():
                pe.wait_ge(gla_act.sem, G_ACT["keT"])
                for h in range(4):
                    for b in range(TB):
                        tok = slice(b * P, (b + 1) * P)
                        last = pe.matmul(bank[6 + h % 2][:, (h // 2) * T + b * P:(h // 2) * T + (b + 1) * P],
                                         kd[half(h), h // 2, tok], qd[half(h), h // 2, tok], start=True, stop=True)
                last.then_inc(gla_pe.sem, 1)

            def chunk_states():
                pe.wait_ge(gla_dve.sem, G_DVE["A"])
                for ch in range(3):
                    rows_ = slice((ch % 2) * CH, (ch % 2 + 1) * CH)
                    for h in range(4):
                        o = bank[6 + ch % 2][half(h), (ch // 2) * T + (h // 2) * P:(ch // 2) * T + (h // 2 + 1) * P]
                        last = pe.matmul(o, keT[rows_, ch // 2, h // 2, half(h)],
                                         pj[rows_, E_V + h // 2, (ch // 2) * T + (h % 2) * P:(ch // 2) * T + (h % 2 + 1) * P],
                                         start=True, stop=True)
                last.then_inc(gla_pe.sem, 1)

            def outputs():
                pe.wait_ge(gla_dve.sem, G_DVE["state"])
                for h in range(4):
                    o, at = bank[6 + h % 2], (h // 2) * T
                    for b in range(TB):
                        pe.matmul(o[:, at + b * P:at + (b + 1) * P],
                                  pj[:, E_V + h // 2, b * T + (h % 2) * P:b * T + (h % 2 + 1) * P],
                                  AT[:, h % 2, at + b * P:at + (b + 1) * P],
                                  start=(h // 2 == 0 and b == 0), stop=False, skip_group_check=True)
                    for ch in range(1, 4):
                        last = pe.matmul(o[:, at + ch * CH:at + (ch + 1) * CH], state[half(h), ch - 1, h // 2, :],
                                         qd[half(h), h // 2, ch * CH:(ch + 1) * CH], start=False, stop=True, skip_group_check=True)
                last.then_inc(gla_pe.sem, 1)

            def norm():
                pe.wait_ge(gla_act.sem, G_ACT["osq"])
                for q in range(2):
                    last = pe.matmul(bank[4 + q][:, :], ones[:, :], osq[:, q * 512:(q + 1) * 512], start=True, stop=True)
                last.then_inc(gla_pe.sem, 1)

            todo = {"small": small, "z": z, "G": cumulate, "kt": turn_keys, "A": scores, "kv": chunk_states,
                    "o": outputs, "norm": norm}
            for step in EVEN:
                if step == 0:
                    pe_first_chunk(s, c0, moving)
                elif isinstance(step, int):
                    pe_chunk(s, step, c0 + step, step in (2, 3, 10, 11))
                elif step in todo:
                    todo[step]()
            pe.wait_ge(gla_dve.sem, G_DVE["o"])
            pe.wait_ge(gla_dve.sem, G_DVE["fsum"])
            pe_attention(s)
            pe_out(s, c0 + 12)

        def pe_odd(s, moving):
            c0 = base[s]

            def turn_wuk():
                pe.wait_ge(mla_loaded.sem, 16)
                for g in range(4):
                    for j in range(4):
                        m = 4 * (g % 2) + j
                        last = pe.transpose(bank[QUAD[g]][:, j * P:(j + 1) * P], wuk[:, m, (g // 2) * P:(g // 2 + 1) * P], ident[:, :])
                    last.then_inc(mla_pe.sem, 1)

            def small():
                pe.wait_ge(wsm_loaded.sem, 16 * 8)
                for o, cols in ((bank[6][:, 0:T], slice(0, P)), (bank[6][0:8, T:2 * T], slice(P, P + 8))):
                    for k in range(KT):
                        pe.wait_ge(xn_made.sem, xn_made.at(moving, k + 1))
                        last = pe.matmul(o, wsm[:, k, cols], xn[:, k, :], start=(k == 0), stop=(k == KT - 1))
                last.then_inc(mla_pe.sem, 1)

            def cnorm():
                pe.wait_ge(mla_act.sem, M_ACT["csq"])
                pe.wait_ge(ada_made.sem, ada_made.at("ffn2"))
                for l in range(2):
                    last = pe.matmul(bank[7][:, 0:T], ones[:, :], csq[:, l * T:(l + 1) * T], start=(l == 0), stop=(l == 1))
                last.then_inc(mla_pe.sem, 1)

            def index():
                pe.wait_ge(mla_act.sem, M_ACT["small"])
                for b in range(TB):
                    last = pe.transpose(bank[6][:, b * 8:(b + 1) * 8], wix[0:8, b * P:(b + 1) * P], ident[0:8, 0:8])
                last.then_inc(mla_pe.sem, 1)
                pe.wait_ge(proj_out.sem, proj_out.at(s, 2))
                for h in range(8):
                    pe.wait_ge(mla_act.sem, M_ACT[f"relu{h - 4}"] if h >= 4 else M_ACT["widx"])
                    b = bank[QUAD[h % 4]]
                    for o, qt, kt in ((b[:, 0:P], slice(0, P), slice(0, P)), (b[:, P:384], slice(P, T), slice(0, T))):
                        last = pe.matmul(o, in_slots(O_QI, h)[:, qt], kix[half(h), kt], start=True, stop=True)
                    last.then_inc(mla_pe.sem, 1)

            def keys():
                pe.wait_ge(mla_act.sem, M_ACT["relu7"])
                pe.wait_ge(mla_dve.sem, M_DVE["c"])
                for g in range(4):
                    for j in range(2):
                        for l in range(2):
                            m = 2 * g + j
                            last = pe.matmul(bank[QUAD[g]][:, j * T:(j + 1) * T], wukT[:, l, m * P:(m + 1) * P], cT[:, l, :],
                                             start=(l == 0), stop=(l == 1))
                    last.then_inc(mla_pe.sem, 1)

            def values():
                pe.wait_ge(wuv_loaded.sem, 16 * 2)
                for g in range(4):
                    pe.wait_ge(mla_act.sem, M_ACT[f"K{g}"])
                    for l in range(2):
                        last = pe.matmul(bank[QUAD[g]][:, :], cT[:, l, (g // 2) * P:(g // 2 + 1) * P],
                                         wuv[:, l, (g % 2) * 512:(g % 2 + 1) * 512], start=(l == 0), stop=(l == 1))
                    last.then_inc(mla_pe.sem, 1)

            todo = {"wuk": turn_wuk, "small": small, "cnorm": cnorm, "index": index, "K": keys, "V": values}
            for step in ODD:
                if step == 0:
                    pe_first_chunk(s, c0, moving)
                elif isinstance(step, int):
                    pe_chunk(s, step, c0 + step, False)
                elif step in todo:
                    todo[step]()
            pe.wait_ge(mla_act.sem, M_ACT["V3"])
            pe.wait_ge(proj_out.sem, proj_out.at(s))
            pe_attention(s)
            pe_out(s, c0 + 7)

        def pe_ada(s):
            pe.wait_ge(ada_summed.sem, ada_summed.at(s))
            for n in range(2 * ADA_PER_FFN):
                last = pe.matmul(bank[7][:, n:n + 1], ada_sum[:, n // 2, (n % 2) * P:(n % 2 + 1) * P], ones[:, 0:1], start=True, stop=True)
            last.then_inc(ada_turned.sem, 1)

        def pe_mix(s, moving):
            c0 = base[s]

            def turned(first):
                for i in range(2):
                    n = first + i
                    pe.wait_ge(proj_out.sem, proj_out.at(s, n + 1))
                    if first == X_Q:
                        pe.wait_ge(ada_made.sem, 4)
                    if first == X_K:
                        pe.wait_ge(rope_dve.sem, rope_dve.at(s, i + 1))
                    for m in range(2):
                        last = pe.matmul(bank[6 + i][:, m * T:(m + 1) * T], turn, pm[:, n, m * T:(m + 1) * T], start=True, stop=True)
                    last.then_inc(rope_pe.sem, 1)

            todo = {"ropeq": lambda: turned(X_Q), "ropek": lambda: turned(X_K)}
            for step in MIX:
                if step == 0:
                    pe_first_chunk(s, c0, moving)
                elif isinstance(step, int):
                    pe_chunk(s, step, c0 + step, step in (8, 9))
                elif step in todo:
                    todo[step]()
            pe.wait_ge(proj_out.sem, proj_out.at(s, 10))
            pe.wait_ge(rope_dve.sem, rope_dve.at(s))
            pe_attention(s, lambda i: pe_chunk(s, 10 + i, c0 + 10 + i, False) if i < 8 else None)
            pe.wait_ge(conv_made.sem, conv_made.at(s))
            pe.wait_ge(pool_step.sem, pool_conv[s])
            for ct in range(CT):
                last = pe.matmul(bank[6][:, 0:T], ones[:, :], cacc[:, ct, :], start=(ct == 0), stop=(ct == CT - 1))
            last.then_inc(cln_pe.sem, 1)
            pe.wait_ge(proj_out.sem, proj_out.at(s))
            for n in range(4):
                c, first = c0 + 18 + n, (0, 4, 2, 6)[n]
                if n == 1:
                    pe.wait_ge(cln_act.sem, cln_act.at(s, 2))
                    for ct in range(CT):
                        last = pe.matmul(bank[7][:, 0:T], ones[:, :], ctmp[:, ct, :], start=(ct == 0), stop=(ct == CT - 1))
                    last.then_inc(cln_pe.sem, 1)
                pe.wait_ge(lo_made.sem, c + 1)
                pe.wait_ge(xl_made.sem, xl_made.at(s, 1 if n < 2 else 3))
                for m in range(4):
                    for k in range(4):
                        at = slice(k * 512 + m * P, k * 512 + (m + 1) * P)
                        kk = 4 * (n // 2) + k
                        last = three(bank[first + m // 2][:, (m % 2) * T:(m % 2 + 1) * T], wh[:, c % RING, at], wl[:, c % RING, at],
                                     xh[:, kk, :], xl[:, kk, :], start=(k == 0), stop=(k == 3))
                last.then_inc(chunk_used.sem, 1)
            pe_out(s, c0 + 22)

        def pe_ln(s):
            for k in range(KT):
                pe.wait_ge(x_ready.sem, xr(s, k))
                last = pe.matmul(bank[6][:, 0:T], ones[:, :], x[:, k, :], start=(k == 0), stop=(k == KT - 1))
            last.then_inc(stat_made.sem, 1)
            for k in range(KT):
                pe.wait_ge(sq_made.sem, sq_made.at(s, k // 2 + 1))
                last = pe.matmul(bank[7][:, 0:T], ones[:, :], xn[:, k, :], start=(k == 0), stop=(k == KT - 1))
            last.then_inc(stat_made.sem, 1)

        def pe_store():
            for q in range(2):
                for k in range(4 * q, 4 * q + 4):
                    pe.wait_ge(x_ready.sem, x_ready.at(xstage, k + 1))
                    for b in range(TB):
                        last = pe.transpose(bank[2 * q + b][:, (k % 4) * P:(k % 4 + 1) * P], x[:, k, b * P:(b + 1) * P], ident[:, :])
                last.then_inc(out_made.sem, 1)

        pe_setup()
        moving = None
        for (_, before), (kind, s) in zip([(None, None)] + STAGES, STAGES):
            if kind == "rms":
                pe_rms(s)
                if before in ADA_OF:
                    pe_ada(before)
                moving = s
            if kind in ("ffn", "sq"):
                pe_ffn(s, moving)
            if kind == "even":
                pe_even(s, moving)
            if kind == "odd":
                pe_odd(s, moving)
            if kind == "mod":
                moving = s
            if kind == "mix":
                pe_mix(s, moving)
            if kind == "ln":
                pe_ln(s)
        pe_store()

    @block.scalar
    def _(act):
        def hi(c, turn=None, per_turn=0):
            if turn is None and c >= n_chunks:
                return
            act.wait_ge(loaded[c % RING].sem, shifted(16 * (c // RING + 1), turn, 16 * per_turn // RING))
            if c >= RING:
                act.wait_ge(chunk_used.sem, shifted(c - RING + 1, turn, per_turn))
            act.activation(wh[:, c % RING, :], raw[:, c % RING, :], ACT.Copy).then_inc(hi_made.sem, 1)

        def act_setup():
            for q in range(4):
                act.wait_ge(setup_pe.sem, q + 1)
                act.activation(x[:, 2 * q:2 * q + 2, :].rearrange("p k t -> p (k t)"), bank[q][:, :], ACT.Copy).then_inc(x_ready.sem, 1)

        def act_table():
            rows8 = bt[0:16, 16 + BIAS_COLS:16 + 2 * BIAS_COLS]
            act.wait_ge(setup_pe.sem, 6)
            act.activation(rows8, bank[STAT][0:16, 0:BIAS_COLS], ACT.Copy, scale=8.0).then_inc(act_step.sem, 1)
            act.wait_ge(act_step.sem, 1)
            act.dma_start(bias_rows.ap(), rows8).then_inc(bias_stored.sem, 16)

        def act_rms(s):
            for k in range(KT):
                act.wait_ge(x_ready.sem, xr(s, k))
                act.activation(xn[:, k, :], x[:, k, :], ACT.Square).then_inc(sq_made.sem, 1)
            if s == "rms0":
                hi(0)
            act.wait_ge(stat_made.sem, stat_made.at(s))
            act.activation(root[:, :], bank[STAT][:, 0:T], ACT.Sqrt, scale=1.0 / D, bias=epsc[:, 0:1]).then_inc(root_made.sem, 1)
            if s == "final":
                return
            for k in range(KT):
                act.wait_ge(xn_made.sem, xn_made.at(s, k + 1))
                act.activation(xh[:, k, :], xn[:, k, :], ACT.Copy).then_inc(xh_made.sem, 1)
            if s == "rms0":
                hi(1)
                act.activation(csil[:, :], vecT[:, 1, V_C:V_C + KT], ACT.Silu).then_inc(csil_made.sem, 1)
            hi(base[s] + 2)

        def act_ffn(s):
            n_in, steps, body, bufs = ffn_shape(s)
            func = ACT.Silu if KIND[s] == "ffn" else ACT.Relu
            c0 = base[s]

            def step(i, st, turn):
                c = c0 + (0 if st == 0 else n_in + (n_in + 1) * (st - 1))
                per = (n_in + 1) * body
                if n_in == 1:
                    act.wait_ge(chunk_used.sem, shifted(c + 1, turn, per))
                    act.activation(flat(fs), bank[4 + st % 3][:, :], func).then_inc(act_made.sem, 1)
                    hi(c + RING, turn, per)
                    act.wait_ge(h_made.sem, shifted(h_made.at(s, st + 1), turn, body))
                    act.activation(hh[:, st % bufs, :], flat(fh[:, st % bufs, :, :]), ACT.Copy).then_inc(hh_made.sem, 1)
                    if st > 0:
                        hi(c + 1 + RING, turn, per)
                    if st == 1:
                        act_ln_bias(x_of[s])
                    return
                hi(c + RING, turn, per)
                act.wait_ge(a_made.sem, shifted(a_made.at(s, st + 1), turn, body))
                act.activation(fs[:, 0, :], bank[4][:, 0:T], func).then_inc(act_made.sem, 1)
                act.wait_ge(chunk_used.sem, shifted(c + n_in, turn, per))
                act.activation(fs[:, 1, :], bank[5][:, 0:T], func).then_inc(act_made.sem, 1)
                hi(c + n_in - 1 + RING, turn, per)
                for f in range(2):
                    act.wait_ge(h_made.sem, shifted(h_made.at(s, 2 * st + f + 1), turn, 2 * body))
                    act.activation(hh[:, st % bufs, f * T:(f + 1) * T], fh[:, st % bufs, f, :], ACT.Copy).then_inc(hh_made.sem, 1)
                if st > 0:
                    hi(c + n_in + RING, turn, per)
                if s == "ffn0" and st == 1:
                    act_table()

            steps_of(act, steps, 2, body, step)
            if KIND[s] == "sq":
                for q in range(4):
                    acc_ready(act, s, q)
                    if q >= 2:
                        act.wait_ge(x_ready.sem, x_ready.at(s, q - 1))
                    for m in range(2):
                        last = act.activation(yt[:, q % 2, m * T:(m + 1) * T], bank[q][:, m * T:(m + 1) * T], ACT.Identity,
                                              scale=ada(int(s[2:]), 5, 2 * q + m, 1))
                    last.then_inc(y_out.sem, 1)

        n_step = [1]

        def link(ins):
            n_step[0] += 1
            ins.then_inc(act_step.sem, 1)
            act.wait_ge(act_step.sem, n_step[0])

        def act_chunk(s, n, c, func=ACT.Copy, pj=pj):
            act.wait_ge(chunk_used.sem, c + 1)
            act.activation(pj[:, n, :], bank[2 + n % 2][:, :], func).then_inc(proj_out.sem, 1)
            hi(c + RING)

        def act_attention(s, meanwhile=None):
            H = heads_of[s]

            def exps(h):
                act.wait_ge(ns_made.sem, ns_made.at(s, h + 1))
                if h >= 3:
                    act.wait_ge(pt_made.sem, pt_made.at(s, h - 2))
                act.activation(pr[:, h % 3, 0:P], ns[:, h % 2, 0:P], ACT.Exp, bias=nm[:, h % 2, 0:1], scale=-1.0,
                               accum_out=rs[:, h % 2, 0:1])
                act.activation(pr[:, h % 3, P:384], ns[:, h % 2, P:384], ACT.Exp, bias=nm[:, h % 2, 1:2], scale=-1.0,
                               accum_out=rs[:, h % 2, 1:2]).then_inc(p_made.sem, 1)

            def evacuate(h):
                act.wait_ge(pt_made.sem, pt_made.at(s, h + 1))
                act.activation(pt[:, h % 2, :], bank[6 + h % 2][:, 0:384], ACT.Copy).then_inc(pt_out.sem, 1)

            def upper(pair):
                act.wait_ge(pv_made.sem, pv_made.at(s, 2 * pair + 2))
                if KIND[s] == "mix":
                    act.activation(ao[:, pair, :], bank[pair % 2][:, 0:T], ACT.Copy).then_inc(ao_made.sem, 1)
                    return
                act.activation(xh[:, X_TILE[s] + pair, :], bank[pair % 2][:, 0:T], ACT.Copy).then_inc(xh_made.sem, 1)

            for i in range(H + 4):
                if i < H:
                    exps(i)
                if meanwhile:
                    meanwhile(i)
                if 2 <= i < H + 2:
                    evacuate(i - 2)
                if i >= 4 and i % 2 == 0:
                    upper((i - 4) // 2)

        def act_even(s):
            c0 = base[s]
            act.wait_ge(bias_stored.sem, 16)

            def small():
                act.wait_ge(small_made.sem, 1)
                act.activation(glow[0:16, :], bank[STAT][0:16, 0:T], ACT.Copy).then_inc(gla_act.sem, 1)

            def z():
                act.wait_ge(gla_pe.sem, G_PE["z"])
                act.activation(zs, bank[7][:, :], ACT.Copy).then_inc(gla_act.sem, 1)

            def log_sigmoid():
                act.wait_ge(gla_dve.sem, G_DVE["fabs"])
                link(act.activation(za, za, ACT.Exp, scale=-1.0))
                link(act.activation(fa[32:40, :], fa[32:40, :], ACT.Exp, scale=-1.0))
                act.activation(za, za, ACT.Ln, bias=1.0).then_inc(gla_act.sem, 1)
                act.activation(fa[32:40, :], fa[32:40, :], ACT.Ln, bias=1.0).then_inc(gla_act.sem, 1)

            def cumulated():
                act.wait_ge(gla_pe.sem, G_PE["G"])
                act.activation(gs.rearrange("p m t -> p (m t)"), bank[7][:, :], ACT.Copy).then_inc(gla_act.sem, 1)

            def decays():
                act.wait_ge(gla_act.sem, G_ACT["gs"])
                g = gs.rearrange("p m t -> p (m t)")
                act.activation(eg, g, ACT.Exp)
                act.activation(eng, g, ACT.Exp, scale=-1.0)
                for m in range(2):
                    for ch in range(4):
                        end = (ch + 1) * CH
                        act.activation(eke[:, m, end - CH:end], gs[:, m, end - CH:end], ACT.Exp, scale=-1.0,
                                       bias=gs[:, m, end - 1:end])
                act.activation(egl, gs[:, :, CH - 1::CH], ACT.Exp).then_inc(gla_act.sem, 1)

            def keys():
                act.wait_ge(gla_pe.sem, G_PE["kt"])
                act.activation(keT.rearrange("p b m d -> p (b m d)"), bank[7][:, :], ACT.Copy).then_inc(gla_act.sem, 1)

            def squares():
                act.wait_ge(gla_pe.sem, G_PE["o"])
                act.activation(osq[:, 0:512], bank[6][:, :], ACT.Square)
                act.activation(osq[:, 512:1024], bank[7][:, :], ACT.Square).then_inc(gla_act.sem, 1)

            def norm():
                act.wait_ge(gla_pe.sem, G_PE["ostat"])
                act.activation(oroot[:, 0:512], bank[4][:, :], ACT.Sqrt, scale=1.0 / DV, bias=epsc[:, 0:1])
                act.activation(oroot[:, 512:1024], bank[5][:, :], ACT.Sqrt, scale=1.0 / DV, bias=epsc[:, 0:1]).then_inc(gla_act.sem, 1)

            def halves():
                act.wait_ge(chunk_used.sem, c0 + 12)
                act.wait_ge(gla_dve.sem, G_DVE["o"])
                act.activation(xh[:, 0:4, :].rearrange("p (a b) t -> p a b t", b=2), osq.rearrange("p (b a t) -> p a b t", a=2, b=2),
                               ACT.Copy).then_inc(xh_made.sem, 1)

            todo = {"small": small, "z": z, "gk": log_sigmoid, "G": cumulated, "decay": decays, "kt": keys, "o": squares, "norm": norm, "halves": halves}
            for step in EVEN:
                if isinstance(step, int):
                    act_chunk(s, step, c0 + step, ACT.Silu if step in (E_G, E_G + 1) else ACT.Copy)
                elif step in todo:
                    todo[step]()
            act_attention(s)
            for j in range(3):
                hi(c0 + 12 + j + RING)

        def act_odd(s):
            c0 = base[s]

            def turn_wuk():
                for g in range(4):
                    act.wait_ge(mla_pe.sem, M_PE[f"wuk{g}"])
                    act.activation(wukT[:, g // 2, (g % 2) * 512:(g % 2 + 1) * 512], bank[QUAD[g]][:, :], ACT.Copy).then_inc(mla_act.sem, 1)

            def small():
                act.wait_ge(mla_pe.sem, M_PE["small"])
                act.activation(kix, bank[6][:, 0:T], ACT.Copy)
                act.activation(wix[0:8, :], bank[6][0:8, T:2 * T], ACT.Copy).then_inc(mla_act.sem, 1)

            def csquares():
                act.wait_ge(proj_out.sem, proj_out.at(s, O_C + 1))
                act.activation(csq, pj[:, O_C, :], ACT.Square).then_inc(mla_act.sem, 1)

            def cnorm():
                act.wait_ge(mla_pe.sem, M_PE["cstat"])
                act.activation(root[:, :], bank[7][:, 0:T], ACT.Sqrt, scale=1.0 / LAT, bias=epsc[:, 0:1]).then_inc(mla_act.sem, 1)

            def index():
                act.wait_ge(mla_pe.sem, M_PE["widx"])
                act.activation(wixT.rearrange("p b h -> p (b h)"), bank[6][:, 0:16], ACT.Copy, scale=8 ** -0.5).then_inc(mla_act.sem, 1)
                for h in range(8):
                    act.wait_ge(mla_pe.sem, M_PE[f"index{h}"])
                    if h >= 2:
                        act.wait_ge(mla_dve.sem, M_DVE[f"scored{h - 2}"])
                    act.activation(rl[:, h % 2, :], bank[QUAD[h % 4]][:, 0:384], ACT.Relu, scale=SCALE).then_inc(mla_act.sem, 1)

            def keys():
                for g in range(4):
                    act.wait_ge(mla_pe.sem, M_PE[f"K{g}"])
                    act.activation(KTm[:, 2 * g:2 * g + 2, :].rearrange("p m t -> p (m t)"), bank[QUAD[g]][:, :], ACT.Copy).then_inc(mla_act.sem, 1)

            def values():
                for g in range(4):
                    act.wait_ge(mla_pe.sem, M_PE[f"V{g}"])
                    act.activation(Vm[:, g // 2, (g % 2) * 512:(g % 2 + 1) * 512], bank[QUAD[g]][:, :], ACT.Copy).then_inc(mla_act.sem, 1)

            todo = {"wuk": turn_wuk, "small": small, "csq": csquares, "cnorm": cnorm, "index": index, "K": keys, "V": values}
            for step in ODD:
                if isinstance(step, int):
                    act_chunk(s, step, c0 + step)
                elif step in todo:
                    todo[step]()
            act_attention(s)
            for j in range(3):
                hi(c0 + 7 + j + RING)

        def act_rope():
            for dst, at in ((sinT, 1), (cosT, 3)):
                act.wait_ge(rope_made.sem, at)
                act.activation(dst, red, ACT.Sin).then_inc(rope_made.sem, 1)

        def act_mod(s, before):
            i = MODS.index(s)
            act.wait_ge(fold_made.sem, i // 2 + 1)
            for k in range(KT):
                act.wait_ge(xn_made.sem, xn_made.at(s, k + 1))
                act.activation(xh[:, k, :], xn[:, k, :], ACT.Identity, bias=fold[:, i, 1, k:k + 1]).then_inc(xh_made.sem, 1)
            hi(base[s] + 2)

        def act_ln_bias(s):
            if s == "final":
                return
            l, b = int(s[2]), V_MIXB if s[3] == "a" else V_FFNB
            for k in range(KT):
                act.wait_ge(ln_made.sem, ln_made.at(s, k + 1))
                act.activation(x[:, k, :], x[:, k, :], ACT.Identity, bias=vec(0, b + KT * l + k)).then_inc(x_ready.sem, 1)

        def act_mix(s):
            l, c0 = int(s[3:]), base[s]
            for step in MIX:
                if isinstance(step, int):
                    act_chunk(s, step, c0 + step, ACT.Sigmoid if step in (2, 3) else ACT.Copy, pm)
                    if step == 1:
                        act_ln_bias(x_of[s])
            act_attention(s, lambda i: act_chunk(s, 10 + i, c0 + 10 + i, ACT.Sigmoid, pm) if i < 8 else None)
            act.wait_ge(ao_made.sem, ao_made.at(s))
            act.activation(flat(xh[:, 0:4, :]), flat(ao), ACT.Copy).then_inc(xh_made.sem, 1)
            act.wait_ge(cln_pe.sem, cln_pe.at(s, 1))
            act.activation(cmu, bank[6][:, 0:T], ACT.Copy, scale=1.0 / CW).then_inc(cln_act.sem, 1)
            act.wait_ge(cln_dve.sem, cln_dve.at(s, 1))
            act.activation(flat(ctmp), flat(cacc), ACT.Square).then_inc(cln_act.sem, 1)
            hi(c0 + 18 + RING)
            act.wait_ge(cln_pe.sem, cln_pe.at(s, 2))
            act.activation(root[:, :], bank[7][:, 0:T], ACT.Sqrt, scale=1.0 / CW, bias=epsc[:, 1:2]).then_inc(cln_act.sem, 1)
            for ct in range(CT):
                act.wait_ge(cln_dve.sem, cln_dve.at(s, 2 + ct))
                act.activation(ctmp[:, ct, :], cacc[:, ct, :], ACT.Silu, bias=vec(1, V_CLNB + 4 * l + ct)).then_inc(cln_act.sem, 1)
            for q in range(2):
                act.wait_ge(cln_act.sem, cln_act.at(s, 5 + 2 * q))
                act.activation(flat(xh[:, 4 + 2 * q:6 + 2 * q, :]), flat(ctmp[:, 2 * q:2 * q + 2, :]), ACT.Copy).then_inc(xh_made.sem, 1)
            hi(c0 + 19 + RING)
            for i in range(4):
                if i == 2:
                    hi(c0 + 20 + RING)
                act.wait_ge(merged.sem, merged.at(s, i + 1))
                act.activation(flat(xh[:, 2 * i:2 * i + 2, :]), flat(xn[:, 2 * i:2 * i + 2, :]), ACT.Copy).then_inc(xh_made.sem, 1)
            hi(c0 + 21 + RING)
            act.wait_ge(ada_made.sem, 4)
            act_scaled(s, c0 + 22, l, 2)

        def act_scaled(s, c0, l, part):
            for j in range(4):
                act.wait_ge(chunk_used.sem, c0 + j + 1)
                if j >= 2:
                    act.wait_ge(x_ready.sem, x_ready.at(s, j - 1))
                for m in range(2):
                    last = act.activation(yt[:, j % 2, m * T:(m + 1) * T], bank[2 + j % 2][:, m * T:(m + 1) * T], ACT.Identity,
                                          scale=ada(l, part, 2 * j + m, 1))
                last.then_inc(y_out.sem, 1)
                if j < 3:
                    hi(c0 + j + RING)

        def act_ln(s):
            act.wait_ge(stat_made.sem, stat_made.at(s, 1))
            act.activation(rstd[:, :], bank[6][:, 0:T], ACT.Copy, scale=1.0 / D).then_inc(root_made.sem, 1)
            for q in range(4):
                act.wait_ge(cen_made.sem, cen_made.at(s, q + 1))
                act.activation(xn[:, 2 * q:2 * q + 2, :], x[:, 2 * q:2 * q + 2, :], ACT.Square).then_inc(sq_made.sem, 1)
            act.wait_ge(stat_made.sem, stat_made.at(s, 2))
            act.activation(root[:, :], bank[7][:, 0:T], ACT.Sqrt, scale=1.0 / D, bias=epsc[:, 1:2]).then_inc(root_made.sem, 1)
            if s == STAGES[-1][1]:
                act_ln_bias(s)

        def act_store():
            for q in range(2):
                act.wait_ge(out_made.sem, q + 1)
                act.activation(xin[:, 0, q * 512:(q + 1) * 512], bank[2 * q][:, :], ACT.Copy).then_inc(out_copied.sem, 1)

        act_setup()
        for kind, s in STAGES:
            if kind == "rms":
                act_rms(s)
            if kind in ("ffn", "sq"):
                act_ffn(s)
            if kind == "even":
                act_even(s)
            if kind == "odd":
                act_odd(s)
            if kind == "rope":
                act_rope()
            if kind == "mod":
                act_mod(s, x_of[s])
            if kind == "mix":
                act_mix(s)
            if kind == "ln":
                act_ln(s)
        act_store()

    @block.vector
    def _(dve):
        def lo(c, turn=None, per_turn=0):
            if turn is None and c >= n_chunks:
                return
            dve.wait_ge(hi_made.sem, shifted(c + 1, turn, per_turn))
            dve.tensor_tensor(wl[:, c % RING, :], raw[:, c % RING, :], wh[:, c % RING, :].bitcast(F32), ALU.subtract).then_inc(lo_made.sem, 1)

        def dve_setup():
            dve.wait_ge(setup_pe.sem, 5)
            for v in range(4):
                last = dve.tensor_copy(vecT[:, v, 0:V_ROWS[v]], bank[7][:, v * P:v * P + V_ROWS[v]])
            last.then_inc(vec_made.sem, 1)
            dve.wait_ge(vec_made.sem, 1)

        def xrest(s, k):
            dve.wait_ge(xh_made.sem, xh_made.at(s, k + 1))
            dve.tensor_tensor(xl[:, k, :], xn[:, k, :], xh[:, k, :].bitcast(F32), ALU.subtract).then_inc(xl_made.sem, 1)

        def dve_rms(s):
            dve.wait_ge(root_made.sem, root_made.at(s))
            dve.reciprocal(rstd[:, :], root[:, :]).then_inc(rstd_made.sem, 1)
            if s == "final":
                return
            dve.wait_ge(rstd_made.sem, rstd_made.at(s))
            for k in range(KT):
                scaled(xn, V_NORM + int(s[3:]) * KT, k).then_inc(xn_made.sem, 1)
                if k >= 1:
                    xrest(s, k - 1)
            xrest(s, KT - 1)
            if s == "rms0":
                lo(1)
            lo(base[s] + 2)

        def scaled(dst, gain, k):
            return dve.scalar_tensor_tensor(out=dst[:, k, :], in0=x[:, k, :], scalar=vec(0, gain + k), in1=rstd[:, :],
                                            op0=ALU.mult, op1=ALU.mult)

        def dve_ffn(s):
            n_in, steps, body, bufs = ffn_shape(s)
            c0 = base[s]

            def step(i, st, turn):
                c = c0 + (0 if st == 0 else n_in + (n_in + 1) * (st - 1))
                per = (n_in + 1) * body
                if n_in == 1:
                    dve.wait_ge(act_made.sem, shifted(act_made.at(s, st + 1), turn, body))
                    h = flat(fh[:, st % bufs, :, :])
                    dve.tensor_tensor(h, flat(fs), flat(fs), ALU.mult).then_inc(h_made.sem, 1)
                    lo(c + RING, turn, per)
                    dve.wait_ge(hh_made.sem, shifted(hh_made.at(s, st + 1), turn, body))
                    dve.tensor_tensor(hl[:, st % bufs, :], h, hh[:, st % bufs, :].bitcast(F32), ALU.subtract).then_inc(hl_made.sem, 1)
                    if st > 0:
                        lo(c + 1 + RING, turn, per)
                    if st == 1:
                        dve_ln_gain(x_of[s])
                    return
                lo(c + RING, turn, per)
                for f in range(2):
                    dve.wait_ge(act_made.sem, shifted(act_made.at(s, 2 * st + f + 1), turn, 2 * body))
                    dve.tensor_tensor(fh[:, st % bufs, f, :], fs[:, f, :], bank[4 + f][:, T:2 * T], ALU.mult).then_inc(h_made.sem, 1)
                lo(c + n_in - 1 + RING, turn, per)
                for f in range(2):
                    dve.wait_ge(hh_made.sem, shifted(hh_made.at(s, 2 * st + f + 1), turn, 2 * body))
                    mv = slice(f * T, (f + 1) * T)
                    dve.tensor_tensor(hl[:, st % bufs, mv], fh[:, st % bufs, f, :], hh[:, st % bufs, mv].bitcast(F32),
                                      ALU.subtract).then_inc(hl_made.sem, 1)
                if st > 0:
                    lo(c + n_in + RING, turn, per)

            steps_of(dve, steps, 2, body, step)
            for q in range(4):
                acc_ready(dve, s, q)
                xs = x[:, 2 * q:2 * q + 2, :].rearrange("p k t -> p (k t)")
                if KIND[s] == "ffn":
                    dve.scalar_tensor_tensor(out=xs, in0=bank[q][:, :], scalar=0.5, in1=xs, op0=ALU.mult,
                                             op1=ALU.add).then_inc(x_ready.sem, 1)
                else:
                    dve.wait_ge(y_out.sem, y_out.at(s, q + 1))
                    dve.wait_ge(x_ready.sem, x_ready.at(x_of[s]))
                    dve.scalar_tensor_tensor(out=xs, in0=xs, scalar=ALPHA, in1=yt[:, q % 2, :], op0=ALU.mult,
                                             op1=ALU.add).then_inc(x_ready.sem, 1)

        n_step = [0]

        def link(ins):
            n_step[0] += 1
            ins.then_inc(dve_step.sem, 1)
            dve.wait_ge(dve_step.sem, n_step[0])

        def dve_attention(s, meanwhile=None):
            H = heads_of[s]
            mask = att_of(s)[3]

            def masked(h):
                dve.wait_ge(score_made.sem, score_made.at(s, h + 1))
                if s == "odd":
                    dve.wait_ge(bm_made.sem, h + 1)
                for b, at in enumerate((slice(0, P), slice(P, 384))):
                    last = dve.tensor_tensor_reduce(ns[:, h % 2, at], bank[4 + h % 2][:, at], mask(h)[:, at], -SCALE, 3e38,
                                                    ALU.add, ALU.min, nm[:, h % 2, b:b + 1])
                last.then_inc(ns_made.sem, 1)

            def normalise(h):
                dve.wait_ge(p_made.sem, p_made.at(s, h + 1))
                link(dve.reciprocal(ri[:, h % 2, :], rs[:, h % 2, :]))
                for b, at in enumerate((slice(0, P), slice(P, 384))):
                    last = dve.tensor_scalar(pr[:, h % 3, at], pr[:, h % 3, at], ri[:, h % 2, b:b + 1], None, ALU.mult)
                last.then_inc(pn_made.sem, 1)

            def rest(pair):
                if KIND[s] == "mix":
                    return
                i = XL_FIRST[s] + pair
                dve.wait_ge(xh_made.sem, xh_made.at(s, i + 1))
                t = X_TILE[s] + pair
                dve.tensor_tensor(xl[:, t, :], bank[pair % 2][:, 0:T], xh[:, t, :].bitcast(F32), ALU.subtract).then_inc(xl_made.sem, 1)

            for i in range(H + 4):
                if i < H:
                    masked(i)
                if 1 <= i <= H:
                    normalise(i - 1)
                if meanwhile:
                    meanwhile(i)
                if i >= 4 and i % 2 == 0:
                    rest((i - 4) // 2)

        def dve_out(s, c0):
            for j in range(4):
                dve.wait_ge(chunk_used.sem, c0 + j + 1)
                xs = x[:, 2 * j:2 * j + 2, :].rearrange("p k t -> p (k t)")
                dve.tensor_tensor(xs, bank[2 + j % 2][:, :], xs, ALU.add).then_inc(x_ready.sem, 1)
                if j < 3:
                    lo(c0 + j + RING)

        def dve_even(s):
            c0 = base[s]

            def small():
                dve.wait_ge(small_made.sem, 1)
                dve.tensor_scalar(fz[32:40, :], bank[STAT][32:40, 0:T], bfox[32:40, 0:1], None, ALU.add).then_inc(gla_dve.sem, 1)

            def z():
                dve.wait_ge(gla_dve.sem, G_DVE["fz"])
                dve.wait_ge(gla_act.sem, G_ACT["z"])
                dve.scalar_tensor_tensor(out=za, in0=zs, scalar=-1.0, in1=zs, op0=ALU.mult, op1=ALU.max).then_inc(gla_dve.sem, 1)
                dve.scalar_tensor_tensor(out=fa[32:40, :], in0=fz[32:40, :], scalar=-1.0, in1=fz[32:40, :], op0=ALU.mult,
                                         op1=ALU.max).then_inc(gla_dve.sem, 1)

            def log_sigmoid():
                dve.wait_ge(gla_act.sem, G_ACT["lnf"])
                dve.scalar_tensor_tensor(out=gk, in0=zs, scalar=0.0, in1=za, op0=ALU.min, op1=ALU.subtract).then_inc(gla_dve.sem, 1)
                link(dve.scalar_tensor_tensor(out=fz[32:40, :], in0=fz[32:40, :], scalar=0.0, in1=fa[32:40, :], op0=ALU.min,
                                              op1=ALU.subtract))
                dve.tensor_tensor_scan(fsum[32:40, :], onesT[32:40, :], fz[32:40, :], 0.0, ALU.mult, ALU.add).then_inc(gla_dve.sem, 1)

            def decayed():
                dve.wait_ge(gla_act.sem, G_ACT["decays"])
                dve.wait_ge(proj_out.sem, proj_out.at(s, 2))
                flat = lambda v: v.rearrange("p m t -> p (m t)")
                dve.scalar_tensor_tensor(out=flat(qd), in0=pj[:, E_Q, :], scalar=SCALE, in1=eg, op0=ALU.mult, op1=ALU.mult)
                dve.tensor_tensor(flat(kd), pj[:, E_K, :], eng, ALU.mult)
                dve.tensor_tensor(flat(ke), pj[:, E_K, :], flat(eke), ALU.mult).then_inc(gla_dve.sem, 1)
                dve.wait_ge(gla_dve.sem, G_DVE["decayed"])
                link(dve.memset(AT[:, :, :], 0.0))

            def scores():
                dve.wait_ge(gla_pe.sem, G_PE["A"])
                for q in range(2):
                    last = dve.copy_predicated(AT[:, q, :].rearrange("p (b i) -> p b i", b=4),
                                               trib[:, :].unsqueeze(1).broadcast_to((P, 4, P)),
                                               bank[6 + q][:, :].rearrange("p (b i) -> p b i", b=4))
                last.then_inc(gla_dve.sem, 1)

            def states():
                dve.wait_ge(gla_pe.sem, G_PE["kv"])
                kv = lambda ch, m: bank[6 + ch % 2][:, (ch // 2) * T + m * P:(ch // 2) * T + (m + 1) * P]
                for m in range(2):
                    last = dve.tensor_copy(state[:, 0, m, :], kv(0, m))
                for ch in (1, 2):
                    link(last)
                    for m in range(2):
                        last = dve.scalar_tensor_tensor(out=state[:, ch, m, :], in0=state[:, ch - 1, m, :],
                                                        scalar=egl[:, m, ch:ch + 1], in1=kv(ch, m), op0=ALU.mult, op1=ALU.add)
                last.then_inc(gla_dve.sem, 1)

            def norm():
                dve.wait_ge(gla_act.sem, G_ACT["oroot"])
                link(dve.reciprocal(orstd, oroot))
                for q in range(2):
                    at = slice(q * 512, (q + 1) * 512)
                    last = dve.scalar_tensor_tensor(out=osq[:, at], in0=bank[6 + q][:, :], scalar=vec(0, V_GLA),
                                                    in1=orstd[:, at], op0=ALU.mult, op1=ALU.mult)
                link(last)
                o4 = osq.rearrange("p (b a t) -> p a b t", a=2, b=2)
                dve.tensor_tensor(o4, o4, pj[:, E_G:E_G + 2, :].rearrange("p a (b t) -> p a b t", b=2), ALU.mult).then_inc(gla_dve.sem, 1)

            def halves():
                o4 = osq.rearrange("p (b a t) -> p a b t", a=2, b=2)
                dve.wait_ge(xh_made.sem, xh_made.at(s, 1))
                dve.tensor_tensor(xl[:, 0:4, :].rearrange("p (a b) t -> p a b t", b=2), o4,
                                  xh[:, 0:4, :].rearrange("p (a b) t -> p a b t", b=2).bitcast(F32), ALU.subtract).then_inc(xl_made.sem, 1)

            todo = {"small": small, "z": z, "gk": log_sigmoid, "decay": decayed, "A": scores, "kv": states, "norm": norm, "halves": halves}
            for step in EVEN:
                if isinstance(step, int):
                    lo(c0 + step + RING)
                elif step in todo:
                    todo[step]()
            dve_attention(s)
            dve_out(s, c0 + 12)

        def dve_odd(s):
            c0 = base[s]
            blocks = (slice(0, P), slice(P, 384))

            def cnorm():
                dve.wait_ge(mla_act.sem, M_ACT["croot"])
                link(dve.reciprocal(rstd[:, :], root[:, :]))
                for l in range(2):
                    last = dve.scalar_tensor_tensor(out=cT[:, l, :], in0=pj[:, O_C, l * T:(l + 1) * T], scalar=vec(0, V_MLA + l),
                                                    in1=rstd[:, :], op0=ALU.mult, op1=ALU.mult)
                last.then_inc(mla_dve.sem, 1)

            def index():
                for h in range(8):
                    dve.wait_ge(mla_act.sem, M_ACT[f"relu{h}"])
                    if h > 0:
                        dve.wait_ge(mla_dve.sem, M_DVE[f"scored{h - 1}"])
                    for b, at in enumerate(blocks):
                        w = wixT[:, b, h:h + 1]
                        if h == 0:
                            last = dve.tensor_scalar(sc[:, at], rl[:, 0, at], w, None, ALU.mult)
                        else:
                            last = dve.scalar_tensor_tensor(out=sc[:, at], in0=rl[:, h % 2, at], scalar=w, in1=sc[:, at],
                                                            op0=ALU.mult, op1=ALU.add)
                    last.then_inc(mla_dve.sem, 1)
                dve.wait_ge(mla_dve.sem, M_DVE["scored7"])
                link(dve.tensor_tensor(sc, sc, cmask[:, :], ALU.add))

            def search():
                for _ in range(SEARCH_ROUNDS):
                    for b, at in enumerate(blocks):
                        last = dve.max(m8[:, b, :], sc[:, at])
                    link(last)
                    for b, at in enumerate(blocks):
                        last = dve.match_replace(sc[:, at], m8[:, b, :], sc[:, at], PICKED)
                    link(last)

            def mask():
                link(dve.tensor_scalar(dm, sc, 0.5 * (PICKED + NEG), NEG, ALU.is_gt, ALU.mult))
                dve.tensor_tensor(dm, dm, cmask[:, :], ALU.add).then_inc(mla_dve.sem, 1)

            todo = {"cnorm": cnorm, "index": index, "top": search, "mask": mask}
            for step in ODD:
                if isinstance(step, int):
                    lo(c0 + step + RING)
                elif step in todo:
                    todo[step]()
            dve_attention(s)
            dve_out(s, c0 + 7)

        def dve_ada(s):
            (l, first), n = ADA_OF[s], 2 * ADA_PER_FFN
            at = slice(2 * first, 2 * first + n)
            dve.wait_ge(ada_turned.sem, ada_made.at(s))
            link(dve.tensor_tensor(adaT[:, l, 0, at], bank[7][:, 0:n], vecT[:, 1, V_ADA + 48 * l + 2 * first:V_ADA + 48 * l + 2 * first + n], ALU.add))
            dve.tensor_scalar(adaT[:, l, 1, at], adaT[:, l, 0, at], 1.0, None, ALU.add).then_inc(ada_made.sem, 1)

        def dve_fold(l):
            norms = [((V_FINAL, None) if l == 0 else (V_FFNG, V_FFNB)), (V_MIXG + l * KT, V_MIXB + l * KT)]
            part = lambda n, plus_one: adaT[:, l, plus_one, n * KT:(n + 1) * KT]
            dve.wait_ge(ada_made.sem, 2 * l + 2)
            for n, (g, b) in enumerate(norms):
                i = 2 * l + n
                dve.tensor_tensor(fold[:, i, 0, :], vecT[:, 0, g:g + KT], part(3 * n + 1, 1), ALU.mult)
                if b is None:
                    last = dve.tensor_copy(fold[:, i, 1, :], part(3 * n, 0))
                else:
                    link(dve.tensor_tensor(fold[:, i, 1, :], vecT[:, 0, b:b + KT], part(3 * n + 1, 1), ALU.mult))
                    last = dve.tensor_tensor(fold[:, i, 1, :], fold[:, i, 1, :], part(3 * n, 0), ALU.add)
            last.then_inc(fold_made.sem, 1)

        def dve_mod(s, before):
            i = MODS.index(s)
            dve.wait_ge(fold_made.sem, i // 2 + 1)
            dve.wait_ge(rstd_made.sem, rstd_made.at(before))

            def rest(k):
                dve.wait_ge(xh_made.sem, xh_made.at(s, k + 1))
                dve.scalar_tensor_tensor(out=xl[:, k, :], in0=xn[:, k, :], scalar=fold[:, i, 1, k:k + 1], in1=xh[:, k, :].bitcast(F32),
                                         op0=ALU.add, op1=ALU.subtract).then_inc(xl_made.sem, 1)

            for k in range(KT):
                dve.scalar_tensor_tensor(out=xn[:, k, :], in0=x[:, k, :], scalar=fold[:, i, 0, k:k + 1], in1=rstd[:, :],
                                         op0=ALU.mult, op1=ALU.mult).then_inc(xn_made.sem, 1)
                if k >= 1:
                    rest(k - 1)
            rest(KT - 1)
            lo(base[s] + 2)

        def dve_ln_gain(s):
            if s == "final":
                for k in range(KT):
                    scaled(x, V_FINAL, k).then_inc(x_ready.sem, 1)
                return
            l, g = int(s[2]), V_MIXG if s[3] == "a" else V_FFNG
            for k in range(KT):
                scaled(x, g + KT * l, k).then_inc(ln_made.sem, 1)

        def dve_mix(s):
            l, c0 = int(s[3:]), base[s]
            taps = [(j, ct) for j in range(CONV_K) for ct in range(2)]

            def convolve(count):
                for j, ct in taps[:count]:
                    n = j * 2 + ct
                    w, src = vec(2 + l, j * CT + ct), hpad[:, ct, j:j + T]
                    if j == 0:
                        dve.wait_ge(glu_made.sem, glu_made.at(s))
                        dve.tensor_scalar(cacc[:, ct, :], src, w, vec(1, V_DWB + 4 * l + ct), ALU.mult, ALU.add).then_inc(conv_made.sem, 1)
                    else:
                        dve.wait_ge(conv_made.sem, conv_made.at(s, n - 1))
                        dve.scalar_tensor_tensor(out=cacc[:, ct, :], in0=src, scalar=w, in1=cacc[:, ct, :], op0=ALU.mult,
                                                 op1=ALU.add).then_inc(conv_made.sem, 1)
                del taps[:count]

            def gated():
                dve.wait_ge(proj_out.sem, proj_out.at(s, 4))
                tiles = lambda n: pm[:, n:n + 2, :].rearrange("p n (j t) -> p (n j) t", j=2)
                dve.tensor_tensor(hpad[:, :, CONV_K - 1:], tiles(0), tiles(2), ALU.mult).then_inc(glu_made.sem, 1)

            def rope(first):
                for i in range(2):
                    n = first + i
                    dve.wait_ge(rope_pe.sem, rope_pe.at(s, (first - X_Q) + i + 1))
                    two = lambda v: v.unsqueeze(1).broadcast_to((P, 2, T))
                    split = lambda v: v.rearrange("p (m t) -> p m t", m=2)
                    t = ctmp[:, 2 * i:2 * i + 2, :]
                    dve.tensor_tensor(t, split(bank[6 + i][:, :]), two(sinT), ALU.mult)
                    link(dve.tensor_tensor(split(pm[:, n, :]), split(pm[:, n, :]), two(cosT), ALU.mult))
                    dve.tensor_tensor(split(pm[:, n, :]), split(pm[:, n, :]), t, ALU.add).then_inc(rope_dve.sem, 1)

            todo = {"glu": gated, "ropeq": lambda: rope(X_Q), "ropek": lambda: rope(X_K)}
            for step in MIX:
                if isinstance(step, int):
                    lo(c0 + step + RING)
                    if step == 1:
                        dve_ln_gain(x_of[s])
                    if step >= X_Q:
                        convolve(TAPS_PER_STEP)
                elif step in todo:
                    todo[step]()

            def meanwhile(i):
                if 1 <= i <= 8:
                    lo(c0 + 9 + i + RING)
                convolve(TAPS_PER_STEP)

            dve_attention(s, meanwhile)
            convolve(len(taps))
            dve.wait_ge(xh_made.sem, xh_made.at(s, 1))
            dve.tensor_tensor(flat(xl[:, 0:4, :]), flat(ao), flat(xh[:, 0:4, :]).bitcast(F32), ALU.subtract).then_inc(xl_made.sem, 1)
            dve.wait_ge(cln_act.sem, cln_act.at(s, 1))
            dve.tensor_tensor(cacc, cacc, cmu.unsqueeze(1).broadcast_to((P, CT, T)), ALU.subtract).then_inc(cln_dve.sem, 1)
            def gate_attention(n):
                dve.wait_ge(chunk_used.sem, c0 + 18 + n + 1)
                for q in range(2):
                    i = 2 * n + q
                    last = dve.tensor_tensor(flat(xn[:, 2 * i:2 * i + 2, :]), bank[4 * n + q][:, :], pm[:, X_GA + i, :], ALU.mult)
                return last

            def merge(n):
                dve.wait_ge(chunk_used.sem, c0 + 20 + n + 1)
                for q in range(2):
                    i = 2 * n + q
                    m, t = flat(xn[:, 2 * i:2 * i + 2, :]), flat(ctmp[:, 2 * q:2 * q + 2, :])
                    link(dve.tensor_tensor(t, bank[4 * n + 2 + q][:, :], pm[:, X_GC + i, :], ALU.mult))
                    dve.tensor_tensor(m, m, t, ALU.add).then_inc(merged.sem, 1)
                for i in (2 * n, 2 * n + 1):
                    dve.wait_ge(xh_made.sem, xh_made.at(s, 3 + i + 1))
                    at = slice(2 * i, 2 * i + 2)
                    dve.tensor_tensor(flat(xl[:, at, :]), flat(xn[:, at, :]), flat(xh[:, at, :]).bitcast(F32), ALU.subtract).then_inc(xl_made.sem, 1)

            link(gate_attention(0))
            dve.wait_ge(cln_act.sem, cln_act.at(s, 3))
            link(dve.reciprocal(rstd[:, :], root[:, :]))
            for ct in range(CT):
                dve.scalar_tensor_tensor(out=cacc[:, ct, :], in0=cacc[:, ct, :], scalar=vec(1, V_CLNG + 4 * l + ct), in1=rstd[:, :],
                                         op0=ALU.mult, op1=ALU.mult).then_inc(cln_dve.sem, 1)
            for q in range(2):
                dve.wait_ge(xh_made.sem, xh_made.at(s, 2 + q))
                dve.tensor_tensor(flat(xl[:, 4 + 2 * q:6 + 2 * q, :]), flat(ctmp[:, 2 * q:2 * q + 2, :]),
                                  flat(xh[:, 4 + 2 * q:6 + 2 * q, :]).bitcast(F32), ALU.subtract).then_inc(xl_made.sem, 1)
            lo(c0 + 18 + RING)
            link(gate_attention(1))
            lo(c0 + 19 + RING)
            merge(0)
            lo(c0 + 20 + RING)
            merge(1)
            lo(c0 + 21 + RING)
            dve.wait_ge(x_ready.sem, x_ready.at(x_of[s]))
            for j in range(4):
                dve.wait_ge(y_out.sem, y_out.at(s, j + 1))
                xs = flat(x[:, 2 * j:2 * j + 2, :])
                dve.scalar_tensor_tensor(out=xs, in0=xs, scalar=ALPHA, in1=yt[:, j % 2, :], op0=ALU.mult, op1=ALU.add).then_inc(x_ready.sem, 1)
                if j < 3:
                    lo(c0 + 22 + j + RING)

        def dve_ln(s):
            dve.wait_ge(root_made.sem, root_made.at(s, 1))
            for q in range(4):
                xs = x[:, 2 * q:2 * q + 2, :]
                last = dve.tensor_tensor(xs, xs, rstd[:, :].unsqueeze(1).broadcast_to((P, 2, T)), ALU.subtract).then_inc(cen_made.sem, 1)
            dve.wait_ge(root_made.sem, root_made.at(s, 2))
            dve.reciprocal(rstd[:, :], root[:, :]).then_inc(rstd_made.sem, 1)
            if s == STAGES[-1][1]:
                dve.wait_ge(rstd_made.sem, rstd_made.at(s))
                dve_ln_gain(s)

        dve_setup()
        lo(0)
        for (_, before), (kind, s) in zip([(None, None)] + STAGES, STAGES):
            if kind == "rms":
                dve_rms(s)
                if before in ADA_OF and s != "final":
                    dve_ada(before)
                if s == "rms5":
                    dve_fold(0)
            if kind in ("ffn", "sq"):
                dve_ffn(s)
            if kind == "even":
                dve_even(s)
            if kind == "odd":
                dve_odd(s)
            if kind == "rope":
                dve.wait_ge(rope_made.sem, 4)
                dve.memset(hpad[:, :, 0:CONV_K - 1], 0.0)
            if kind == "mod":
                dve_mod(s, x_of[s])
                if s == "mod0a":
                    dve_ada("ffn3")
                    dve_fold(1)
            if kind == "mix":
                dve_mix(s)
            if kind == "ln":
                dve_ln(s)

        for q in range(2):
            dve.wait_ge(out_made.sem, q + 1)
            dve.tensor_copy(xin[:, 1, q * 512:(q + 1) * 512], bank[2 * q + 1][:, :]).then_inc(out_copied_dve.sem, 1)

    ctx.close()


OUTS = [((1, T, D), "float32")]


def kernel(**inputs):
    import numpy as _np
    import concourse.bacc as _bacc
    from concourse import mybir as _mybir
    from concourse.bass_utils import run_bass_kernel_spmd as _run

    nc = _bacc.Bacc("TRN2", target_bir_lowering=False, num_devices=1)
    arrays, aps = {}, {}
    for name, value in {**inputs, **constants()}.items():
        a = _np.ascontiguousarray(value)
        arrays[f"in_{name}"] = a
        aps[name] = nc.dram_tensor(f"in_{name}", a.shape, _mybir.dt.from_np(a.dtype), kind="ExternalInput").ap()
    out = nc.dram_tensor("out_0", OUTS[0][0], F32, kind="ExternalOutput").ap()
    build(nc, aps, out)
    r = _run(nc, [arrays], core_ids=[0])
    return r.results[0]["out_0"]
```
